# Optimizing a Trainium2 kernel written in Bass

```python
import jax, jax.numpy as jnp
from jax import lax
import numpy as np

D_MODEL = 1024
BATCH = 1
SEQ = 512
DEPTH = 2

CHUNK = 64
Q_BLOCK = 128
HEAD_DIM = 64
MIX_HEADS = D_MODEL // HEAD_DIM
A_HEADS = MIX_HEADS // 2
A_KV_HEADS = 2
A_GROUP = A_HEADS // A_KV_HEADS
A_WINDOW = 128
A_BACK = A_WINDOW // CHUNK - 1
B_HEADS = MIX_HEADS - A_HEADS
B_BACK = 8
REL_CLIP = 256
REL_TABLE = 2 * REL_CLIP + 1
C_HEADS = MIX_HEADS // 2
D_HEADS = MIX_HEADS - C_HEADS
INDEX_HEADS = 4
INDEX_DIM = 64
INDEX_TOPK = 256
FF_HIDDEN = ((8 * D_MODEL + 3 * 256 - 1) // (3 * 256)) * 256
N_EVEN = (DEPTH + 1) // 2
N_ODD = DEPTH // 2
ATTN_SCALE = HEAD_DIM ** -0.5
INDEX_SCALE = (INDEX_DIM * INDEX_HEADS) ** -0.5
RMS_EPS = 1e-6

AB_SIZES = (A_HEADS * HEAD_DIM, A_KV_HEADS * HEAD_DIM, A_KV_HEADS * HEAD_DIM,
            B_HEADS * HEAD_DIM, B_HEADS * HEAD_DIM, B_HEADS * HEAD_DIM)
CD_SIZES = (C_HEADS * HEAD_DIM, C_HEADS * HEAD_DIM, C_HEADS * HEAD_DIM, C_HEADS,
            D_HEADS * HEAD_DIM, HEAD_DIM, HEAD_DIM,
            INDEX_HEADS * INDEX_DIM, INDEX_DIM, INDEX_HEADS)
AB_IN = sum(AB_SIZES)
CD_IN = sum(CD_SIZES)
AB_OUT = (A_HEADS + B_HEADS) * HEAD_DIM
CD_OUT = (C_HEADS + D_HEADS) * HEAD_DIM

kernel_name = 'hybrid_chunk_causal_encoder_block'

def rms_norm(x, g):
    xf = x.astype(jnp.float32)
    y = xf * lax.rsqrt(jnp.mean(xf * xf, axis=-1, keepdims=True) + RMS_EPS)
    return (y * g.astype(jnp.float32)).astype(x.dtype)

def split_cols(t, sizes):
    out, start = [], 0
    for n in sizes:
        out.append(t[..., start:start + n])
        start += n
    return out

def alibi_slopes(n_heads):
    return jnp.exp2(-8.0 * jnp.arange(1, n_heads + 1, dtype=jnp.float32) / n_heads)

def band_distance(n_back):
    i = jnp.arange(CHUNK)[:, None]
    j = jnp.arange((n_back + 1) * CHUNK)[None, :]
    return i + n_back * CHUNK - j

def chunk_band(t, n_back):
    b, s = t.shape[:2]
    nc = s // CHUNK
    pad = [(0, 0), (n_back * CHUNK, 0)] + [(0, 0)] * (t.ndim - 2)
    tp = jnp.pad(t, pad).reshape((b, nc + n_back, CHUNK) + t.shape[2:])
    idx = jnp.arange(nc)[:, None] + jnp.arange(n_back + 1)[None, :]
    band = tp[:, idx].reshape((b, nc, (n_back + 1) * CHUNK) + t.shape[2:])
    valid = jnp.repeat(idx >= n_back, CHUNK, axis=1)
    return band, valid

def sliding_sink_gqa(q, k, v, qn, kn, sink):
    b, s = q.shape[:2]
    nc = s // CHUNK
    q = rms_norm(q, qn)
    k = rms_norm(k, kn)
    qc = q.reshape(b, nc, CHUNK, A_KV_HEADS, A_GROUP, HEAD_DIM)
    kb, valid = chunk_band(k, A_BACK)
    vb, _ = chunk_band(v, A_BACK)
    sc = jnp.einsum('bnqkgd,bnskd->bnkgqs', qc, kb).astype(jnp.float32) * ATTN_SCALE
    slopes = alibi_slopes(A_HEADS).reshape(A_KV_HEADS, A_GROUP)
    dist = jnp.abs(band_distance(A_BACK)).astype(jnp.float32)
    sc = sc - slopes[:, :, None, None] * dist
    sc = jnp.where(valid[None, :, None, None, None, :], sc, -jnp.inf)
    snk = sink.astype(jnp.float32).reshape(A_KV_HEADS, A_GROUP)[:, :, None, None]
    m = jnp.maximum(jnp.max(sc, axis=-1, keepdims=True), snk)
    e = jnp.exp(sc - m)
    p = e / (jnp.sum(e, axis=-1, keepdims=True) + jnp.exp(snk - m))
    o = jnp.einsum('bnkgqs,bnskd->bnqkgd', p.astype(v.dtype), vb)
    return o.reshape(b, s, A_HEADS * HEAD_DIM)

def chunk_relbias_attn(q, k, v, qn, kn, rel):
    b, s = q.shape[:2]
    nc = s // CHUNK
    q = rms_norm(q, qn)
    k = rms_norm(k, kn)
    qc = q.reshape(b, nc, CHUNK, B_HEADS, HEAD_DIM)
    kb, valid = chunk_band(k, B_BACK)
    vb, _ = chunk_band(v, B_BACK)
    sc = jnp.einsum('bnqhd,bnshd->bnhqs', qc, kb).astype(jnp.float32) * ATTN_SCALE
    rel_idx = jnp.clip(band_distance(B_BACK), -REL_CLIP, REL_CLIP) + REL_CLIP
    sc = sc + rel.astype(jnp.float32)[:, rel_idx]
    sc = jnp.where(valid[None, :, None, None, :], sc, -jnp.inf)
    p = jax.nn.softmax(sc, axis=-1)
    o = jnp.einsum('bnhqs,bnshd->bnqhd', p.astype(v.dtype), vb)
    return o.reshape(b, s, B_HEADS * HEAD_DIM)

def forgetting_attn(q, k, v, f_logit, qn, kn, fbias):
    b, s = q.shape[:2]
    nb = s // Q_BLOCK
    q = rms_norm(q, qn)
    k = rms_norm(k, kn)
    log_f = jax.nn.log_sigmoid(f_logit.astype(jnp.float32) + fbias.astype(jnp.float32))
    cum = jnp.cumsum(log_f, axis=1)
    ck = jnp.transpose(cum, (0, 2, 1))
    qb = q.reshape(b, nb, Q_BLOCK, C_HEADS, HEAD_DIM).swapaxes(0, 1)
    cq = cum.reshape(b, nb, Q_BLOCK, C_HEADS).swapaxes(0, 1)
    kpos = jnp.arange(s)

    def block(args):
        qi, ci, blk = args
        tpos = blk * Q_BLOCK + jnp.arange(Q_BLOCK)
        sc = jnp.einsum('bqhd,bshd->bhqs', qi, k).astype(jnp.float32) * ATTN_SCALE
        sc = sc + jnp.transpose(ci, (0, 2, 1))[..., None] - ck[:, :, None, :]
        sc = jnp.where(kpos[None, :] <= tpos[:, None], sc, -jnp.inf)
        p = jax.nn.softmax(sc, axis=-1)
        return jnp.einsum('bhqs,bshd->bqhd', p.astype(v.dtype), v)

    o = lax.map(block, (qb, cq, jnp.arange(nb)))
    return o.swapaxes(0, 1).reshape(b, s, C_HEADS * HEAD_DIM)

def dsa_sparse_attn(q, k, v, q_idx, k_idx, w_idx, qn, kn):
    b, s = q.shape[:2]
    nb = s // Q_BLOCK
    top = min(INDEX_TOPK, s // 4)
    q = rms_norm(q, qn)
    k = rms_norm(k, kn)
    slopes = alibi_slopes(D_HEADS)
    kchunk = jnp.arange(s) // CHUNK
    qb = q.reshape(b, nb, Q_BLOCK, D_HEADS, HEAD_DIM).swapaxes(0, 1)
    qib = q_idx.reshape(b, nb, Q_BLOCK, INDEX_HEADS, INDEX_DIM).swapaxes(0, 1)
    wib = w_idx.reshape(b, nb, Q_BLOCK, INDEX_HEADS).swapaxes(0, 1)

    def block(args):
        qi, qii, wi, blk = args
        tpos = blk * Q_BLOCK + jnp.arange(Q_BLOCK)
        isc = jax.nn.relu(jnp.einsum('bqhd,bsd->bqhs', qii, k_idx).astype(jnp.float32))
        isc = jnp.einsum('bqh,bqhs->bqs', wi.astype(jnp.float32), isc) * INDEX_SCALE
        adm = kchunk[None, :] <= (tpos // CHUNK)[:, None]
        isc = jnp.where(adm[None], isc, -jnp.inf)
        ival, idx = lax.top_k(isc, top)
        ksel = jax.vmap(lambda kk, ii: kk[ii])(k, idx)
        vsel = jax.vmap(lambda vv, ii: vv[ii])(v, idx)
        sc = jnp.einsum('bqhd,bqkd->bhqk', qi, ksel).astype(jnp.float32) * ATTN_SCALE
        dist = jnp.abs(tpos[None, :, None] - idx).astype(jnp.float32)
        sc = sc - slopes[None, :, None, None] * dist[:, None]
        sc = jnp.where(jnp.isfinite(ival)[:, None], sc, -jnp.inf)
        p = jax.nn.softmax(sc, axis=-1)
        return jnp.einsum('bhqk,bqkd->bqhd', p.astype(v.dtype), vsel)

    o = lax.map(block, (qb, qib, wib, jnp.arange(nb)))
    return o.swapaxes(0, 1).reshape(b, s, D_HEADS * HEAD_DIM)

def mixer_ab(h, w_in, w_out, a_qn, a_kn, a_sink, b_qn, b_kn, b_rel):
    b, s, _ = h.shape
    qa, ka, va, qb, kb, vb = split_cols(h @ w_in, AB_SIZES)
    oa = sliding_sink_gqa(qa.reshape(b, s, A_HEADS, HEAD_DIM),
                          ka.reshape(b, s, A_KV_HEADS, HEAD_DIM),
                          va.reshape(b, s, A_KV_HEADS, HEAD_DIM), a_qn, a_kn, a_sink)
    ob = chunk_relbias_attn(qb.reshape(b, s, B_HEADS, HEAD_DIM),
                            kb.reshape(b, s, B_HEADS, HEAD_DIM),
                            vb.reshape(b, s, B_HEADS, HEAD_DIM), b_qn, b_kn, b_rel)
    return jnp.concatenate([oa, ob], axis=-1) @ w_out

def mixer_cd(h, w_in, w_out, c_qn, c_kn, c_fb, d_qn, d_kn):
    b, s, _ = h.shape
    qc, kc, vc, fc, qd, kd, vd, qi, ki, wi = split_cols(h @ w_in, CD_SIZES)
    oc = forgetting_attn(qc.reshape(b, s, C_HEADS, HEAD_DIM),
                         kc.reshape(b, s, C_HEADS, HEAD_DIM),
                         vc.reshape(b, s, C_HEADS, HEAD_DIM), fc, c_qn, c_kn, c_fb)
    od = dsa_sparse_attn(qd.reshape(b, s, D_HEADS, HEAD_DIM), kd, vd,
                         qi.reshape(b, s, INDEX_HEADS, INDEX_DIM), ki, wi, d_qn, d_kn)
    return jnp.concatenate([oc, od], axis=-1) @ w_out

def swiglu(h, w_gate_up, w_down):
    g, u = jnp.split(h @ w_gate_up, 2, axis=-1)
    return (jax.nn.silu(g) * u) @ w_down

def setup_inputs(seed: int = 0) -> dict:
    key = jax.random.key(seed)
    ks = jax.random.split(key, 23)
    nrm = lambda k, shape, s: jax.random.normal(k, shape, jnp.float32) * s
    gain = lambda k, shape: 1.0 + 0.05 * jax.random.normal(k, shape, jnp.float32)
    return {
        'x': nrm(ks[0], (BATCH, SEQ, D_MODEL), 1.0),
        'c': nrm(ks[1], (BATCH, D_MODEL), 1.0),
        'ada_w': nrm(ks[2], (DEPTH, D_MODEL, 6 * D_MODEL), 0.5 * D_MODEL ** -0.5),
        'ada_b': nrm(ks[3], (DEPTH, 6 * D_MODEL), 0.01),
        'mix_norm_g': gain(ks[4], (DEPTH, D_MODEL)),
        'ffn_norm_g': gain(ks[5], (DEPTH, D_MODEL)),
        'ab_w_in': nrm(ks[6], (N_EVEN, D_MODEL, AB_IN), D_MODEL ** -0.5),
        'ab_w_out': nrm(ks[7], (N_EVEN, AB_OUT, D_MODEL), AB_OUT ** -0.5),
        'a_q_norm': gain(ks[8], (N_EVEN, HEAD_DIM)),
        'a_k_norm': gain(ks[9], (N_EVEN, HEAD_DIM)),
        'a_sink': nrm(ks[10], (N_EVEN, A_HEADS), 1.0),
        'b_q_norm': gain(ks[11], (N_EVEN, HEAD_DIM)),
        'b_k_norm': gain(ks[12], (N_EVEN, HEAD_DIM)),
        'b_rel_bias': nrm(ks[13], (N_EVEN, B_HEADS, REL_TABLE), 0.5),
        'cd_w_in': nrm(ks[14], (N_ODD, D_MODEL, CD_IN), D_MODEL ** -0.5),
        'cd_w_out': nrm(ks[15], (N_ODD, CD_OUT, D_MODEL), CD_OUT ** -0.5),
        'c_q_norm': gain(ks[16], (N_ODD, HEAD_DIM)),
        'c_k_norm': gain(ks[17], (N_ODD, HEAD_DIM)),
        'c_forget_bias': 3.0 + nrm(ks[18], (N_ODD, C_HEADS), 0.5),
        'd_q_norm': gain(ks[19], (N_ODD, HEAD_DIM)),
        'd_k_norm': gain(ks[20], (N_ODD, HEAD_DIM)),
        'ffn_w_gate_up': nrm(ks[21], (DEPTH, D_MODEL, 2 * FF_HIDDEN), D_MODEL ** -0.5),
        'ffn_w_down': nrm(ks[22], (DEPTH, FF_HIDDEN, D_MODEL), FF_HIDDEN ** -0.5),
    }

def reference(x, c, ada_w, ada_b, mix_norm_g, ffn_norm_g, ab_w_in, ab_w_out, a_q_norm,
              a_k_norm, a_sink, b_q_norm, b_k_norm, b_rel_bias, cd_w_in, cd_w_out,
              c_q_norm, c_k_norm, c_forget_bias, d_q_norm, d_k_norm, ffn_w_gate_up,
              ffn_w_down):
    cond = jax.nn.silu(c)
    for layer in range(DEPTH):
        mods = cond @ ada_w[layer] + ada_b[layer]
        sh_m, sc_m, g_m, sh_f, sc_f, g_f = jnp.split(mods[:, None, :], 6, axis=-1)
        h = rms_norm(x, mix_norm_g[layer]) * (1 + sc_m) + sh_m
        i = layer // 2
        if layer % 2 == 0:
            y = mixer_ab(h, ab_w_in[i], ab_w_out[i], a_q_norm[i], a_k_norm[i], a_sink[i],
                         b_q_norm[i], b_k_norm[i], b_rel_bias[i])
        else:
            y = mixer_cd(h, cd_w_in[i], cd_w_out[i], c_q_norm[i], c_k_norm[i],
                         c_forget_bias[i], d_q_norm[i], d_k_norm[i])
        x = x + g_m * y
        h = rms_norm(x, ffn_norm_g[layer]) * (1 + sc_f) + sh_f
        x = x + g_f * swiglu(h, ffn_w_gate_up[layer], ffn_w_down[layer])
    return x


_drawn_inputs = setup_inputs


def setup_inputs(seed=0):
    import zlib

    import numpy as np

    out = dict(_drawn_inputs(seed))
    spreads = {}
    factors = {'ada_b': 3.128,
     'mix_norm_g': 2.777,
     'a_q_norm': 8.0,
     'a_k_norm': 8.0,
     'a_sink': 3.679,
     'b_q_norm': 8.0,
     'b_k_norm': 8.0,
     'b_rel_bias': 3.861,
     'c_q_norm': 8.0,
     'c_k_norm': 8.0,
     'c_forget_bias': 3.013,
     'd_q_norm': 8.0,
     'd_k_norm': 8.0}
    for name, (base, spread) in spreads.items():
        noise = np.random.default_rng([zlib.crc32(name.encode()), seed]).standard_normal(out[name].shape)
        drawn = base * np.exp(spread * noise) if base else spread * noise
        out[name] = __import__('jax').numpy.asarray(drawn.astype(out[name].dtype))
    for name, factor in factors.items():
        out[name] = (out[name] * factor).astype(out[name].dtype)
    return out
```

```python
from contextlib import ExitStack

import numpy as np
import concourse.bass as bass
from concourse import mybir

F32 = mybir.dt.float32
F32R = mybir.dt.float32r
BF16 = mybir.dt.bfloat16
I32 = mybir.dt.int32
ALU = mybir.AluOpType
ACT = mybir.ActivationFunctionType
AX = mybir.AxisListType

P = 128
D = 1024
S = 512
KC = D // P
TT = S // P
HD = 64
CHUNK = 64
FF = 2816
FT = FF // P
HALF = (12, 10)
AB_IN, CD_IN = 2304, 2508
IN_W = (AB_IN, CD_IN)
IN_SLOTS = (9, 10)
SLOT_BASE = (0, IN_SLOTS[0] + 4 + FT + 16)
REL = 256
RELW = 640
BIG = 1e30
OUT_OF_REACH = -1e38
TAKEN = -3.4e38
TOPK = 128
EPS = 1e-6
QA, KA, VA, QB, KB, VB = 0, 512, 640, 768, 1280, 1792
QC, KCOL, VC, FC, QD, KD, VD, QI, KI, WI = 0, 512, 1024, 1536, 1544, 2056, 2120, 2184, 2440, 2504
NORMED = (((QA, 10, 0), (QB, 16, 10)), ((QC, 16, 0), (QD, 9, 16)))
NSTAT = 26


class Group:

    def __init__(self, index, kind, qcol, qstat, kcol, kstat, vcol, qgain, kgain):
        self.index, self.kind = index, kind
        self.qcol, self.qstat, self.kcol, self.kstat = qcol, qstat, kcol, kstat
        self.vcol, self.qgain, self.kgain = vcol, qgain, kgain
        self.pair_keys = kind != "D"


GROUPS = (Group(0, "A", QA, 0, KA, 8, VA, 8, 9), Group(1, "B", QB, 10, KB, 18, VB, 10, 11),
          Group(2, "C", QC, 0, KCOL, 8, VC, 12, 13), Group(3, "D", QD, 16, KD, 24, VD, 14, 15))
JOB_BASE = (0, 8, 16, 24)
D_FIXED = 4
PAIRS = 4
UNITS_PER_PAIR = 2 * TT
W_FREE, RAW_FREE, ADA_FREE, ACC_FREE, PEV_FREE = 2, 2, 8, 2, 4
JOB_FREE, JEV_FREE, SC_FREE, SDV_FREE, PT_FREE, PTE_FREE, PV_FREE, O_FREE = 2, 2, 16, 2, 4, 2, 4, 2
GA_FREE, GHI_FREE, GLO_FREE = 2, 2, 2


def build_program(nc, x, c, ada_w, ada_b, mix_norm_g, ffn_norm_g, ab_w_in, ab_w_out, a_q_norm,
                  a_k_norm, a_sink, b_q_norm, b_k_norm, b_rel_bias, cd_w_in, cd_w_out,
                  c_q_norm, c_k_norm, c_forget_bias, d_q_norm, d_k_norm, ffn_w_gate_up,
                  ffn_w_down, out):
    ctx = ExitStack()
    with ctx:
        arena = nc.alloc_sbuf_tensor("arena", [P, 52000], F32)
        del arena
        base = [16640]

        def at(name, shape, dt=F32, offset=None):
            size = int(np.prod(shape[1:])) * (2 if dt == BF16 else 4)
            if offset is None:
                offset = base[0]
                base[0] += (size + 63) // 64 * 64
            t = nc.alloc_sbuf_tensor_at(name, shape, dt, offset=offset)
            return t, offset

        def sb(name, shape, dt=F32, offset=None):
            return at(name, shape, dt, offset)[0]

        xT = sb("xT", [P, KC, S])
        raw = [sb(f"raw{i}", [P, 2048]) for i in range(2)]
        whi = [sb(f"whi{i}", [P, 2048], F32R) for i in range(2)]
        wlo = [sb(f"wlo{i}", [P, 2048], F32R) for i in range(2)]
        ada_at = base[0]
        ada = [sb(f"ada{i}", [P, 4, 512]) for i in range(2)]
        toep = sb("toep", [P, 8, S], offset=ada_at)
        hhi, hhi_at = at("hhi", [P, KC, S], F32R)
        hlo, hlo_at = at("hlo", [P, KC, S], F32R)
        jn = [sb(f"jn{i}", [P, TT, P], offset=hhi_at + 2048 * i) for i in range(2)]
        qT = [sb(f"qT{i}", [P, S], offset=hhi_at + 4096 + 2048 * i) for i in range(2)]
        kT = [sb(f"kT{i}", [P, S], offset=hhi_at + 8192 + 2048 * i) for i in range(2)]
        kfix = sb("kfix", [P, 2, S], offset=hhi_at + 12288)
        PTs = sb("PTs", [P, 4, S], offset=hlo_at)
        sqs = sb("sqs", [P, 1664], offset=hlo_at)
        idxr = [sb(f"idxr{i}", [P, S], offset=hlo_at + 8192 + 2048 * i) for i in range(2)]
        cumT = sb("cumT", [8, S], offset=hlo_at + 12288)
        U = base[0]
        acthi = sb("acthi", [P, HALF[0], S], F32R)
        actlo = sb("actlo", [P, HALF[0], S], F32R)
        proj = [sb("projAB", [P, TT, AB_IN], offset=U), sb("projCD", [P, TT, CD_IN], offset=U)]
        xtok = sb("xtok", [P, TT, D], offset=U)
        TRI = sb("TRI", [P, 896], offset=U + TT * CD_IN * 4)
        SEL = sb("SEL", [8, 8, P], offset=U + TT * CD_IN * 4 + 3584)
        BT, BT_at = at("BT", [P, 8, S])
        nck = sb("nck", [P, 8, S], offset=BT_at)
        relv = sb("relv", [8, RELW], offset=BT_at)
        dsel = sb("dsel", [P, 1280])
        DS_OFF = (0, 128, 384, 768)
        Ssb, Ssb_at = at("Ssb", [P, 4, 520])
        sq = [sb(f"sq{i}", [P, S]) for i in range(2)]
        tmp = [sb(f"tmp{i}", [P, S]) for i in range(2)]
        AD = sb("AD", [P, S])
        AW = sb("AW", [P, 256])
        adi = sb("adi", [P, S], I32, offset=BT_at + 8192)
        ident = sb("ident", [P, P])
        identb = sb("identb", [P, P], BF16)
        maskb = sb("maskb", [P, P], BF16)
        ones = sb("ones", [P, P])
        diag = sb("diag", [P, TT, P], offset=Ssb_at)
        acc = [sb(f"acc{i}", [P, 512], offset=Ssb_at + 2048 + 2048 * i) for i in range(2)]
        rows1 = sb("rows1", [P, P], offset=Ssb_at + 6144)
        rows2 = sb("rows2", [16, P], offset=Ssb_at + 6656)
        cols1 = sb("cols1", [P, P])
        cols2 = sb("cols2", [P, 16])
        qg8 = sb("qg8", [P, 16])
        cond = sb("cond", [P, 8])
        mods = sb("mods", [P, 2, 48])
        coef = sb("coef", [P, 4, 8])
        snk = sb("snk", [P, 8])
        fb = sb("fb", [P, 8])
        slopes = sb("slopes", [P, 8])
        ssq = sb("ssq", [P, TT, NSTAT])
        rt = sb("rt", [P, TT, NSTAT])
        rs = sb("rs", [P, TT, NSTAT])
        nt1 = sb("nt1", [P, TT, NSTAT])
        nms = sb("nms", [P, TT])
        nsr = sb("nsr", [P, TT])
        nrs = sb("nrs", [P, TT])
        nnt = sb("nnt", [P, TT])
        epsc = sb("epsc", [P, 1])
        zt = sb("zt", [P, TT, 8])
        za = sb("za", [P, TT, 8])
        ze = sb("ze", [P, TT, 8])
        wis = sb("wis", [P, TT, 4])
        nm = sb("nm", [P, 4])
        scr4 = sb("scr4", [P, 4])
        rsum = [sb(f"rsum{i}", [P, TT, 2]) for i in range(2)]
        rinv = [sb(f"rinv{i}", [P, TT, 2]) for i in range(2)]
        top8 = sb("top8", [P, 8])
        assert base[0] <= 229000, base[0]

        psum = [ctx.enter_context(nc.psum_tensor(f"bank{i}", [P, 512], F32)) for i in range(8)]
        rel_scratch = nc.dram_tensor("rel_scratch", (8, RELW), F32, kind="Internal").ap()

        def sem(name):
            return ctx.enter_context(nc.semaphore(name))

        small_in = sem("small_in")
        x_in = sem("x_in")
        raw_in = [sem("raw_in0"), sem("raw_in1")]
        ada_in = [sem("ada_in0"), sem("ada_in1")]
        rel_in = sem("rel_in")
        rel_rev = sem("rel_rev")
        rel_out = sem("rel_out")
        bt_in = sem("bt_in")
        bt_ok = sem("bt_ok")
        y_out = sem("y_out")
        consts = sem("consts")
        tables = sem("tables")
        w_hi = sem("w_hi")
        w_lo = sem("w_lo")
        w_used = sem("w_used")
        ac_step = sem("ac_step")
        acc_used = sem("acc_used")
        mods_done = sem("mods_done")
        rows_t = sem("rows_t")
        cols_d = sem("cols_d")
        cond_ok = sem("cond_ok")
        dchain = sem("dchain")
        xt_mm = sem("xt_mm")
        x_done = sem("x_done")
        q_sq = sem("q_sq")
        ss_mm = sem("ss_mm")
        n_rt = sem("n_rt")
        n_dg = sem("n_dg")
        n_bc = sem("n_bc")
        h_t = sem("h_t")
        h_hi = sem("h_hi")
        h_lo = sem("h_lo")
        p_mm = sem("p_mm")
        p_ev = sem("p_ev")
        st_sq = sem("st_sq")
        st_rd = sem("st_rd")
        st_rt = sem("st_rt")
        st_ok = sem("st_ok")
        job_go = sem("job_go")
        job_in = sem("job_in")
        job_mm = sem("job_mm")
        job_ev = sem("job_ev")
        sc_mm = sem("sc_mm")
        sc_dv = sem("sc_dv")
        sc_mx = sem("sc_mx")
        sc_ex = sem("sc_ex")
        pt_mm = sem("pt_mm")
        pt_ev = sem("pt_ev")
        pv_mm = sem("pv_mm")
        o_done = sem("o_done")
        fg_z = sem("fg_z")
        fg_e = sem("fg_e")
        fg_l = sem("fg_l")
        fg_n = sem("fg_n")
        cm_mm = sem("cm_mm")
        cm_ev = sem("cm_ev")
        ix_mm = sem("ix_mm")
        ix_rl = sem("ix_rl")
        ix_ac = sem("ix_ac")
        tk = sem("tk")
        sel_done = sem("sel_done")
        ot_mm = sem("ot_mm")
        ot_hi = sem("ot_hi")
        ot_lo = sem("ot_lo")
        sink_in = sem("sink_in")
        o_rcp = sem("o_rcp")
        y_half = sem("y_half")
        g_si = sem("g_si")
        g_a = sem("g_a")
        g_hi = sem("g_hi")
        g_lo = sem("g_lo")
        yt_mm = sem("yt_mm")
        yt_ev = sem("yt_ev")

        w_in = (ab_w_in[0], cd_w_in[0])
        w_out = (ab_w_out[0], cd_w_out[0])
        OUT_BASE = [SLOT_BASE[l] + IN_SLOTS[l] for l in range(2)]
        GU_BASE = [[OUT_BASE[l] + 4, OUT_BASE[l] + 4 + HALF[0] + 8] for l in range(2)]
        DN_BASE = [[GU_BASE[l][0] + HALF[0], GU_BASE[l][1] + HALF[1]] for l in range(2)]
        N_SMALL = 6 + 1 + 16 + 2
        IN_BASE = (0, IN_SLOTS[0])
        ALL_EV = [4 * (IN_BASE[l] + IN_SLOTS[l]) + PEV_FREE for l in range(2)]

        def in_width(l, j):
            return min(256, IN_W[l] - 256 * j)

        def slot_width(l, stage, half=0, j=0):
            if stage == "in":
                return KC * in_width(l, j)
            return HALF[half] * P if stage == "down" else 2048

        block = ctx.enter_context(nc.Block())

        @block.sync
        def _(sp):
            sp.dma_start(rows2[0:8, :], c.rearrange("a (r f) -> (a r) f", f=P)).then_inc(small_in, 16)
            for i, g in enumerate((a_q_norm, a_k_norm, b_q_norm, b_k_norm, c_q_norm, c_k_norm,
                                   d_q_norm, d_k_norm)):
                for h in range(2):
                    sp.dma_start(rows2[8 + i:9 + i, HD * h:HD * h + HD], g).then_inc(small_in, 16)
            for l in range(2):
                sp.dma_start(rows1[48 * l:48 * l + 48, :],
                             ada_b[l].rearrange("(r f) -> r f", f=P)).then_inc(small_in, 16)
                sp.dma_start(rows1[96 + 8 * l:104 + 8 * l, :],
                             mix_norm_g[l].rearrange("(r f) -> r f", f=P)).then_inc(small_in, 16)
                sp.dma_start(rows1[112 + 8 * l:120 + 8 * l, :],
                             ffn_norm_g[l].rearrange("(r f) -> r f", f=P)).then_inc(small_in, 16)
            sp.dma_start(snk[:, :], a_sink.partition_broadcast(P)[:, 0, :]).then_inc(small_in, 16)
            sp.dma_start(fb[:, :], c_forget_bias.partition_broadcast(P)[:, 0, :])\
                .then_inc(small_in, 16)
            sp.dma_start(xtok[:, :, :], x[0].rearrange("(t p) f -> p t f", p=P)).then_inc(x_in, 16)
            sp.dma_start(relv[:, 0:384], b_rel_bias[0, :, REL - P + 1:2 * REL + 1])\
                .then_inc(rel_in, 16)

            def load(n, parity, dst_src):
                sp.wait_ge(w_lo, n + 1)
                for dst, src in dst_src:
                    sp.dma_start(dst, src).then_inc(raw_in[parity], 16)

            def in_slot(l, col, width, parity):
                dst = raw[parity][:, 0:KC * width].rearrange("p (k c) -> p k c", k=KC)
                src = w_in[l].rearrange("(k p) c -> p k c", p=P)
                return [(dst[:, 4 * a:4 * a + 4, :], src[:, 4 * a:4 * a + 4, bass.ds(col, width)])
                        for a in range(2)]

            def out_slot(l, i, parity):
                dst = raw[parity][:, :].rearrange("p (k c) -> p k c", k=KC)
                src = w_out[l].rearrange("(k p) c -> p k c", p=P)
                return [(dst[:, 4 * a:4 * a + 4, :],
                         src[:, 4 * a:4 * a + 4, 256 * i:256 * i + 256]) for a in range(2)]

            def gu_slot(l, col, parity):
                dst = raw[parity][:, :].rearrange("p (h k c) -> p h k c", h=2, k=KC)
                src = ffn_w_gate_up[l].rearrange("(k p) c -> p k c", p=P)
                return [(dst[:, h], src[:, :, bass.ds(col + FF * h, P)]) for h in range(2)]

            def down_slot(l, half, col, parity):
                n_k = HALF[half]
                row = P * HALF[0] * half
                dst = raw[parity][:, 0:n_k * P].rearrange("p (k c) -> p k c", k=n_k)
                src = ffn_w_down[l, row:row + P * n_k, :].rearrange("(k p) c -> p k c", p=P)
                m = n_k // 2
                return [(dst[:, a * m:a * m + m, :], src[:, a * m:a * m + m, bass.ds(col, P)])
                        for a in range(2)]

            for l in range(2):
                n0 = SLOT_BASE[l]
                with sp.Fori(0, 4) as pair_of_slots:
                    i = pair_of_slots * 2
                    for j in range(2):
                        b = (n0 + j) % 2
                        load(i + (n0 + j), b, in_slot(l, i * 256 + 256 * j, 256, b))
                for j in range(8, IN_SLOTS[l]):
                    b = (n0 + j) % 2
                    load(n0 + j, b, in_slot(l, 256 * j, in_width(l, j), b))
                if l == 0:
                    sp.wait_ge(rel_rev, 1)
                    sp.dma_start(rel_scratch, relv[:, :]).then_inc(rel_out, 16)
                    sp.wait_ge(rel_out, 16)
                    sp.wait_ge(ac_step, 12 * 8 + ADA_FREE)
                    sp.dma_start(toep[:, :, :], bass.AP(tensor=rel_scratch.tensor, offset=0,
                                                        ap=[[1, P], [RELW, 8], [1, S]]))\
                        .then_inc(bt_in, 16)
                for i in range(4):
                    n = OUT_BASE[l] + i
                    load(n, n % 2, out_slot(l, i, n % 2))
                for half in range(2):
                    n0 = GU_BASE[l][half]
                    with sp.Fori(0, HALF[half] // 2) as pair_of_slots:
                        i = pair_of_slots * 2
                        for j in range(2):
                            b = (n0 + j) % 2
                            load(i + (n0 + j), b,
                                 gu_slot(l, i * P + P * (HALF[0] * half + j), b))
                    n0 = DN_BASE[l][half]
                    with sp.Fori(0, 4) as pair_of_slots:
                        i = pair_of_slots * 2
                        for j in range(2):
                            b = (n0 + j) % 2
                            load(i + (n0 + j), b, down_slot(l, half, i * P + P * j, b))
            sp.wait_ge(yt_ev, KC)
            sp.dma_start(out[0].rearrange("(t p) f -> p t f", p=P), xtok[:, :, :])\
                .then_inc(y_out, 16)
            sp.wait_ge(y_out, 16)

        @block.gpsimd
        def _(pool):
            n_const = [0]

            def step(ins):
                n_const[0] += 1
                ins.then_inc(consts, 1)
                pool.wait_ge(consts, n_const[0])

            def ada_load(l, a, col, half):
                pool.wait_ge(ac_step, a * 4 + 4)
                src = ada_w[l].rearrange("(k p) c -> p k c", p=P)
                pool.dma_start(ada[half][:, :, :],
                               src[:, 4 * half:4 * half + 4, bass.ds(col, 512)])\
                    .then_inc(ada_in[half], 16)

            for a in range(2):
                ada_load(0, a, 0, a)
            step(nc.gpsimd.memset(ident[:, :], 0.0))
            step(nc.gpsimd.affine_select(out=ident[:, :], in_=ident[:, :],
                                         compare_op=ALU.not_equal, fill=1.0, base=0,
                                         pattern=[[-1, P]], channel_multiplier=1))
            step(nc.gpsimd.memset(ones[:, :], 1.0))
            step(nc.gpsimd.memset(epsc[:, :], EPS))
            step(nc.gpsimd.iota(adi[:, :], pattern=[[-1, S]], base=S - P, channel_multiplier=1))
            for a in range(2, 8):
                ada_load(0, a, 512 * (a // 2), a % 2)
            for h in range(8):
                step(nc.gpsimd.memset(slopes[:, h:h + 1], -2.0 ** (-(h + 1))))
            step(nc.gpsimd.memset(maskb[:, :], 0.0))
            step(nc.gpsimd.affine_select(out=maskb[:, :], in_=maskb[:, :], compare_op=ALU.is_ge,
                                         fill=-BIG, base=0, pattern=[[-1, P]],
                                         channel_multiplier=1))
            step(nc.gpsimd.tensor_copy(identb[:, :], ident[:, :]))
            with pool.Fori(0, 8) as i:
                for half in range(2):
                    ada_load(0, i * 2 + (8 + half), i * 512 + 2048, half)

            def scaled(n, parity, l, col, stat, doubled):
                pool.wait_ge(job_mm, n + 1)
                pool.sem_inc(job_go, 1)
                for h in range(2):
                    dh = 0 if doubled else h
                    ins = nc.gpsimd.tensor_tensor(
                        jn[parity][:, :, HD * h:HD * h + HD],
                        proj[l][:, :, bass.ds(col + HD * dh, HD)],
                        rs[:, :, bass.ds(stat + dh, 1)].to_broadcast([P, TT, HD]), ALU.mult)
                ins.then_inc(job_in, 1)

            def copied(n, parity, cols):
                pool.wait_ge(job_mm, n + 1)
                for h in range(2):
                    ins = nc.gpsimd.tensor_copy(jn[parity][:, :, HD * h:HD * h + HD],
                                                proj[1][:, :, cols[h]:cols[h] + HD])
                ins.then_inc(job_in, 1)

            for l in range(2):
                pool.wait_ge(p_ev, ALL_EV[l])
                pool.wait_ge(st_ok, l + 1)
                for g in GROUPS[2 * l:2 * l + 2]:
                    jb = JOB_BASE[g.index]
                    if g.kind == "D":
                        scaled(jb, 0, l, g.kcol, g.kstat, True)
                        copied(jb + 1, 1, (KI, KI))
                        for k in range(2):
                            copied(jb + 2 + k, k, (QI + P * k, QI + P * k + HD))
                        with pool.Fori(0, 2) as i:
                            for pp in range(2):
                                scaled(i * 2 + (jb + D_FIXED + pp), pp, l,
                                       i * 256 + (g.qcol + P * pp), i * 4 + (g.qstat + 2 * pp),
                                       False)
                        continue
                    with pool.Fori(0, 2) as i:
                        for pp in range(2):
                            scaled(i * 4 + (jb + 2 * pp), 0, l, i * 256 + (g.qcol + P * pp),
                                   i * 4 + (g.qstat + 2 * pp), False)
                            if g.kind == "A":
                                scaled(i * 4 + (jb + 2 * pp + 1), 1, l, i * HD + g.kcol,
                                       i + g.kstat, True)
                            else:
                                scaled(i * 4 + (jb + 2 * pp + 1), 1, l,
                                       i * 256 + (g.kcol + P * pp), i * 4 + (g.kstat + 2 * pp),
                                       False)
                if l == 0:
                    pool.wait_ge(bt_ok, 1)
                    with pool.Fori(0, 12) as i:
                        for half in range(2):
                            ada_load(1, i * 2 + (24 + half), i * 512, half)
                    pool.wait_ge(x_done, 8 + 24)
                    step(nc.gpsimd.memset(TRI[:, 0:384], 0.0))
                    step(nc.gpsimd.memset(TRI[:, 384:896], 1.0))
                    step(nc.gpsimd.affine_select(out=TRI[:, 384:512], in_=TRI[:, 384:512],
                                                 compare_op=ALU.is_ge, fill=0.0, base=0,
                                                 pattern=[[1, P]], channel_multiplier=-1))
                    step(nc.gpsimd.memset(SEL[:, :, :], 0.0))
                    step(nc.gpsimd.affine_select(out=SEL[:, :, :], in_=SEL[:, :, :],
                                                 compare_op=ALU.not_equal, fill=1.0, base=0,
                                                 pattern=[[-1, 8], [0, P]],
                                                 channel_multiplier=1))

        N_CONST0 = 5 + 8 + 3
        N_CONST1 = N_CONST0 + 5

        @block.scalar
        def _(act):
            act.sem_inc(p_ev, PEV_FREE)
            act.sem_inc(job_ev, JEV_FREE)
            act.sem_inc(pt_ev, PTE_FREE)
            act.sem_inc(g_hi, GHI_FREE)

            def cut_hi(n, b, landed, width):
                act.wait_ge(raw_in[b], landed)
                act.wait_ge(w_used, n + 1)
                nc.scalar.activation(whi[b][:, 0:width], raw[b][:, 0:width], ACT.Copy)\
                    .then_inc(w_hi, 1)

            def landed(n):
                return 32 * (n // 2 + 1)

            def square(q, b, x_ap, x_count):
                act.wait_ge(x_done, x_count)
                act.wait_ge(ss_mm, q)
                nc.scalar.activation(sq[b][:, :], x_ap, ACT.Square).then_inc(q_sq, 1)

            def norm_h(nn, shift, l):
                act.wait_ge(ss_mm, 8 * nn + 8 + 1)
                nc.scalar.activation(nsr[:, :], psum[6][:, 0:TT], ACT.Sqrt, bias=epsc[:, 0:1],
                                     scale=1.0 / D).then_inc(n_rt, 1)
                for k in range(KC):
                    act.wait_ge(h_t, 8 * nn + k + 1)
                    nc.scalar.activation(hhi[:, k, :], tmp[k % 2][:, :], ACT.Identity,
                                         bias=mods[:, l, shift + k:shift + k + 1])\
                        .then_inc(h_hi, 1)

            def in_out(l, s, j, t, width, col):
                if t < 3:
                    act.wait_ge(p_mm, s * 3 + (t + 1))
                else:
                    act.wait_ge(w_used, s + (SLOT_BASE[l] - IN_BASE[l] + 1 + W_FREE))
                nc.scalar.activation(proj[l][:, t, bass.ds(col, width)],
                                     psum[t][:, 0:width], ACT.Copy).then_inc(p_ev, 1)

            act.wait_ge(consts, 4)
            act.wait_ge(cols_d, 2)
            nc.scalar.activation(cond[:, :], cols2[:, 0:8], ACT.Silu).then_inc(cond_ok, 1)
            for m in range(KC):
                square(m, m % 2, xT[:, m, :], m + 1)
            cut_hi(0, 0, landed(0), 2048)

            for l in range(2):
                n0, s0 = SLOT_BASE[l], IN_BASE[l]
                norm_h(2 * l, 0, l)
                with act.Fori(0, 4) as pair_of_slots:
                    i = pair_of_slots * 2
                    for j in range(2):
                        b = (n0 + j + 1) % 2
                        cut_hi(i + (n0 + j + 1), b, i * 16 + landed(n0 + j + 1),
                               2048)
                        for t in range(TT):
                            in_out(l, i + (s0 + j), j, t, 256, i * 256 + 256 * j)
                for j in range(8, IN_SLOTS[l]):
                    nxt = slot_width(l, "in", j=j + 1) if j + 1 < IN_SLOTS[l] else 2048
                    cut_hi(n0 + j + 1, (n0 + j + 1) % 2, landed(n0 + j + 1), nxt)
                    for t in range(TT):
                        in_out(l, s0 + j, j, t, in_width(l, j), 256 * j)

                for t in range(TT):
                    act.wait_ge(p_ev, ALL_EV[l])
                    if t:
                        act.wait_ge(st_rd, 4 * l + t)
                    for r, (col, heads, stat) in enumerate(NORMED[l]):
                        ins = nc.scalar.activation(sqs[:, HD * stat:HD * (stat + heads)],
                                                   proj[l][:, t, col:col + HD * heads], ACT.Square)
                    ins.then_inc(st_sq, 1)
                nst = NORMED[l][1][2] + NORMED[l][1][1]
                act.wait_ge(st_rd, 4 * l + TT)
                nc.scalar.activation(rt[:, :, 0:nst], ssq[:, :, 0:nst], ACT.Sqrt,
                                     bias=epsc[:, 0:1], scale=1.0 / HD).then_inc(st_rt, 1)
                if l == 1:
                    act.wait_ge(fg_z, 2)
                    nc.scalar.activation(ze[:, :, :], za[:, :, :], ACT.Exp, scale=-1.0)\
                        .then_inc(fg_e, 1)
                    act.wait_ge(fg_e, 1)
                    nc.scalar.activation(za[:, :, :], ze[:, :, :], ACT.Ln, bias=ones[:, 0:1])\
                        .then_inc(fg_l, 1)
                    act.wait_ge(cm_mm, 1)
                    nc.scalar.activation(cumT[:, :], psum[0][0:8, :], ACT.Copy).then_inc(cm_ev, 1)
                    for h in range(8):
                        act.wait_ge(cm_mm, 2 + h)
                        nc.scalar.activation(nck[:, h, :], psum[2 + h % 2][:, :], ACT.Copy)\
                            .then_inc(cm_ev, 1)

                def turned(n, parity, dst, gain):
                    act.wait_ge(job_mm, n + (1 + JOB_FREE))
                    nc.scalar.activation(dst, psum[5 + parity][:, :], ACT.Copy,
                                         scale=gain).then_inc(job_ev, 1)

                for g in GROUPS[2 * l:2 * l + 2]:
                    jb, ub = JOB_BASE[g.index], 32 * g.index
                    if g.kind == "D":
                        turned(jb, 0, kfix[:, 0, :], cols2[:, g.kgain:g.kgain + 1])
                        turned(jb + 1, 1, kfix[:, 1, :], 1.0)
                        for k in range(2):
                            turned(jb + 2 + k, k, idxr[k][:, :], 1.0)
                        for t in range(1, TT):
                            for h in range(4):
                                u = 4 * (t - 1) + h
                                act.wait_ge(ix_mm, u + 1)
                                if u >= 2:
                                    act.wait_ge(ix_ac, u - 1)
                                nc.scalar.activation(sq[h % 2][:, 0:P * (t + 1)],
                                                     psum[h % 2][:, 0:P * (t + 1)], ACT.Relu)\
                                    .then_inc(ix_rl, 1)

                    def jobs(i, pp):
                        act.wait_ge(sc_mm, i * 16 + 8 * (4 * g.index + pp + 1))
                        q_gain = qg8[:, g.qgain:g.qgain + 1]
                        if g.kind == "D":
                            turned(i * 2 + (jb + D_FIXED + pp), pp, qT[pp][:, :], q_gain)
                        else:
                            turned(i * 4 + (jb + 2 * pp), 0, qT[pp][:, :], q_gain)
                            turned(i * 4 + (jb + 2 * pp + 1), 1, kT[pp][:, :],
                                   cols2[:, g.kgain:g.kgain + 1])

                    def width(t):
                        if g.kind == "A":
                            return P * min(t + 1, 2)
                        return P * (t + 1)

                    def exps(i, u):
                        t, h, pp = u % 8 // 2, u % 2, u // 8
                        w = width(t) + (g.kind == "A")
                        if u % 8 == 0:
                            act.wait_ge(o_done, i * 2 + (4 * g.index + pp + 1))
                        act.wait_ge(sc_mx, i * 16 + (ub + u + 1))
                        nc.scalar.activation(Ssb[:, u % 4, 0:w], Ssb[:, u % 4, 0:w], ACT.Exp,
                                             bias=nm[:, u % 4:u % 4 + 1],
                                             accum_out=rsum[pp][:, t, h:h + 1]).then_inc(sc_ex, 1)

                    def probs_out(i, u):
                        w = width(u % 8 // 2)
                        act.wait_ge(pt_mm, i * 16 + (ub + u + 1 + PT_FREE))
                        act.wait_ge(pv_mm, i * 16 + (ub + u + 1))
                        nc.scalar.activation(PTs[:, u % 4, 0:w], psum[2 + u % 2][:, 0:w],
                                             ACT.Copy).then_inc(pt_ev, 1)

                    with act.Fori(0, 2) as i:
                        jobs(i, 0)
                        for u in range(16):
                            if u == 4:
                                jobs(i, 1)
                            exps(i, u)
                            if u >= 2:
                                probs_out(i, u - 2)
                        for u in (14, 15):
                            probs_out(i, u)

                for f in range(KC):
                    act.wait_ge(ot_mm, 8 * l + f + 1)
                    nc.scalar.activation(hhi[:, f, :], psum[5 + f % 2][:, :], ACT.Copy)\
                        .then_inc(ot_hi, 1)

                for i in range(4):
                    n = OUT_BASE[l] + i
                    cut_hi(n + 1, (n + 1) % 2, landed(n + 1), 2048)
                    for m in (2 * i, 2 * i + 1):
                        square(16 * l + 8 + m, m % 2, xT[:, m, :], 24 * l + 8 + m + 1)
                norm_h(2 * l + 1, 24, l)

                for half in range(2):
                    nh, n0, f0 = HALF[half], GU_BASE[l][half], FT * l + HALF[0] * half

                    def hidden(n, f, b, out_ap):
                        act.wait_ge(w_used, n + (1 + W_FREE))
                        act.wait_ge(g_a, f + 1)
                        nc.scalar.activation(sq[b][:, :], psum[2 * b][:, :], ACT.Silu)\
                            .then_inc(g_si, 1)
                        act.wait_ge(g_a, f + (1 + GA_FREE))
                        nc.scalar.activation(out_ap, tmp[b][:, :], ACT.Copy).then_inc(g_hi, 1)

                    with act.Fori(0, nh // 2 - 1) as pair_of_slots:
                        i = pair_of_slots * 2
                        for j in range(2):
                            b = (n0 + j + 1) % 2
                            cut_hi(i + (n0 + j + 1), b, i * 16 + landed(n0 + j + 1), 2048)
                            hidden(i + (n0 + j), i + (f0 + j), j,
                                   acthi[:, bass.ds(i + j, 1), :])
                    for j in (nh - 2, nh - 1):
                        nxt = 2048 if j < nh - 1 else nh * P
                        cut_hi(n0 + j + 1, (n0 + j + 1) % 2, landed(n0 + j + 1), nxt)
                        hidden(n0 + j, f0 + j, j % 2, acthi[:, j:j + 1, :])
                    n0 = DN_BASE[l][half]
                    with act.Fori(0, 3) as pair_of_slots:
                        i = pair_of_slots * 2
                        for j in range(2):
                            b = (n0 + j + 1) % 2
                            cut_hi(i + (n0 + j + 1), b, i * 16 + landed(n0 + j + 1), nh * P)
                            if half == 1 and l == 0:
                                square(i + (16 * l + 16 + j), j, xT[:, bass.ds(i + j, 1), :],
                                       i + (24 * l + 24 + j + 1))
                    for j in (6, 7):
                        last = l == 1 and half == 1 and j == 7
                        if not last:
                            nxt = nh * P if j == 6 else 2048
                            cut_hi(n0 + j + 1, (n0 + j + 1) % 2, landed(n0 + j + 1), nxt)
                        if half == 1 and l == 0:
                            square(16 * l + 16 + j, j % 2, xT[:, j, :], 24 * l + 24 + j + 1)

            for m in range(KC):
                act.wait_ge(yt_mm, m + 1)
                nc.scalar.activation(xtok[:, :, P * m:P * m + P],
                                     psum[m % 2][:, :].rearrange("p (t c) -> p t c", t=TT),
                                     ACT.Copy).then_inc(yt_ev, 1)

        @block.vector
        def _(dve):
            dve.sem_inc(w_lo, RAW_FREE)
            dve.sem_inc(ac_step, ADA_FREE)
            dve.sem_inc(sc_dv, SDV_FREE)
            dve.sem_inc(o_done, O_FREE)
            dve.sem_inc(g_a, GA_FREE)
            dve.sem_inc(g_lo, GLO_FREE)
            links = [0]

            def link(ins):
                links[0] += 1
                ins.then_inc(dchain, 1)
                dve.wait_ge(dchain, links[0])

            def cut_lo(n, b, width):
                dve.wait_ge(w_hi, n + 1)
                nc.vector.tensor_tensor(wlo[b][:, 0:width], raw[b][:, 0:width],
                                        whi[b][:, 0:width], ALU.subtract).then_inc(w_lo, 1)

            def ada_panel(panel, landed, b):
                for half in range(2):
                    dve.wait_ge(ada_in[half], landed)
                    for k in range(4):
                        s = 4 * half + k
                        src, by = ada[half][:, k, :], cond[:, s:s + 1]
                        dve.wait_ge(ac_step, panel * 8 + (s + ADA_FREE))
                        if s == 0:
                            dve.wait_ge(acc_used, panel + 1)
                            ins = nc.vector.tensor_scalar(acc[b][:, :], src, by, None, ALU.mult)
                        else:
                            ins = nc.vector.scalar_tensor_tensor(
                                out=acc[b][:, :], in0=src, scalar=by, in1=acc[b][:, :],
                                op0=ALU.mult, op1=ALU.add)
                        ins.then_inc(ac_step, 1)

            def take_mods(l, lo, hi, panels):
                dve.wait_ge(acc_used, panels + ACC_FREE)
                link(nc.vector.tensor_tensor(mods[:, l, lo:hi], psum[7][:, lo:hi],
                                             cols1[:, 48 * l + lo:48 * l + hi], ALU.add))

            def take_coef(nn, l, scale, gain):
                link(nc.vector.scalar_tensor_tensor(
                    out=coef[:, nn, :], in0=mods[:, l, scale:scale + 8], scalar=1.0,
                    in1=cols1[:, gain:gain + 8], op0=ALU.add, op1=ALU.mult))

            def inverse(out_ap, root, mean, t1):
                link(nc.vector.reciprocal(out_ap, root))
                link(nc.vector.tensor_tensor(t1, out_ap, out_ap, ALU.mult))
                link(nc.vector.tensor_tensor(t1, t1, mean, ALU.mult))
                link(nc.vector.tensor_scalar(t1, t1, -0.5, 1.5, ALU.mult, ALU.add))
                return nc.vector.tensor_tensor(out_ap, out_ap, t1, ALU.mult)

            def norm_h(nn, l, shift):
                dve.wait_ge(n_rt, nn + 1)
                link(nc.vector.tensor_scalar(nms[:, :], psum[6][:, 0:TT], 1.0 / D, EPS,
                                             ALU.mult, ALU.add))
                link(inverse(nrs[:, :], nsr[:, :], nms[:, :], nnt[:, :]))
                for t in range(TT):
                    ins = nc.vector.tensor_scalar(diag[:, t, :], ident[:, :], nrs[:, t:t + 1],
                                                  None, ALU.mult)
                ins.then_inc(n_dg, 1)
                dve.wait_ge(n_bc, nn + 1)

                def lo(k):
                    dve.wait_ge(h_hi, 8 * nn + k + 1)
                    nc.vector.scalar_tensor_tensor(
                        out=hlo[:, k, :], in0=tmp[k % 2][:, :],
                        scalar=mods[:, l, shift + k:shift + k + 1], in1=hhi[:, k, :],
                        op0=ALU.add, op1=ALU.subtract).then_inc(h_lo, 1)

                for k in range(KC):
                    if k >= 2:
                        dve.wait_ge(h_lo, 8 * nn + k - 1)
                    nc.vector.scalar_tensor_tensor(
                        out=tmp[k % 2][:, :], in0=xT[:, k, :], scalar=coef[:, nn, k:k + 1],
                        in1=psum[5][:, :], op0=ALU.mult, op1=ALU.mult).then_inc(h_t, 1)
                    if k:
                        lo(k - 1)
                lo(KC - 1)

            for r, (dst, n) in enumerate(((cols1, P), (cols2, 16))):
                dve.wait_ge(rows_t, 2)
                nc.vector.tensor_copy(dst[:, :], psum[5][:, P * r:P * r + n]).then_inc(cols_d, 1)
            dve.wait_ge(cols_d, 2)
            link(nc.vector.tensor_scalar(qg8[:, :], cols2[:, :], HD ** -0.5, None, ALU.mult))
            for k in range(KC):
                dve.wait_ge(xt_mm, k + 1)
                nc.vector.tensor_copy(xT[:, k, :], psum[k % 2][:, :]).then_inc(x_done, 1)
            dve.wait_ge(consts, 5)
            nc.vector.scalar_tensor_tensor(out=AD[:, :], in0=adi[:, :], scalar=-1.0,
                                           in1=adi[:, :], op0=ALU.mult, op1=ALU.max)\
                .then_inc(tables, 1)
            dve.wait_ge(tables, 1)
            link(nc.vector.memset(AD[0:CHUNK, 448:512], BIG))
            link(nc.vector.tensor_copy(AW[:, :], AD[:, 256:512]))
            link(nc.vector.memset(AW[0:CHUNK, 0:64], BIG))
            link(nc.vector.memset(AW[CHUNK:P, 0:128], BIG))
            dve.wait_ge(rel_in, 16)
            nc.vector.tensor_copy(relv[:, 384:RELW], relv[:, 383:384].to_broadcast([8, 256]))\
                .then_inc(rel_rev, 1)
            dve.wait_ge(cond_ok, 1)
            for panel in range(4):
                ada_panel(panel, 16 * (panel + 1), panel % 2)
            take_mods(0, 0, 16, 4)
            take_coef(0, 0, 8, 96)
            cut_lo(0, 0, 2048)

            for l in range(2):
                n0 = SLOT_BASE[l]
                norm_h(2 * l, l, 0)
                with dve.Fori(0, 4) as pair_of_slots:
                    i = pair_of_slots * 2
                    for j in range(2):
                        cut_lo(i + (n0 + j + 1), (n0 + j + 1) % 2, 2048)
                        if l == 0:
                            ada_panel(i + (4 + j), i * 16 + 16 * (5 + j), j)
                for j in range(8, IN_SLOTS[l]):
                    nxt = slot_width(l, "in", j=j + 1) if j + 1 < IN_SLOTS[l] else 2048
                    cut_lo(n0 + j + 1, (n0 + j + 1) % 2, nxt)
                if l == 0:
                    take_mods(0, 16, 48, 12)
                    take_coef(1, 0, 32, 112)
                    nc.vector.memset(scr4[:, 0:1], 0.0).then_inc(mods_done, 1)

                for t in range(TT):
                    dve.wait_ge(st_sq, 4 * l + t + 1)
                    nst = NORMED[l][1][2] + NORMED[l][1][1]
                    nc.vector.tensor_reduce(
                        ssq[:, t, 0:nst],
                        sqs[:, 0:HD * nst].rearrange("p (h d) -> p h d", d=HD),
                        AX.X, ALU.add).then_inc(st_rd, 1)
                dve.wait_ge(st_rt, l + 1)
                link(nc.vector.tensor_scalar(ssq[:, :, 0:nst], ssq[:, :, 0:nst], 1.0 / HD, EPS,
                                             ALU.mult, ALU.add))
                inverse(rs[:, :, 0:nst], rt[:, :, 0:nst], ssq[:, :, 0:nst],
                        nt1[:, :, 0:nst]).then_inc(st_ok, 1)
                if l == 0:
                    dve.wait_ge(bt_in, 16)
                    link(nc.vector.tensor_copy(BT[:, :, :], toep[:, :, ::-1]))
                    nc.vector.memset(BT[0:CHUNK, :, S - CHUNK:S], -BIG).then_inc(bt_ok, 1)
                    dve.wait_ge(bt_ok, 1)
                else:
                    link(nc.vector.tensor_tensor(
                        zt[:, :, :], proj[1][:, :, FC:FC + 8],
                        fb[:, :].unsqueeze(1).to_broadcast([P, TT, 8]), ALU.add))
                    nc.vector.scalar_tensor_tensor(out=za[:, :, :], in0=zt[:, :, :], scalar=-1.0,
                                                   in1=zt[:, :, :], op0=ALU.mult, op1=ALU.max)\
                        .then_inc(fg_z, 1)
                    link(nc.vector.tensor_scalar(zt[:, :, :], zt[:, :, :], 0.0, None, ALU.min))
                    nc.vector.tensor_scalar(wis[:, :, :], proj[1][:, :, WI:WI + 4],
                                            (HD * 4) ** -0.5, None, ALU.mult).then_inc(fg_z, 1)
                    dve.wait_ge(fg_l, 1)
                    nc.vector.tensor_tensor(zt[:, :, :], za[:, :, :], zt[:, :, :], ALU.subtract)\
                        .then_inc(fg_n, 1)
                    dve.wait_ge(cm_ev, 9)

                for g in GROUPS[2 * l:2 * l + 2]:
                    ub = 32 * g.index
                    if g.kind == "D":
                        for t in range(1, TT):
                            w = P * (t + 1)
                            row = dsel[:, DS_OFF[t]:DS_OFF[t] + w]
                            for h in range(4):
                                v = 4 * (t - 1) + h
                                dve.wait_ge(ix_rl, v + 1)
                                by = wis[:, t, h:h + 1]
                                if h == 0:
                                    ins = nc.vector.tensor_scalar(row, sq[h % 2][:, 0:w], by, 0.0,
                                                                  ALU.mult, ALU.add)
                                else:
                                    dve.wait_ge(ix_ac, v)
                                    ins = nc.vector.scalar_tensor_tensor(
                                        out=row, in0=sq[h % 2][:, 0:w], scalar=by, in1=row,
                                        op0=ALU.mult, op1=ALU.add)
                                ins.then_inc(ix_ac, 1)
                        dve.wait_ge(ix_ac, 12)
                        for t in range(1, TT):
                            w = P * (t + 1)
                            row = dsel[:, DS_OFF[t]:DS_OFF[t] + w]
                            link(nc.vector.memset(
                                dsel[0:CHUNK, DS_OFF[t] + w - 64:DS_OFF[t] + w], OUT_OF_REACH))
                            for q in range(TOPK // 8):
                                s = TOPK // 8 * 2 * (t - 1) + 2 * q
                                nc.vector.max(top8[:, :], row).then_inc(tk, 1)
                                dve.wait_ge(tk, s + 1)
                                nc.vector.match_replace(row, top8[:, :], row, TAKEN)\
                                    .then_inc(tk, 1)
                                dve.wait_ge(tk, s + 2)
                            link(nc.vector.tensor_scalar(row, row, 2 * OUT_OF_REACH, BIG,
                                                         ALU.is_gt, ALU.mult))
                            link(nc.vector.tensor_tensor(row, row, AD[:, S - w:S], ALU.add))
                        link(nc.vector.tensor_copy(dsel[:, 0:P], AD[:, S - P:S]))

                    def unit(i, u):
                        t, h, pp = u % 8 // 2, u % 2, u // 8
                        w = P * (min(t + 1, 2) if g.kind == "A" else t + 1)
                        dve.wait_ge(sc_mm, i * 16 + (ub + u + 1 + SC_FREE))
                        dve.wait_ge(pt_mm, i * 16 + (ub + u + 1))
                        head = i * 4 + (2 * pp + h)
                        if g.kind == "A":
                            table, by = AW[:, 256 - w:256], slopes[:, bass.ds(head, 1)]
                        elif g.kind == "B":
                            table, by = BT[:, bass.ds(head, 1), S - w:S], 1.0
                        elif g.kind == "C":
                            table, by = nck[:, bass.ds(head, 1), 0:w], 1.0
                        else:
                            table = dsel[:, DS_OFF[t]:DS_OFF[t] + w]
                            by = slopes[:, bass.ds(head, 1)]
                        s_out = Ssb[:, u % 4, 0:w]
                        if g.kind in "AD":
                            nc.vector.scalar_tensor_tensor(
                                out=s_out, in0=table, scalar=by, in1=psum[u % 2][:, 0:w],
                                op0=ALU.mult, op1=ALU.add).then_inc(sc_dv, 1)
                        else:
                            nc.vector.tensor_tensor(s_out, psum[u % 2][:, 0:w],
                                                    table if g.kind == "A" else
                                                    table.rearrange("p a w -> p (a w)"),
                                                    ALU.add).then_inc(sc_dv, 1)
                        if g.kind == "A":
                            nc.vector.tensor_copy(Ssb[:, u % 4, w:w + 1],
                                                  snk[:, bass.ds(head, 1)]).then_inc(sink_in, 1)
                            dve.wait_ge(sink_in, i * 16 + (ub + u + 1))
                            w += 1
                        dve.wait_ge(sc_dv, i * 16 + (ub + u + 1 + SDV_FREE))
                        nc.vector.tensor_reduce(nm[:, u % 4:u % 4 + 1], Ssb[:, u % 4, 0:w],
                                                AX.X, ALU.max, negate=True).then_inc(sc_mx, 1)

                    def normalise(i, pp):
                        pair = i * 2 + (4 * g.index + pp)
                        dve.wait_ge(pv_mm, i * 16 + (ub + 8 * pp + 8 + PV_FREE))
                        nc.vector.reciprocal(rinv[pp][:, :, :], rsum[pp][:, :, :])\
                            .then_inc(o_rcp, 1)
                        dve.wait_ge(o_rcp, pair + 1)
                        bank = psum[4 if pp == 0 else 7]
                        src = bank[:, :].rearrange("p (t c) -> p t c", t=TT)
                        for h in range(2):
                            ins = nc.vector.tensor_tensor(
                                proj[l][:, :, bass.ds(i * 256 + (g.qcol + P * pp + HD * h), HD)],
                                src[:, :, HD * h:HD * h + HD],
                                rinv[pp][:, :, h:h + 1].to_broadcast([P, TT, HD]), ALU.mult)
                        ins.then_inc(o_done, 1)

                    with dve.Fori(0, 2) as i:
                        for u in range(16):
                            unit(i, u)
                            if u == 11:
                                normalise(i, 0)
                        normalise(i, 1)

                for f in range(KC):
                    dve.wait_ge(ot_hi, 8 * l + f + 1)
                    nc.vector.tensor_tensor(hlo[:, f, :], psum[5 + f % 2][:, :], hhi[:, f, :],
                                            ALU.subtract).then_inc(ot_lo, 1)

                def add_chunk(bank, gate, m, x_ap):
                    nc.vector.scalar_tensor_tensor(
                        out=x_ap, in0=psum[bank][:, :], scalar=mods[:, l, bass.ds(gate + m, 1)]
                        if not isinstance(m, int) else mods[:, l, gate + m:gate + m + 1],
                        in1=x_ap, op0=ALU.mult, op1=ALU.add).then_inc(x_done, 1)

                for i in range(4):
                    n = OUT_BASE[l] + i
                    cut_lo(n + 1, (n + 1) % 2, 2048)
                    dve.wait_ge(y_half, 4 * l + i + 1)
                    add_chunk(4, 16, 2 * i, xT[:, 2 * i, :])
                    dve.wait_ge(w_used, n + 1 + W_FREE)
                    add_chunk(5, 16, 2 * i + 1, xT[:, 2 * i + 1, :])
                norm_h(2 * l + 1, l, 24)

                for half in range(2):
                    nh, n0, f0 = HALF[half], GU_BASE[l][half], FT * l + HALF[0] * half

                    def hidden(n, f, b, hi_ap, lo_ap):
                        dve.wait_ge(g_si, f + 1)
                        dve.wait_ge(g_hi, f + 1)
                        dve.wait_ge(g_lo, f + 1)
                        nc.vector.tensor_tensor(tmp[b][:, :], sq[b][:, :], psum[2 * b + 1][:, :],
                                                ALU.mult).then_inc(g_a, 1)
                        dve.wait_ge(g_hi, f + (1 + GHI_FREE))
                        nc.vector.tensor_tensor(lo_ap, tmp[b][:, :], hi_ap, ALU.subtract)\
                            .then_inc(g_lo, 1)

                    with dve.Fori(0, nh // 2 - 1) as pair_of_slots:
                        i = pair_of_slots * 2
                        for j in range(2):
                            cut_lo(i + (n0 + j + 1), (n0 + j + 1) % 2, 2048)
                            if l == 0 and half == 0:
                                ada_panel(i + (12 + j), i * 16 + 16 * (13 + j), j)
                            hidden(i + (n0 + j), i + (f0 + j), j,
                                   acthi[:, bass.ds(i + j, 1), :], actlo[:, bass.ds(i + j, 1), :])
                    for j in (nh - 2, nh - 1):
                        cut_lo(n0 + j + 1, (n0 + j + 1) % 2, 2048 if j < nh - 1 else nh * P)
                        if l == 0 and half == 0:
                            ada_panel(12 + j, 16 * (13 + j), j % 2)
                        hidden(n0 + j, f0 + j, j % 2, acthi[:, j:j + 1, :], actlo[:, j:j + 1, :])
                    if l == 0 and half == 0:
                        take_mods(1, 0, 48, 24)
                        take_coef(2, 1, 8, 104)
                        take_coef(3, 1, 32, 120)
                    n0 = DN_BASE[l][half]
                    with dve.Fori(0, 3) as pair_of_slots:
                        i = pair_of_slots * 2
                        for j in range(2):
                            cut_lo(i + (n0 + j + 1), (n0 + j + 1) % 2, nh * P)
                            dve.wait_ge(w_used, i + (n0 + j + 1 + W_FREE))
                            add_chunk(4 + j, 40, i + j, xT[:, bass.ds(i + j, 1), :])
                    for j in (6, 7):
                        if not (l == 1 and half == 1 and j == 7):
                            cut_lo(n0 + j + 1, (n0 + j + 1) % 2, nh * P if j == 6 else 2048)
                        dve.wait_ge(w_used, n0 + j + 1 + W_FREE)
                        add_chunk(4 + j % 2, 40, j, xT[:, j, :])

        @block.tensor
        def _(pe):
            pe.sem_inc(w_used, W_FREE)
            pe.sem_inc(acc_used, ACC_FREE)
            pe.sem_inc(job_mm, JOB_FREE)
            pe.sem_inc(sc_mm, SC_FREE)
            pe.sem_inc(pt_mm, PT_FREE)
            pe.sem_inc(pv_mm, PV_FREE)
            pe.sem_inc(ss_mm, 1)

            def three(dst, a_hi, a_lo, b_hi, b_lo, first, last):
                nc.tensor.matmul(dst, a_hi, b_hi, start=first, stop=False)
                nc.tensor.matmul(dst, a_hi, b_lo, start=False, stop=False)
                return nc.tensor.matmul(dst, a_lo, b_hi, start=False, stop=last)

            def sum_squares(q, b, first, last):
                pe.wait_ge(q_sq, q + 1)
                for t in range(TT):
                    ins = nc.tensor.matmul(psum[6][:, t:t + 1], sq[b][:, P * t:P * t + P],
                                           ones[:, 0:1], start=first and t == 0, stop=last,
                                           skip_group_check=True)
                ins.then_inc(ss_mm, 1)

            def spread(nn):
                pe.wait_ge(n_dg, nn + 1)
                for t in range(TT):
                    ins = nc.tensor.matmul(psum[5][:, P * t:P * t + P], ones[:, :], diag[:, t, :],
                                           start=True, stop=True)
                ins.then_inc(n_bc, 1)

            def mods_mm(panel, b, col):
                pe.wait_ge(ac_step, panel * 8 + (8 + ADA_FREE))
                for j in range(4):
                    ins = nc.tensor.matmul(psum[7][:, bass.ds(col + j, 1)],
                                           acc[b][:, P * j:P * j + P], ones[:, 0:1],
                                           start=True, stop=True)
                ins.then_inc(acc_used, 1)

            pe.wait_ge(consts, 3)
            pe.wait_ge(small_in, 16 * N_SMALL)
            nc.tensor.transpose(psum[5][:, 0:P], rows1[:, :], ident[:, :]).then_inc(rows_t, 1)
            nc.tensor.transpose(psum[5][:, P:P + 16], rows2[:, :], ident[0:16, 0:16])\
                .then_inc(rows_t, 1)
            pe.wait_ge(x_in, 16)
            for k in range(KC):
                if k >= 2:
                    pe.wait_ge(x_done, k - 1)
                for t in range(TT):
                    ins = nc.tensor.transpose(psum[k % 2][:, P * t:P * t + P],
                                              xtok[:, t, P * k:P * k + P], ident[:, :])
                ins.then_inc(xt_mm, 1)
            for m in range(KC):
                sum_squares(m, m % 2, m == 0, m == KC - 1)
            for panel in range(4):
                mods_mm(panel, panel % 2, 4 * panel)

            for l in range(2):
                n0, s0 = SLOT_BASE[l], IN_BASE[l]
                pe.wait_ge(cols_d, 2)
                spread(2 * l)
                pe.wait_ge(h_lo, 16 * l + 8)

                def project(n, s, j, width):
                    b = (n0 + j) % 2
                    pe.wait_ge(w_lo, n + (1 + RAW_FREE))
                    for t in range(TT):
                        pe.wait_ge(p_ev, s * 4 + (t + 1))
                        for k in range(KC):
                            tok = slice(P * t, P * t + P)
                            cols = slice(k * width, k * width + width)
                            ins = three(psum[t][:, 0:width], hhi[:, k, tok],
                                        hlo[:, k, tok], whi[b][:, cols], wlo[b][:, cols],
                                        k == 0, k == KC - 1)
                        ins.then_inc(p_mm if t < 3 else w_used, 1)

                with pe.Fori(0, 4) as pair_of_slots:
                    i = pair_of_slots * 2
                    for j in range(2):
                        project(i + (n0 + j), i + (s0 + j), j, 256)
                        if l == 0:
                            mods_mm(i + (4 + j), j, i * 4 + (16 + 4 * j))
                for j in range(8, IN_SLOTS[l]):
                    project(n0 + j, s0 + j, j, in_width(l, j))

                if l == 1:
                    pe.wait_ge(consts, N_CONST1)
                    pe.wait_ge(fg_n, 1)
                    pe.wait_ge(p_ev, ALL_EV[1])
                    for t in range(TT):
                        ins = nc.tensor.matmul(psum[0][0:8, :], zt[:, t, :],
                                               TRI[:, 384 - P * t:896 - P * t],
                                               start=t == 0, stop=t == TT - 1)
                    ins.then_inc(cm_mm, 1)
                    pe.wait_ge(cm_ev, 1)
                    for h in range(8):
                        if h >= 2:
                            pe.wait_ge(cm_ev, h)
                        nc.tensor.matmul(psum[2 + h % 2][:, :], SEL[:, h, :], cumT[:, :],
                                         start=True, stop=True).then_inc(cm_mm, 1)

                pe.wait_ge(p_ev, ALL_EV[l])
                if l == 0:
                    pe.wait_ge(mods_done, 1)
                pe.wait_ge(consts, N_CONST0)
                for g in GROUPS[2 * l:2 * l + 2]:
                    jb, ub = JOB_BASE[g.index], 32 * g.index

                    def turn(n, parity):
                        pe.wait_ge(job_in, n + 1)
                        pe.wait_ge(job_ev, n + 1)
                        for t in range(TT):
                            ins = nc.tensor.transpose(psum[5 + parity][:, P * t:P * t + P],
                                                      jn[parity][:, t, :], ident[:, :])
                        ins.then_inc(job_mm, 1)

                    if g.kind == "D":
                        for k in range(D_FIXED):
                            turn(jb + k, k % 2)
                        pe.wait_ge(job_ev, jb + D_FIXED + JEV_FREE)
                        pe.wait_ge(sc_dv, ub + SDV_FREE)
                        for t in range(1, TT):
                            for h in range(4):
                                v = 4 * (t - 1) + h
                                if v >= 2:
                                    pe.wait_ge(ix_rl, v - 1)
                                rows = slice(HD * (h % 2), HD * (h % 2) + HD)
                                nc.tensor.matmul(psum[h % 2][:, 0:P * (t + 1)],
                                                 idxr[h // 2][rows, P * t:P * t + P],
                                                 kfix[rows, 1, 0:P * (t + 1)],
                                                 start=True, stop=True).then_inc(ix_mm, 1)
                        pe.wait_ge(ix_rl, 12)

                    def jobs(i, pp):
                        if g.kind == "D":
                            turn(i * 2 + (jb + D_FIXED + pp), pp)
                        else:
                            for q in range(2):
                                turn(i * 4 + (jb + 2 * pp + q), q)

                    def scores(i, u):
                        t, h, pp = u % 8 // 2, u % 2, u // 8
                        if u % 8 == 0:
                            if g.kind == "D":
                                pe.wait_ge(job_ev, i * 2 + (jb + D_FIXED + pp + 1 + JEV_FREE))
                            else:
                                pe.wait_ge(job_ev, i * 4 + (jb + 2 * pp + 2 + JEV_FREE))
                        pe.wait_ge(sc_dv, i * 16 + (ub + u + 1))
                        rows = slice(HD * h, HD * h + HD)
                        first = max(t - 1, 0) if g.kind == "A" else 0
                        w = P * (t + 1 - first)
                        keys = kfix[rows, 0, :] if g.kind == "D" else kT[pp][rows, :]
                        query = qT[pp][rows, P * t:P * t + P]
                        if g.kind == "C":
                            if t:
                                nc.tensor.matmul(psum[u % 2][:, 0:w - P], query,
                                                 keys[:, 0:w - P], start=True, stop=True)
                            nc.tensor.matmul(psum[u % 2][:, w - P:w], identb[:, :], maskb[:, :],
                                             start=True, stop=False)
                            ins = nc.tensor.matmul(psum[u % 2][:, w - P:w], query,
                                                   keys[:, w - P:w], start=False, stop=True)
                        else:
                            ins = nc.tensor.matmul(psum[u % 2][:, 0:w], query,
                                                   keys[:, P * first:P * first + w],
                                                   start=True, stop=True)
                        ins.then_inc(sc_mm, 1)

                    def turn_probs(i, u):
                        t = u % 8 // 2
                        pe.wait_ge(sc_ex, i * 16 + (ub + u + 1))
                        pe.wait_ge(pt_ev, i * 16 + (ub + u + 1))
                        for k in range(min(t + 1, 2) if g.kind == "A" else t + 1):
                            ins = nc.tensor.transpose(psum[2 + u % 2][:, P * k:P * k + P],
                                                      Ssb[:, u % 4, P * k:P * k + P], ident[:, :])
                        ins.then_inc(pt_mm, 1)

                    def values(i, u):
                        t, h, pp = u % 8 // 2, u % 2, u // 8
                        if u % 8 == 0:
                            pe.wait_ge(o_done, i * 2 + (4 * g.index + pp + 1))
                        pe.wait_ge(pt_ev, i * 16 + (ub + u + 1 + PTE_FREE))
                        if g.kind == "A":
                            vcol = i * HD + g.vcol
                        elif g.kind == "D":
                            vcol = g.vcol
                        else:
                            vcol = i * 256 + (g.vcol + P * pp + HD * h)
                        first = max(t - 1, 0) if g.kind == "A" else 0
                        bank = psum[4 if pp == 0 else 7]
                        for k in range(first, t + 1):
                            ins = nc.tensor.matmul(
                                bank[:, P * t + HD * h:P * t + HD * h + HD],
                                PTs[:, u % 4, P * (k - first):P * (k - first) + P],
                                proj[l][:, k, bass.ds(vcol, HD)], start=k == first, stop=k == t)
                        ins.then_inc(pv_mm, 1)

                    with pe.Fori(0, 2) as i:
                        jobs(i, 0)
                        for u in range(16):
                            if u == 4:
                                jobs(i, 1)
                            scores(i, u)
                            if u >= 2:
                                turn_probs(i, u - 2)
                            if u >= 3:
                                values(i, u - 3)
                        turn_probs(i, 14)
                        values(i, 13)
                        turn_probs(i, 15)
                        values(i, 14)
                        values(i, 15)

                pe.wait_ge(o_done, 8 * l + 8 + O_FREE)
                ga, gb = GROUPS[2 * l], GROUPS[2 * l + 1]
                for f in range(KC):
                    if f >= 2:
                        pe.wait_ge(ot_lo, 8 * l + f - 1)
                    col = ga.qcol + P * f if f < 4 else gb.qcol + P * (f - 4)
                    for t in range(TT):
                        ins = nc.tensor.transpose(psum[5 + f % 2][:, P * t:P * t + P],
                                                  proj[l][:, t, col:col + P], ident[:, :])
                    ins.then_inc(ot_mm, 1)

                def chunk(bank, b, nk, cols, hi, lo):
                    for k in range(nk):
                        a = cols(k)
                        ins = three(psum[bank][:, :], whi[b][:, a:a + P], wlo[b][:, a:a + P],
                                    hi[:, k, :], lo[:, k, :], k == 0, k == nk - 1)
                    return ins

                pe.wait_ge(ot_lo, 8 * l + 8)
                for i in range(4):
                    n = OUT_BASE[l] + i
                    pe.wait_ge(w_lo, n + 1 + RAW_FREE)
                    for m in (2 * i, 2 * i + 1):
                        pe.wait_ge(x_done, 24 * l + m + 7)
                        ins = chunk(4 + m % 2, n % 2, KC,
                                    lambda k: 256 * k + P * (m % 2), hhi, hlo)
                        ins.then_inc(y_half if m % 2 == 0 else w_used, 1)
                        if m:
                            sum_squares(16 * l + 8 + m - 1, (m - 1) % 2, m == 1, False)
                sum_squares(16 * l + 8 + 7, 1, False, True)
                spread(2 * l + 1)
                pe.wait_ge(h_lo, 16 * l + 16)

                for half in range(2):
                    nh, n0, f0 = HALF[half], GU_BASE[l][half], FT * l + HALF[0] * half

                    def gate_up(n, f, b, j):
                        pe.wait_ge(w_lo, n + (1 + RAW_FREE))
                        pe.wait_ge(g_a, f + 1)
                        for q in range(2):
                            ins = chunk(2 * j + q, b, KC, lambda k: 1024 * q + P * k, hhi, hlo)
                        ins.then_inc(w_used, 1)

                    with pe.Fori(0, nh // 2) as pair_of_slots:
                        i = pair_of_slots * 2
                        for j in range(2):
                            gate_up(i + (n0 + j), i + (f0 + j), (n0 + j) % 2, j)
                            if l == 0 and half == 0:
                                mods_mm(i + (12 + j), j, i * 4 + 4 * j)
                    pe.wait_ge(g_lo, FT * l + HALF[0] * half + nh + GLO_FREE)
                    n0 = DN_BASE[l][half]
                    squares = l == 0 and half == 1

                    def down(n, y, b, j):
                        pe.wait_ge(w_lo, n + (1 + RAW_FREE))
                        pe.wait_ge(x_done, y + 7)
                        chunk(4 + j, b, nh, lambda k: P * k, acthi, actlo).then_inc(w_used, 1)

                    y0 = 24 * l + 8 + 8 * half
                    if squares:
                        down(n0, y0, n0 % 2, 0)
                        down(n0 + 1, y0 + 1, (n0 + 1) % 2, 1)
                        sum_squares(16, 0, True, False)
                    with pe.Fori(1 if squares else 0, 4) as pair_of_slots:
                        i = pair_of_slots * 2
                        for j in range(2):
                            down(i + (n0 + j), i + (y0 + j), (n0 + j) % 2, j)
                            if squares:
                                sum_squares(i + (16 + j - 1), (j + 1) % 2, False, False)
                    if squares:
                        sum_squares(23, 1, False, True)

            for m in range(KC):
                pe.wait_ge(x_done, 48 + m + 1 if m else 8 + 48)
                if m >= 2:
                    pe.wait_ge(yt_ev, m - 1)
                for t in range(TT):
                    ins = nc.tensor.transpose(psum[m % 2][:, P * t:P * t + P],
                                              xT[:, m, P * t:P * t + P], ident[:, :])
                ins.then_inc(yt_mm, 1)


_INS = ['x', 'c', 'ada_w', 'ada_b', 'mix_norm_g', 'ffn_norm_g', 'ab_w_in', 'ab_w_out', 'a_q_norm',
        'a_k_norm', 'a_sink', 'b_q_norm', 'b_k_norm', 'b_rel_bias', 'cd_w_in', 'cd_w_out',
        'c_q_norm', 'c_k_norm', 'c_forget_bias', 'd_q_norm', 'd_k_norm', 'ffn_w_gate_up',
        'ffn_w_down']
_OUTS = [((1, 512, 1024), 'float32')]


def kernel(**inputs):
    import numpy as _np
    import concourse.bacc as _bacc
    from concourse import mybir as _mybir
    from concourse.bass_utils import run_bass_kernel_spmd as _run

    nc = _bacc.Bacc("TRN2", target_bir_lowering=False, num_devices=1)
    arrays, args = {}, []
    for name in _INS:
        a = _np.ascontiguousarray(inputs[name])
        arrays[f"in_{name}_dram"] = a
        args.append(nc.dram_tensor(f"in_{name}_dram", a.shape, _mybir.dt.from_np(a.dtype),
                                   kind="ExternalInput").ap())
    for i, (shape, dtype) in enumerate(_OUTS):
        dt = _mybir.dt.from_np(_np.dtype(dtype))
        args.append(nc.dram_tensor(f"out_{i}_dram", shape, dt, kind="ExternalOutput").ap())
    build_program(nc, *args)
    r = _run(nc, [arrays], core_ids=[0])
    return _np.asarray(r.results[0]["out_0_dram"])
```

```python
from contextlib import ExitStack

import numpy as np
import concourse.bass as bass
from concourse import mybir

F32 = mybir.dt.float32
F32R = mybir.dt.float32r
BF16 = mybir.dt.bfloat16
I32 = mybir.dt.int32
ALU = mybir.AluOpType
ACT = mybir.ActivationFunctionType
AX = mybir.AxisListType

P = 128
D = 1024
S = 512
KC = D // P
TT = S // P
HD = 64
CHUNK = 64
FF = 2816
FT = FF // P
HALF = (12, 10)
AB_IN, CD_IN = 2304, 2508
IN_W = (AB_IN, CD_IN)
IN_SLOTS = (9, 10)
SLOT_BASE = (0, IN_SLOTS[0] + 4 + FT + 16)
REL = 256
RELW = 640
BIG = 1e30
OUT_OF_REACH = -1e38
TAKEN = -3.4e38
TOPK = 128
EPS = 1e-6
QA, KA, VA, QB, KB, VB = 0, 512, 640, 768, 1280, 1792
QC, KCOL, VC, FC, QD, KD, VD, QI, KI, WI = 0, 512, 1024, 1536, 1544, 2056, 2120, 2184, 2440, 2504
NORMED = (((QA, 10, 0), (QB, 16, 10)), ((QC, 16, 0), (QD, 9, 16)))
NSTAT = 26


class Group:

    def __init__(self, kind, qcol, qstat, kcol, kstat, vcol, qgain, kgain):
        self.kind, self.qcol, self.qstat, self.kcol, self.kstat = kind, qcol, qstat, kcol, kstat
        self.vcol, self.qgain, self.kgain = vcol, qgain, kgain
        self.own_keys = kind in "BC"


GROUPS = ((Group("A", QA, 0, KA, 8, VA, 8, 9), Group("B", QB, 10, KB, 18, VB, 10, 11)),
          (Group("C", QC, 0, KCOL, 8, VC, 12, 13), Group("D", QD, 16, KD, 24, VD, 14, 15)))
PAIRS, HEADS, UNITS = 8, 16, 64


class Unit:

    def __init__(self, l, v):
        self.v = v
        self.n = UNITS * l + v
        self.t, self.head, self.pair = v % TT, v // 4, v // 8
        self.h = self.head % 2
        self.group = GROUPS[l][self.pair // 4]
        self.group_head = self.head % 8
        self.first = max(self.t - 1, 0) if self.group.kind == "A" else 0
        self.width = P * (self.t + 1 - self.first)
        if self.group.kind == "A":
            self.keys = (0, self.pair // 2)
        elif self.group.kind == "D":
            self.keys = (1, 0)
        else:
            self.keys = ((self.pair + 1) % 2, self.h)


class Job:

    def __init__(self, what, buf, h, col, stat, gain, pair, step):
        self.what, self.buf, self.h = what, buf, h
        self.col, self.stat, self.gain = col, stat, gain
        self.pair, self.step = pair, step
        self.n = 0


def layer_jobs(l):
    jobs = []
    if l == 0:
        jobs += [Job("k", 0, j, KA + HD * j, 8 + j, 9, 0, -1) for j in range(2)]
    for pair in range(PAIRS):
        g, p = GROUPS[l][pair // 4], pair % 4
        mine = []
        if g.kind == "D" and p == 0:
            mine.append(("k", 1, 0, g.kcol, g.kstat, g.kgain))
        for h in range(2):
            mine.append(("q", pair % 2, h, g.qcol + P * p + HD * h, g.qstat + 2 * p + h, g.qgain))
            if g.own_keys:
                mine.append(("k", (pair + 1) % 2, h, g.kcol + P * p + HD * h,
                             g.kstat + 2 * p + h, g.kgain))
        jobs += [Job(*m, pair, max(8 * pair - 8 + 2 * i, -1)) for i, m in enumerate(mine)]
    return jobs


JOBS = (layer_jobs(0), layer_jobs(1))
for number, each in enumerate(JOBS[0] + JOBS[1]):
    each.n = number
BLOCKS = (tuple(range(9)), (8, 9, 6, 7, 0, 1, 2, 3, 4, 5))
INDEX_COLS = (KI, QI, QI + HD, QI + 2 * HD, QI + 3 * HD)
INDEX_TURNS = {(2, 1): 0, (2, 2): 1, (2, 3): 2, (3, 0): 3, (3, 1): 4}
INDEX_PRODUCTS = {(3, 2): (1, 0), (3, 3): (1, 2), (4, 0): (2, 0), (4, 1): (2, 2), (4, 2): (3, 0),
                  (4, 3): (3, 2)}
TOP_K_SLOTS = {4: (0, 5), 5: (5, 13), 6: (13, 21), 7: (21, 29), 8: (29, 34), 9: (34, 39)}
TOP_K_LATE = 39
STATS = ({(8, 0): (0, 1), (8, 1): (2,), (8, 2): (3,)},
         {(8, 0): (0,), (8, 2): (1,), (9, 0): (2,), (9, 2): (3,)})
FORGET_SLOT, CUM_AT = 4, (5, 3)
SPREAD = {(6, 0): 0, (6, 1): 1, (6, 2): 2, (6, 3): 3, (7, 0): 4, (7, 1): 5, (7, 2): 6, (7, 3): 7}
SCALE_LAG, TURN_LAG, OUT_LAG, VALUES_LAG, O_HI_LAG, O_LO_LAG = 1, 3, 3, 8, 9, 10
LAY_AHEAD = 3

STEPS = UNITS + O_LO_LAG
DIAGS = 4
RING, SCORE_W = 5, 514
ROUNDS = TOPK // 8
W_FREE, RAW_FREE, ADA_FREE, ACC_FREE, PEV_FREE = 2, 2, 8, 2, 4
GA_FREE, GHI_FREE, GLO_FREE = 2, 2, 2


def build_program(nc, x, c, ada_w, ada_b, mix_norm_g, ffn_norm_g, ab_w_in, ab_w_out, a_q_norm,
                  a_k_norm, a_sink, b_q_norm, b_k_norm, b_rel_bias, cd_w_in, cd_w_out,
                  c_q_norm, c_k_norm, c_forget_bias, d_q_norm, d_k_norm, ffn_w_gate_up,
                  ffn_w_down, out):
    ctx = ExitStack()
    with ctx:
        arena = nc.alloc_sbuf_tensor("arena", [P, 52000], F32)
        del arena
        base = [16640]

        def at(name, shape, dt=F32, offset=None):
            size = int(np.prod(shape[1:])) * (2 if dt == BF16 else 4)
            if offset is None:
                offset = base[0]
                base[0] += (size + 63) // 64 * 64
            t = nc.alloc_sbuf_tensor_at(name, shape, dt, offset=offset)
            return t, offset

        def sb(name, shape, dt=F32, offset=None):
            return at(name, shape, dt, offset)[0]

        xT = sb("xT", [P, KC, S])
        raw = [sb(f"raw{i}", [P, 2048]) for i in range(2)]
        whi = [sb(f"whi{i}", [P, 2048], F32R) for i in range(2)]
        wlo = [sb(f"wlo{i}", [P, 2048], F32R) for i in range(2)]
        ada_at = base[0]
        ada = [sb(f"ada{i}", [P, 4, 512]) for i in range(2)]
        toep = sb("toep", [P, 8, S], offset=ada_at)
        kh = [[sb(f"kh{b}{h}", [P, S], F32R, offset=ada_at + 8192 * b + 4096 * h)
               for h in range(2)] for b in range(2)]
        kl = [[sb(f"kl{b}{h}", [P, S], F32R, offset=ada_at + 8192 * b + 4096 * h + 2048)
               for h in range(2)] for b in range(2)]
        hhi, hhi_at = at("hhi", [P, KC, S], F32R)
        hlo, hlo_at = at("hlo", [P, KC, S], F32R)
        ijn = [sb(f"ijn{i}", [P, TT, P], offset=ada_at + 2048 * i) for i in range(2)]
        iq = [sb(f"iq{h}", [P, S], F32R, offset=ada_at + 4096 + 2048 * h) for h in range(4)]
        ikh = sb("ikh", [P, S], F32R, offset=ada_at + 12288)
        ikl = sb("ikl", [P, S], F32R, offset=ada_at + 14336)
        cumT = sb("cumT", [8, S], offset=ada_at)
        qs = [[sb(f"qs{b}{h}", [P, S], F32R, offset=hhi_at + 4096 + 4096 * b + 2048 * h)
               for h in range(2)] for b in range(2)]
        PT = [sb(f"PT{i}", [P, TT, S], offset=hlo_at + 8192 * i) for i in range(2)]
        U = base[0]
        acthi = sb("acthi", [P, HALF[0], S], F32R)
        actlo = sb("actlo", [P, HALF[0], S], F32R)
        proj = [sb("projAB", [P, TT, AB_IN], offset=U), sb("projCD", [P, TT, CD_IN], offset=U)]
        projR = [sb("projABr", [P, TT, AB_IN], F32R, offset=U),
                 sb("projCDr", [P, TT, CD_IN], F32R, offset=U)]
        loA = sb("loA", [P, 4, S], F32R, offset=U + TT * AB_IN * 4)
        xtok = sb("xtok", [P, TT, D], offset=U)
        ada_first = [ada] + [[sb(f"ada_first{p}{i}", [P, 4, 512], offset=at_ + 8192 * i)
                              for i in range(2)]
                             for p, at_ in enumerate((hhi_at, hlo_at, U + TT * D * 4))]
        TRI = sb("TRI", [P, 896], offset=U + TT * CD_IN * 4)
        SEL = sb("SEL", [8, 8, P], offset=U + TT * CD_IN * 4 + 3584)
        BT, BT_at = at("BT", [P, 8, S])
        nck = sb("nck", [P, 8, S], offset=BT_at)
        loD = sb("loD", [P, 4, S], F32R, offset=BT_at)
        relv = sb("relv", [8, RELW], offset=BT_at)
        sqs = [[sb(f"sqs{l}{i}", [P, HD * NSTAT], offset=at_ + 6656 * i) for i in range(2)]
               for l, at_ in enumerate((BT_at + 2560, ada_at + 2048))]
        dsel = sb("dsel", [P, 1280])
        DS_OFF = (0, 128, 384, 768)
        scratch, Ssb_at = at("scratch", [P, 2080])
        Ssb = sb("Ssb", [P, RING, SCORE_W], offset=Ssb_at)
        dg = [sb(f"dg{i}", [P, P], offset=Ssb_at + 10304 + 512 * i) for i in range(DIAGS)]
        sq = [sb(f"sq{i}", [P, S]) for i in range(2)]
        tmp = [sb(f"tmp{i}", [P, S]) for i in range(2)]
        jn = [sb(f"jn{i}", [P, TT, P], offset=Ssb_at + 12416 + 2048 * i) for i in range(2)]
        AD = sb("AD", [P, S])
        AW = sb("AW", [P, 256])
        adi = sb("adi", [P, S], I32, offset=BT_at + 8192)
        ident = sb("ident", [P, P])
        identb = sb("identb", [P, P], BF16)
        maskb = sb("maskb", [P, P], BF16)
        ones = sb("ones", [P, P])
        diag = sb("diag", [P, TT, P], offset=Ssb_at)
        acc = [sb(f"acc{i}", [P, 512], offset=Ssb_at + 2048 + 2048 * i) for i in range(2)]
        rows1 = sb("rows1", [P, P], offset=Ssb_at + 6144)
        rows2 = sb("rows2", [16, P], offset=Ssb_at + 6656)
        rows3 = sb("rows3", [8, P], offset=Ssb_at + 7168)
        cols1 = sb("cols1", [P, P])
        cols2 = sb("cols2", [P, 16])
        qg8 = sb("qg8", [P, 16])
        cond = sb("cond", [P, 8])
        mods = sb("mods", [P, 2, 48])
        coef = sb("coef", [P, 4, 8])
        snk = sb("snk", [P, 8])
        fb = sb("fb", [P, 8])
        slopes = sb("slopes", [P, 8])
        ssq = sb("ssq", [P, TT, NSTAT])
        rt = sb("rt", [P, TT, NSTAT])
        rs = sb("rs", [P, TT, NSTAT])
        nt1 = sb("nt1", [P, TT, NSTAT])
        nms = sb("nms", [P, TT])
        nsr = sb("nsr", [P, TT])
        nrs = sb("nrs", [P, TT])
        nnt = sb("nnt", [P, TT])
        epsc = sb("epsc", [P, 1])
        zt = sb("zt", [P, TT, 8])
        za = sb("za", [P, TT, 8])
        ze = sb("ze", [P, TT, 8])
        wis = sb("wis", [P, TT, 4])
        nm = sb("nm", [P, RING])
        scr4 = sb("scr4", [P, 4])
        rsum = sb("rsum", [P, RING])
        rinv = sb("rinv", [P, RING])
        top8 = sb("top8", [P, 8])
        assert base[0] <= 229000, base[0]

        psum = [ctx.enter_context(nc.psum_tensor(f"bank{i}", [P, 512], F32)) for i in range(8)]
        rel_scratch = nc.dram_tensor("rel_scratch", (8, RELW), F32, kind="Internal").ap()

        def sem(name):
            return ctx.enter_context(nc.semaphore(name))

        small_in = sem("small_in")
        x_in = sem("x_in")
        raw_in = [sem("raw_in0"), sem("raw_in1")]
        c_mm = sem("c_mm")
        c_in = sem("c_in")
        first_in = [sem(f"first_in{p}") for p in range(4)]
        ada_in = [sem("ada_in0"), sem("ada_in1")]
        rel_in = sem("rel_in")
        rel_rev = sem("rel_rev")
        rel_out = sem("rel_out")
        bt_in = sem("bt_in")
        bt_ok = sem("bt_ok")
        y_out = sem("y_out")
        consts = sem("consts")
        tables = sem("tables")
        w_hi = sem("w_hi")
        w_lo = sem("w_lo")
        w_used = sem("w_used")
        ac_step = sem("ac_step")
        acc_used = sem("acc_used")
        mods_done = sem("mods_done")
        rows_t = sem("rows_t")
        cols_d = sem("cols_d")
        cond_ok = sem("cond_ok")
        dchain = sem("dchain")
        xt_mm = sem("xt_mm")
        x_done = sem("x_done")
        q_sq = sem("q_sq")
        ss_mm = sem("ss_mm")
        n_rt = sem("n_rt")
        n_dg = sem("n_dg")
        n_bc = sem("n_bc")
        h_t = sem("h_t")
        h_hi = sem("h_hi")
        h_lo = sem("h_lo")
        p_mm = sem("p_mm")
        p_ev = sem("p_ev")
        st_sq = sem("st_sq")
        st_rd = sem("st_rd")
        st_rt = sem("st_rt")
        st_ok = sem("st_ok")
        j_in = sem("j_in")
        j_mm = sem("j_mm")
        j_hi = sem("j_hi")
        j_lo = sem("j_lo")
        sc_mm = sem("sc_mm")
        sc_dv = sem("sc_dv")
        sink_in = sem("sink_in")
        sc_mx = sem("sc_mx")
        sc_ex = sem("sc_ex")
        sc_rc = sem("sc_rc")
        sc_dg = sem("sc_dg")
        pt_mm = sem("pt_mm")
        pt_ev = sem("pt_ev")
        pv_mm = sem("pv_mm")
        o_hi = sem("o_hi")
        o_lo = sem("o_lo")
        fg_z = sem("fg_z")
        fg_e = sem("fg_e")
        fg_l = sem("fg_l")
        fg_n = sem("fg_n")
        cm_mm = sem("cm_mm")
        cm_ev = sem("cm_ev")
        ij_in = sem("ij_in")
        ij_mm = sem("ij_mm")
        ij_hi = sem("ij_hi")
        ij_lo = sem("ij_lo")
        ix_mm = sem("ix_mm")
        ix_rl = sem("ix_rl")
        ix_ac = sem("ix_ac")
        tk = sem("tk")
        sel_done = sem("sel_done")
        y_half = sem("y_half")
        g_si = sem("g_si")
        g_a = sem("g_a")
        g_hi = sem("g_hi")
        g_lo = sem("g_lo")
        yt_mm = sem("yt_mm")
        yt_ev = sem("yt_ev")

        w_in = (ab_w_in[0], cd_w_in[0])
        w_out = (ab_w_out[0], cd_w_out[0])
        OUT_BASE = [SLOT_BASE[l] + IN_SLOTS[l] for l in range(2)]
        GU_BASE = [[OUT_BASE[l] + 4, OUT_BASE[l] + 4 + HALF[0] + 8] for l in range(2)]
        DN_BASE = [[GU_BASE[l][0] + HALF[0], GU_BASE[l][1] + HALF[1]] for l in range(2)]
        N_SMALL = 6 + 1 + 16 + 2
        IN_BASE = (0, IN_SLOTS[0])
        ALL_EV = [4 * (IN_BASE[l] + IN_SLOTS[l]) + PEV_FREE for l in range(2)]

        IX_EV = 4 * (IN_BASE[1] + 2) + PEV_FREE

        def in_width(l, j):
            return min(256, IN_W[l] - 256 * j)

        def in_slot_width(l, i):
            return KC * in_width(l, BLOCKS[l][i]) if i < IN_SLOTS[l] else 2048

        def out_parts(l, pair):
            g, p = GROUPS[l][pair // 4], pair % 4
            hi = projR[l][:, :, g.qcol + P * p:g.qcol + P * p + P]
            if g.own_keys:
                return hi, projR[l][:, :, g.kcol + P * p:g.kcol + P * p + P]
            lo = (loA if g.kind == "A" else loD)[:, p, :]
            return hi, lo.rearrange("p (t c) -> p t c", t=TT)

        def out_bank(pair):
            return psum[4 if pair % 2 == 0 else 7]

        block = ctx.enter_context(nc.Block())

        @block.sync
        def _(sp):
            def first_panel(p):
                src = ada_w[0].rearrange("(k p) c -> p k c", p=P)
                for half in range(2):
                    sp.dma_start(ada_first[p][half][:, :, :],
                                 src[:, 4 * half:4 * half + 4, 512 * p:512 * p + 512])\
                        .then_inc(first_in[p], 16)

            sp.dma_start(rows3[:, :], c.rearrange("a (r f) -> (a r) f", f=P)).then_inc(c_in, 16)
            for p in range(2):
                first_panel(p)
            sp.dma_start(rows2[0:8, :], c.rearrange("a (r f) -> (a r) f", f=P)).then_inc(small_in, 16)
            for i, g in enumerate((a_q_norm, a_k_norm, b_q_norm, b_k_norm, c_q_norm, c_k_norm,
                                   d_q_norm, d_k_norm)):
                for h in range(2):
                    sp.dma_start(rows2[8 + i:9 + i, HD * h:HD * h + HD], g).then_inc(small_in, 16)
            for l in range(2):
                sp.dma_start(rows1[48 * l:48 * l + 48, :],
                             ada_b[l].rearrange("(r f) -> r f", f=P)).then_inc(small_in, 16)
                sp.dma_start(rows1[96 + 8 * l:104 + 8 * l, :],
                             mix_norm_g[l].rearrange("(r f) -> r f", f=P)).then_inc(small_in, 16)
                sp.dma_start(rows1[112 + 8 * l:120 + 8 * l, :],
                             ffn_norm_g[l].rearrange("(r f) -> r f", f=P)).then_inc(small_in, 16)
            sp.dma_start(snk[:, :], a_sink.partition_broadcast(P)[:, 0, :]).then_inc(small_in, 16)
            sp.dma_start(fb[:, :], c_forget_bias.partition_broadcast(P)[:, 0, :])\
                .then_inc(small_in, 16)
            for p in range(2, 4):
                first_panel(p)
            sp.dma_start(relv[:, 0:384], b_rel_bias[0, :, REL - P + 1:2 * REL + 1])\
                .then_inc(rel_in, 16)

            def load(n, parity, dst_src):
                sp.wait_ge(w_lo, n + 1)
                for dst, src in dst_src:
                    sp.dma_start(dst, src).then_inc(raw_in[parity], 16)

            def in_slot(l, col, width, parity):
                dst = raw[parity][:, 0:KC * width].rearrange("p (k c) -> p k c", k=KC)
                src = w_in[l].rearrange("(k p) c -> p k c", p=P)
                return [(dst[:, 4 * a:4 * a + 4, :], src[:, 4 * a:4 * a + 4, bass.ds(col, width)])
                        for a in range(2)]

            def out_slot(l, i, parity):
                dst = raw[parity][:, :].rearrange("p (k c) -> p k c", k=KC)
                src = w_out[l].rearrange("(k p) c -> p k c", p=P)
                return [(dst[:, 4 * a:4 * a + 4, :],
                         src[:, 4 * a:4 * a + 4, 256 * i:256 * i + 256]) for a in range(2)]

            def gu_slot(l, col, parity):
                dst = raw[parity][:, :].rearrange("p (h k c) -> p h k c", h=2, k=KC)
                src = ffn_w_gate_up[l].rearrange("(k p) c -> p k c", p=P)
                return [(dst[:, h], src[:, :, bass.ds(col + FF * h, P)]) for h in range(2)]

            def down_slot(l, half, col, parity):
                n_k = HALF[half]
                row = P * HALF[0] * half
                dst = raw[parity][:, 0:n_k * P].rearrange("p (k c) -> p k c", k=n_k)
                src = ffn_w_down[l, row:row + P * n_k, :].rearrange("(k p) c -> p k c", p=P)
                m = n_k // 2
                return [(dst[:, a * m:a * m + m, :], src[:, a * m:a * m + m, bass.ds(col, P)])
                        for a in range(2)]

            for l in range(2):
                n0 = SLOT_BASE[l]
                if l == 1:
                    for i, block in enumerate(BLOCKS[1][0:4]):
                        load(n0 + i, (n0 + i) % 2,
                             in_slot(l, 256 * block, in_width(l, block), (n0 + i) % 2))
                first = n0 + 4 * l
                with sp.Fori(0, 4 - l) as pair_of_slots:
                    i = pair_of_slots * 2
                    for j in range(2):
                        b = (first + j) % 2
                        load(i + (first + j), b, in_slot(l, i * 256 + 256 * j, 256, b))
                if l == 0:
                    load(n0 + 8, (n0 + 8) % 2, in_slot(l, 2048, 256, (n0 + 8) % 2))
                for i in range(4):
                    n = OUT_BASE[l] + i
                    load(n, n % 2, out_slot(l, i, n % 2))
                    if l == 0 and i == 0:
                        sp.wait_ge(rel_rev, 1)
                        sp.dma_start(rel_scratch, relv[:, :]).then_inc(rel_out, 16)
                        sp.wait_ge(rel_out, 16)
                        sp.wait_ge(ac_step, 12 * 8 + ADA_FREE)
                        sp.dma_start(toep[:, :, :], bass.AP(tensor=rel_scratch.tensor, offset=0,
                                                            ap=[[1, P], [RELW, 8], [1, S]]))\
                            .then_inc(bt_in, 16)
                for half in range(2):
                    n0 = GU_BASE[l][half]
                    with sp.Fori(0, HALF[half] // 2) as pair_of_slots:
                        i = pair_of_slots * 2
                        for j in range(2):
                            b = (n0 + j) % 2
                            load(i + (n0 + j), b,
                                 gu_slot(l, i * P + P * (HALF[0] * half + j), b))
                    n0 = DN_BASE[l][half]
                    with sp.Fori(0, 4) as pair_of_slots:
                        i = pair_of_slots * 2
                        for j in range(2):
                            b = (n0 + j) % 2
                            load(i + (n0 + j), b, down_slot(l, half, i * P + P * j, b))
            sp.wait_ge(yt_ev, KC)
            sp.dma_start(out[0].rearrange("(t p) f -> p t f", p=P), xtok[:, :, :])\
                .then_inc(y_out, 16)
            sp.wait_ge(y_out, 16)

        @block.gpsimd
        def _(pool):
            n_const = [0]

            def step(ins):
                n_const[0] += 1
                ins.then_inc(consts, 1)
                pool.wait_ge(consts, n_const[0])

            def ada_load(l, a, col, half):
                pool.wait_ge(ac_step, a * 4 + 4)
                src = ada_w[l].rearrange("(k p) c -> p k c", p=P)
                pool.dma_start(ada[half][:, :, :],
                               src[:, 4 * half:4 * half + 4, bass.ds(col, 512)])\
                    .then_inc(ada_in[half], 16)

            step(nc.gpsimd.memset(ident[:, :], 0.0))
            step(nc.gpsimd.affine_select(out=ident[:, :], in_=ident[:, :],
                                         compare_op=ALU.not_equal, fill=1.0, base=0,
                                         pattern=[[-1, P]], channel_multiplier=1))
            step(nc.gpsimd.memset(ones[:, :], 1.0))
            step(nc.gpsimd.memset(epsc[:, :], EPS))
            step(nc.gpsimd.iota(adi[:, :], pattern=[[-1, S]], base=S - P, channel_multiplier=1))
            for h in range(8):
                step(nc.gpsimd.memset(slopes[:, h:h + 1], -2.0 ** (-(h + 1))))
            step(nc.gpsimd.memset(maskb[:, :], 0.0))
            step(nc.gpsimd.affine_select(out=maskb[:, :], in_=maskb[:, :], compare_op=ALU.is_ge,
                                         fill=-BIG, base=0, pattern=[[-1, P]],
                                         channel_multiplier=1))
            step(nc.gpsimd.tensor_copy(identb[:, :], ident[:, :]))
            with pool.Fori(0, 8) as i:
                for half in range(2):
                    ada_load(0, i * 2 + (8 + half), i * 512 + 2048, half)

            def lay_out(l, job):
                if job.n >= 2:
                    pool.wait_ge(j_mm, job.n - 1)
                for half in range(2):
                    dst = jn[job.n % 2][:, :, HD * half:HD * half + HD]
                    src = proj[l][:, :, job.col:job.col + HD]
                    ins = nc.gpsimd.tensor_tensor(
                        dst, src, rs[:, :, job.stat:job.stat + 1].to_broadcast([P, TT, HD]),
                        ALU.mult)
                ins.then_inc(j_in, 1)

            for l in range(2):
                if l == 1:
                    pool.wait_ge(p_ev, IX_EV)
                    for n, col in enumerate(INDEX_COLS):
                        if n >= 2:
                            pool.wait_ge(ij_mm, n - 1)
                        for half in range(2):
                            ins = nc.gpsimd.tensor_copy(
                                ijn[n % 2][:, :, HD * half:HD * half + HD],
                                proj[1][:, :, col:col + HD])
                        ins.then_inc(ij_in, 1)
                pool.wait_ge(st_ok, l + 1)
                for v in range(UNITS + SCALE_LAG):
                    for job in JOBS[l]:
                        if job.step == v + LAY_AHEAD or v == 0 and -1 <= job.step < LAY_AHEAD:
                            lay_out(l, job)
                    if v >= SCALE_LAG:
                        u = Unit(l, v - SCALE_LAG)
                        if u.n >= DIAGS:
                            pool.wait_ge(pt_mm, u.n - DIAGS + 1)
                        pool.wait_ge(sc_rc, u.n + 1)
                        nc.gpsimd.tensor_scalar(dg[u.v % DIAGS][:, :], ident[:, :],
                                                rinv[:, u.v % RING:u.v % RING + 1],
                                                None, ALU.mult).then_inc(sc_dg, 1)
                if l == 0:
                    pool.wait_ge(sc_mm, UNITS)
                    with pool.Fori(0, 12) as i:
                        for half in range(2):
                            ada_load(1, i * 2 + (24 + half), i * 512, half)
                    pool.wait_ge(x_done, 8 + 24)
                    step(nc.gpsimd.memset(TRI[:, 0:384], 0.0))
                    step(nc.gpsimd.memset(TRI[:, 384:896], 1.0))
                    step(nc.gpsimd.affine_select(out=TRI[:, 384:512], in_=TRI[:, 384:512],
                                                 compare_op=ALU.is_ge, fill=0.0, base=0,
                                                 pattern=[[1, P]], channel_multiplier=-1))
                    step(nc.gpsimd.memset(SEL[:, :, :], 0.0))
                    step(nc.gpsimd.affine_select(out=SEL[:, :, :], in_=SEL[:, :, :],
                                                 compare_op=ALU.not_equal, fill=1.0, base=0,
                                                 pattern=[[-1, 8], [0, P]],
                                                 channel_multiplier=1))

        N_CONST0 = 5 + 8 + 3
        N_CONST1 = N_CONST0 + 5

        @block.scalar
        def _(act):
            for t in range(TT):
                act.dma_start(xtok[:, t, :], x[0, P * t:P * t + P, :]).then_inc(x_in, 16)
            act.sem_inc(p_ev, PEV_FREE)
            act.sem_inc(g_hi, GHI_FREE)

            def cut_hi(n, b, landed, width):
                act.wait_ge(raw_in[b], landed)
                act.wait_ge(w_used, n + 1)
                nc.scalar.activation(whi[b][:, 0:width], raw[b][:, 0:width], ACT.Copy)\
                    .then_inc(w_hi, 1)

            def landed(n):
                return 32 * (n // 2 + 1)

            def square(q, b, x_ap, x_count):
                act.wait_ge(x_done, x_count)
                act.wait_ge(ss_mm, q)
                nc.scalar.activation(sq[b][:, :], x_ap, ACT.Square).then_inc(q_sq, 1)

            def norm_h(nn, shift, l):
                act.wait_ge(ss_mm, 8 * nn + 8 + 1)
                nc.scalar.activation(nsr[:, :], psum[6][:, 0:TT], ACT.Sqrt, bias=epsc[:, 0:1],
                                     scale=1.0 / D).then_inc(n_rt, 1)
                for k in range(KC):
                    act.wait_ge(h_t, 8 * nn + k + 1)
                    nc.scalar.activation(hhi[:, k, :], tmp[k % 2][:, :], ACT.Identity,
                                         bias=mods[:, l, shift + k:shift + k + 1])\
                        .then_inc(h_hi, 1)

            def in_out(l, s, t, width, col):
                if t < 3:
                    act.wait_ge(p_mm, s * 3 + (t + 1))
                else:
                    act.wait_ge(w_used, s + (SLOT_BASE[l] - IN_BASE[l] + 1 + W_FREE))
                nc.scalar.activation(proj[l][:, t, bass.ds(col, width)],
                                     psum[t][:, 0:width], ACT.Copy).then_inc(p_ev, 1)

            act.wait_ge(consts, 4)
            act.wait_ge(c_mm, 1)
            nc.scalar.activation(cond[:, :], psum[4][:, 0:8], ACT.Silu).then_inc(cond_ok, 1)
            for m in range(KC):
                square(m, m % 2, xT[:, m, :], m + 1)
            cut_hi(0, 0, landed(0), 2048)

            for l in range(2):
                n0, s0 = SLOT_BASE[l], IN_BASE[l]
                norm_h(2 * l, 0, l)
                nst = NORMED[l][1][2] + NORMED[l][1][1]
                if l == 0:
                    with act.Fori(0, 4) as pair_of_slots:
                        i = pair_of_slots * 2
                        for j in range(2):
                            b = (n0 + j + 1) % 2
                            cut_hi(i + (n0 + j + 1), b, i * 16 + landed(n0 + j + 1),
                                   2048)
                            for t in range(TT):
                                in_out(l, i + (s0 + j), t, 256, i * 256 + 256 * j)
                for i in range(8 if l == 0 else 0, IN_SLOTS[l]):
                    cut_hi(n0 + i + 1, (n0 + i + 1) % 2, landed(n0 + i + 1),
                           in_slot_width(l, i + 1))
                    if l == 1 and i == FORGET_SLOT:
                        act.wait_ge(fg_z, 2)
                        nc.scalar.activation(ze[:, :, :], za[:, :, :], ACT.Exp, scale=-1.0)\
                            .then_inc(fg_e, 1)
                        act.wait_ge(fg_e, 1)
                        nc.scalar.activation(za[:, :, :], ze[:, :, :], ACT.Ln,
                                             bias=ones[:, 0:1]).then_inc(fg_l, 1)
                    for t in range(TT):
                        if i == IN_SLOTS[l] - 1 and t == TT - 1:
                            act.wait_ge(st_rd, 4 * l + TT)
                            nc.scalar.activation(rt[:, :, 0:nst], ssq[:, :, 0:nst], ACT.Sqrt,
                                                 bias=epsc[:, 0:1], scale=1.0 / HD)\
                                .then_inc(st_rt, 1)
                        block = BLOCKS[l][i]
                        in_out(l, s0 + i, t, in_width(l, block), 256 * block)
                        for tile in STATS[l].get((i, t), ()):
                            act.wait_ge(p_ev, 4 * (s0 + 8) + PEV_FREE)
                            if tile >= 2:
                                act.wait_ge(st_rd, 4 * l + tile - 1)
                            for col, heads, stat in NORMED[l]:
                                ins = nc.scalar.activation(
                                    sqs[l][tile % 2][:, HD * stat:HD * (stat + heads)],
                                    proj[l][:, tile, col:col + HD * heads], ACT.Square)
                            ins.then_inc(st_sq, 1)
                        if l == 1 and (i, t) == CUM_AT:
                            act.wait_ge(cm_mm, 1)
                            nc.scalar.activation(cumT[:, :], psum[4][0:8, :], ACT.Copy)\
                                .then_inc(cm_ev, 1)
                        if l == 1 and (i, t) in SPREAD:
                            h = SPREAD[i, t]
                            act.wait_ge(cm_mm, 2 + h)
                            nc.scalar.activation(nck[:, h, :], psum[4 + 3 * (h % 2)][:, :],
                                                 ACT.Copy).then_inc(cm_ev, 1)
                        if l == 1 and (i, t) in INDEX_TURNS:
                            n = INDEX_TURNS[i, t]
                            act.wait_ge(ij_mm, n + 1)
                            dst = ikh if n == 0 else iq[n - 1]
                            nc.scalar.activation(dst[:, :], psum[5 + n % 2][:, :], ACT.Copy)\
                                .then_inc(ij_hi, 1)
                        if l == 1 and (i, t) in INDEX_PRODUCTS:
                            tile, head = INDEX_PRODUCTS[i, t]
                            for h in (head, head + 1):
                                u = 4 * (tile - 1) + h
                                act.wait_ge(ix_mm, u + 1)
                                if u >= 2:
                                    act.wait_ge(ix_ac, u - 1)
                                nc.scalar.activation(sq[h % 2][:, 0:P * (tile + 1)],
                                                     psum[4 + 3 * (h % 2)][:, 0:P * (tile + 1)],
                                                     ACT.Relu).then_inc(ix_rl, 1)

                def part_hi(job):
                    act.wait_ge(j_mm, job.n + 1)
                    if job.pair >= 2:
                        act.wait_ge(sc_mm, UNITS * l + 8 * (job.pair - 1))
                    dst = (qs if job.what == "q" else kh)[job.buf][job.h]
                    gain = (qg8 if job.what == "q" else cols2)[:, job.gain:job.gain + 1]
                    nc.scalar.activation(dst[:, :], psum[5 + job.n % 2][:, :], ACT.Copy,
                                         scale=gain).then_inc(j_hi, 1)

                if l == 0:
                    act.wait_ge(bt_ok, 1)

                def exps(v):
                    u = Unit(l, v)
                    w = u.width + (u.group.kind == "A")
                    act.wait_ge(sc_mx, u.n + 1)
                    nc.scalar.activation(Ssb[:, v % RING, 0:w], Ssb[:, v % RING, 0:w], ACT.Exp,
                                         bias=nm[:, v % RING:v % RING + 1],
                                         accum_out=rsum[:, v % RING:v % RING + 1]).then_inc(sc_ex, 1)

                def probs_out(v):
                    u = Unit(l, v)
                    act.wait_ge(pt_mm, u.n + 1)
                    if u.head >= 2:
                        act.wait_ge(pv_mm, HEADS * l + u.head - 1)
                    nc.scalar.activation(
                        PT[u.h][:, u.first:u.t + 1, P * u.t:P * u.t + P],
                        psum[2 + v % 2][:, 0:u.width].rearrange("p (k c) -> p k c", c=P),
                        ACT.Copy).then_inc(pt_ev, 1)

                def output_hi(pair):
                    act.wait_ge(pv_mm, HEADS * l + 2 * pair + 2)
                    nc.scalar.activation(
                        out_parts(l, pair)[0],
                        out_bank(pair)[:, :].rearrange("p (t c) -> p t c", t=TT),
                        ACT.Copy).then_inc(o_hi, 1)

                for job in JOBS[l]:
                    if job.step == -1:
                        part_hi(job)
                for v in range(STEPS):
                    for job in JOBS[l]:
                        if job.step == v:
                            part_hi(job)
                    if v < UNITS:
                        exps(v)
                    if 0 <= v - OUT_LAG < UNITS:
                        probs_out(v - OUT_LAG)
                    if v >= O_HI_LAG and (v - O_HI_LAG) % 8 == 7:
                        output_hi((v - O_HI_LAG) // 8)

                for i in range(4):
                    n = OUT_BASE[l] + i
                    cut_hi(n + 1, (n + 1) % 2, landed(n + 1), 2048)
                    for m in (2 * i, 2 * i + 1):
                        square(16 * l + 8 + m, m % 2, xT[:, m, :], 24 * l + 8 + m + 1)
                norm_h(2 * l + 1, 24, l)

                for half in range(2):
                    nh, n0, f0 = HALF[half], GU_BASE[l][half], FT * l + HALF[0] * half

                    def hidden(n, f, b, out_ap):
                        act.wait_ge(w_used, n + (1 + W_FREE))
                        act.wait_ge(g_a, f + 1)
                        nc.scalar.activation(sq[b][:, :], psum[2 * b][:, :], ACT.Silu)\
                            .then_inc(g_si, 1)
                        act.wait_ge(g_a, f + (1 + GA_FREE))
                        nc.scalar.activation(out_ap, tmp[b][:, :], ACT.Copy).then_inc(g_hi, 1)

                    with act.Fori(0, nh // 2 - 1) as pair_of_slots:
                        i = pair_of_slots * 2
                        for j in range(2):
                            b = (n0 + j + 1) % 2
                            cut_hi(i + (n0 + j + 1), b, i * 16 + landed(n0 + j + 1), 2048)
                            hidden(i + (n0 + j), i + (f0 + j), j,
                                   acthi[:, bass.ds(i + j, 1), :])
                    for j in (nh - 2, nh - 1):
                        nxt = 2048 if j < nh - 1 else nh * P
                        cut_hi(n0 + j + 1, (n0 + j + 1) % 2, landed(n0 + j + 1), nxt)
                        hidden(n0 + j, f0 + j, j % 2, acthi[:, j:j + 1, :])
                    n0 = DN_BASE[l][half]
                    with act.Fori(0, 3) as pair_of_slots:
                        i = pair_of_slots * 2
                        for j in range(2):
                            b = (n0 + j + 1) % 2
                            cut_hi(i + (n0 + j + 1), b, i * 16 + landed(n0 + j + 1), nh * P)
                            if half == 1 and l == 0:
                                square(i + (16 * l + 16 + j), j, xT[:, bass.ds(i + j, 1), :],
                                       i + (24 * l + 24 + j + 1))
                    for j in (6, 7):
                        last = l == 1 and half == 1 and j == 7
                        if not last:
                            nxt = nh * P if j == 6 else 2048
                            cut_hi(n0 + j + 1, (n0 + j + 1) % 2, landed(n0 + j + 1), nxt)
                        if half == 1 and l == 0:
                            square(16 * l + 16 + j, j % 2, xT[:, j, :], 24 * l + 24 + j + 1)

            for m in range(KC):
                act.wait_ge(yt_mm, m + 1)
                nc.scalar.activation(xtok[:, :, P * m:P * m + P],
                                     psum[m % 2][:, :].rearrange("p (t c) -> p t c", t=TT),
                                     ACT.Copy).then_inc(yt_ev, 1)

        @block.vector
        def _(dve):
            dve.sem_inc(w_lo, RAW_FREE)
            dve.sem_inc(ac_step, ADA_FREE)
            dve.sem_inc(g_a, GA_FREE)
            dve.sem_inc(g_lo, GLO_FREE)
            links = [0]

            def link(ins):
                links[0] += 1
                ins.then_inc(dchain, 1)
                dve.wait_ge(dchain, links[0])

            def cut_lo(n, b, width):
                dve.wait_ge(w_hi, n + 1)
                nc.vector.tensor_tensor(wlo[b][:, 0:width], raw[b][:, 0:width],
                                        whi[b][:, 0:width], ALU.subtract).then_inc(w_lo, 1)

            def ada_panel(panel, landed, b, first=False):
                for half in range(2):
                    if first:
                        dve.wait_ge(first_in[panel], 32)
                    else:
                        dve.wait_ge(ada_in[half], landed)
                    for k in range(4):
                        s = 4 * half + k
                        halves = ada_first[panel] if first else ada
                        src, by = halves[half][:, k, :], cond[:, s:s + 1]
                        dve.wait_ge(ac_step, panel * 8 + (s + ADA_FREE))
                        if s == 0:
                            dve.wait_ge(acc_used, panel + 1)
                            ins = nc.vector.tensor_scalar(acc[b][:, :], src, by, None, ALU.mult)
                        else:
                            ins = nc.vector.scalar_tensor_tensor(
                                out=acc[b][:, :], in0=src, scalar=by, in1=acc[b][:, :],
                                op0=ALU.mult, op1=ALU.add)
                        ins.then_inc(ac_step, 1)

            def take_mods(l, lo, hi, panels):
                dve.wait_ge(acc_used, panels + ACC_FREE)
                link(nc.vector.tensor_tensor(mods[:, l, lo:hi], psum[7][:, lo:hi],
                                             cols1[:, 48 * l + lo:48 * l + hi], ALU.add))

            def take_coef(nn, l, scale, gain):
                link(nc.vector.scalar_tensor_tensor(
                    out=coef[:, nn, :], in0=mods[:, l, scale:scale + 8], scalar=1.0,
                    in1=cols1[:, gain:gain + 8], op0=ALU.add, op1=ALU.mult))

            def inverse(out_ap, root, mean, t1):
                link(nc.vector.reciprocal(out_ap, root))
                link(nc.vector.tensor_tensor(t1, out_ap, out_ap, ALU.mult))
                link(nc.vector.tensor_tensor(t1, t1, mean, ALU.mult))
                link(nc.vector.tensor_scalar(t1, t1, -0.5, 1.5, ALU.mult, ALU.add))
                return nc.vector.tensor_tensor(out_ap, out_ap, t1, ALU.mult)

            def norm_h(nn, l, shift):
                dve.wait_ge(n_rt, nn + 1)
                link(nc.vector.tensor_scalar(nms[:, :], psum[6][:, 0:TT], 1.0 / D, EPS,
                                             ALU.mult, ALU.add))
                link(inverse(nrs[:, :], nsr[:, :], nms[:, :], nnt[:, :]))
                for t in range(TT):
                    ins = nc.vector.tensor_scalar(diag[:, t, :], ident[:, :], nrs[:, t:t + 1],
                                                  None, ALU.mult)
                ins.then_inc(n_dg, 1)
                dve.wait_ge(n_bc, nn + 1)

                def lo(k):
                    dve.wait_ge(h_hi, 8 * nn + k + 1)
                    nc.vector.scalar_tensor_tensor(
                        out=hlo[:, k, :], in0=tmp[k % 2][:, :],
                        scalar=mods[:, l, shift + k:shift + k + 1], in1=hhi[:, k, :],
                        op0=ALU.add, op1=ALU.subtract).then_inc(h_lo, 1)

                for k in range(KC):
                    if k >= 2:
                        dve.wait_ge(h_lo, 8 * nn + k - 1)
                    nc.vector.scalar_tensor_tensor(
                        out=tmp[k % 2][:, :], in0=xT[:, k, :], scalar=coef[:, nn, k:k + 1],
                        in1=psum[5][:, :], op0=ALU.mult, op1=ALU.mult).then_inc(h_t, 1)
                    if k:
                        lo(k - 1)
                lo(KC - 1)

            def index_scores(t, head):
                w = P * (t + 1)
                row = dsel[:, DS_OFF[t]:DS_OFF[t] + w]
                for h in (head, head + 1):
                    v = 4 * (t - 1) + h
                    dve.wait_ge(ix_rl, v + 1)
                    by = wis[:, t, h:h + 1]
                    if h == 0:
                        ins = nc.vector.tensor_scalar(row, sq[h % 2][:, 0:w], by, 0.0,
                                                      ALU.mult, ALU.add)
                    else:
                        dve.wait_ge(ix_ac, v)
                        ins = nc.vector.scalar_tensor_tensor(
                            out=row, in0=sq[h % 2][:, 0:w], scalar=by, in1=row,
                            op0=ALU.mult, op1=ALU.add)
                    ins.then_inc(ix_ac, 1)

            def top_k(r):
                t, q = 1 + r // ROUNDS, r % ROUNDS
                w = P * (t + 1)
                row = dsel[:, DS_OFF[t]:DS_OFF[t] + w]
                if q == 0:
                    link(nc.vector.memset(
                        dsel[0:CHUNK, DS_OFF[t] + w - 64:DS_OFF[t] + w], OUT_OF_REACH))
                nc.vector.max(top8[:, :], row).then_inc(tk, 1)
                dve.wait_ge(tk, 2 * r + 1)
                nc.vector.match_replace(row, top8[:, :], row, TAKEN).then_inc(tk, 1)
                dve.wait_ge(tk, 2 * r + 2)
                if q == ROUNDS - 1:
                    link(nc.vector.tensor_scalar(row, row, 2 * OUT_OF_REACH, BIG,
                                                 ALU.is_gt, ALU.mult))
                    link(nc.vector.tensor_tensor(row, row, AD[:, S - w:S], ALU.add))

            for k in range(KC):
                dve.wait_ge(xt_mm, k + 1)
                nc.vector.tensor_copy(xT[:, k, :], psum[k % 2][:, :]).then_inc(x_done, 1)
            dve.wait_ge(consts, 5)
            nc.vector.scalar_tensor_tensor(out=AD[:, :], in0=adi[:, :], scalar=-1.0,
                                           in1=adi[:, :], op0=ALU.mult, op1=ALU.max)\
                .then_inc(tables, 1)
            dve.wait_ge(tables, 1)
            link(nc.vector.memset(AD[0:CHUNK, 448:512], BIG))
            link(nc.vector.tensor_copy(AW[:, :], AD[:, 256:512]))
            link(nc.vector.memset(AW[0:CHUNK, 0:64], BIG))
            link(nc.vector.memset(AW[CHUNK:P, 0:128], BIG))
            dve.wait_ge(cond_ok, 1)
            for panel in range(4):
                ada_panel(panel, None, panel % 2, first=True)
            for r, (dst, n) in enumerate(((cols1, P), (cols2, 16))):
                dve.wait_ge(rows_t, 2)
                nc.vector.tensor_copy(dst[:, :], psum[5][:, P * r:P * r + n]).then_inc(cols_d, 1)
            dve.wait_ge(cols_d, 2)
            link(nc.vector.tensor_scalar(qg8[:, :], cols2[:, :], HD ** -0.5, None, ALU.mult))
            dve.wait_ge(rel_in, 16)
            nc.vector.tensor_copy(relv[:, 384:RELW], relv[:, 383:384].to_broadcast([8, 256]))\
                .then_inc(rel_rev, 1)
            take_mods(0, 0, 16, 4)
            take_coef(0, 0, 8, 96)
            cut_lo(0, 0, 2048)

            for l in range(2):
                n0, s0 = SLOT_BASE[l], IN_BASE[l]
                nst = NORMED[l][1][2] + NORMED[l][1][1]
                norm_h(2 * l, l, 0)
                if l == 0:
                    with dve.Fori(0, 4) as pair_of_slots:
                        i = pair_of_slots * 2
                        for j in range(2):
                            cut_lo(i + (n0 + j + 1), (n0 + j + 1) % 2, 2048)
                            ada_panel(i + (4 + j), i * 16 + 16 * (1 + j), j)
                for i in range(8 if l == 0 else 0, IN_SLOTS[l]):
                    cut_lo(n0 + i + 1, (n0 + i + 1) % 2, in_slot_width(l, i + 1))
                    if l == 1 and i == FORGET_SLOT:
                        dve.wait_ge(p_ev, 4 * (s0 + 3) + PEV_FREE)
                        link(nc.vector.tensor_tensor(
                            zt[:, :, :], proj[1][:, :, FC:FC + 8],
                            fb[:, :].unsqueeze(1).to_broadcast([P, TT, 8]), ALU.add))
                        nc.vector.scalar_tensor_tensor(
                            out=za[:, :, :], in0=zt[:, :, :], scalar=-1.0, in1=zt[:, :, :],
                            op0=ALU.mult, op1=ALU.max).then_inc(fg_z, 1)
                        nc.vector.tensor_scalar(zt[:, :, :], zt[:, :, :], 0.0, None, ALU.min)\
                            .then_inc(fg_z, 1)
                        dve.wait_ge(fg_z, 2)
                    if l == 1 and i == FORGET_SLOT + 1:
                        dve.wait_ge(fg_l, 1)
                        nc.vector.tensor_tensor(zt[:, :, :], za[:, :, :], zt[:, :, :],
                                                ALU.subtract).then_inc(fg_n, 1)
                    for t in range(TT):
                        for tile in STATS[l].get((i, t), ()):
                            dve.wait_ge(st_sq, 4 * l + tile + 1)
                            nc.vector.tensor_reduce(
                                ssq[:, tile, 0:nst],
                                sqs[l][tile % 2][:, 0:HD * nst].rearrange("p (h d) -> p h d", d=HD),
                                AX.X, ALU.add).then_inc(st_rd, 1)
                    if i == IN_SLOTS[l] - 1:
                        dve.wait_ge(st_rt, l + 1)
                        link(nc.vector.tensor_scalar(ssq[:, :, 0:nst], ssq[:, :, 0:nst], 1.0 / HD,
                                                     EPS, ALU.mult, ALU.add))
                        inverse(rs[:, :, 0:nst], rt[:, :, 0:nst], ssq[:, :, 0:nst],
                                nt1[:, :, 0:nst]).then_inc(st_ok, 1)
                    if l == 0:
                        continue
                    if i == 2:
                        dve.wait_ge(p_ev, IX_EV)
                        link(nc.vector.tensor_scalar(wis[:, :, :], proj[1][:, :, WI:WI + 4],
                                                     (HD * 4) ** -0.5, None, ALU.mult))
                        link(nc.vector.tensor_copy(dsel[:, 0:P], AD[:, S - P:S]))
                    for t in range(TT):
                        if (i, t) in INDEX_TURNS:
                            n = INDEX_TURNS[i, t]
                            dve.wait_ge(ij_hi, n + 1)
                            if n == 0:
                                hi, lo, rows = ikh, ikl, slice(0, P)
                            else:
                                hi, lo, rows = iq[n - 1], iq[n - 1], slice(HD, P)
                            nc.vector.tensor_tensor(lo[rows, :], psum[5 + n % 2][rows, :],
                                                    hi[rows, :], ALU.subtract).then_inc(ij_lo, 1)
                        if (i, t) in INDEX_PRODUCTS:
                            index_scores(*INDEX_PRODUCTS[i, t])
                    for q in range(*TOP_K_SLOTS.get(i, (0, 0))):
                        if q == 0:
                            dve.wait_ge(ix_ac, 12)
                        top_k(q)
                if l == 0:
                    take_mods(0, 16, 48, 12)
                    take_coef(1, 0, 32, 112)
                    nc.vector.memset(scr4[:, 0:1], 0.0).then_inc(mods_done, 1)

                def part_lo(job):
                    dve.wait_ge(j_hi, job.n + 1)
                    rows = slice(HD, P) if job.what == "q" else slice(0, P)
                    hi = (qs if job.what == "q" else kh)[job.buf][job.h][rows, :]
                    lo = (qs if job.what == "q" else kl)[job.buf][job.h][rows, :]
                    src = psum[5 + job.n % 2][rows, :]
                    gain = (qg8 if job.what == "q" else cols2)[rows, job.gain:job.gain + 1]
                    nc.vector.scalar_tensor_tensor(out=lo, in0=src, scalar=gain, in1=hi,
                                                   op0=ALU.mult, op1=ALU.subtract)\
                        .then_inc(j_lo, 1)

                if l == 0:
                    dve.wait_ge(bt_in, 16)
                    link(nc.vector.tensor_copy(BT[:, :, :], toep[:, :, ::-1]))
                    nc.vector.memset(BT[0:CHUNK, :, S - CHUNK:S], -BIG).then_inc(bt_ok, 1)
                    dve.wait_ge(bt_ok, 1)
                else:
                    dve.wait_ge(cm_ev, 9)

                def add_bias(v):
                    u = Unit(l, v)
                    w, kind, head = u.width, u.group.kind, u.group_head
                    dve.wait_ge(sc_mm, u.n + 1)
                    if u.n >= RING:
                        dve.wait_ge(pt_mm, u.n - RING + 1)
                    s_out = Ssb[:, v % RING, 0:w]
                    if kind in "AD":
                        if kind == "A":
                            table = AW[:, 256 - w:256]
                        else:
                            table = dsel[:, DS_OFF[u.t]:DS_OFF[u.t] + w]
                        nc.vector.scalar_tensor_tensor(
                            out=s_out, in0=table, scalar=slopes[:, head:head + 1],
                            in1=psum[v % 2][:, 0:w], op0=ALU.mult, op1=ALU.add).then_inc(sc_dv, 1)
                    else:
                        table = BT[:, head, S - w:S] if kind == "B" else nck[:, head, 0:w]
                        nc.vector.tensor_tensor(s_out, psum[v % 2][:, 0:w], table, ALU.add)\
                            .then_inc(sc_dv, 1)
                    if kind == "A":
                        nc.vector.tensor_copy(Ssb[:, v % RING, w:w + 1], snk[:, head:head + 1])\
                            .then_inc(sink_in, 1)
                        dve.wait_ge(sink_in, u.n + 1)
                        w += 1
                    dve.wait_ge(sc_dv, u.n + 1)
                    nc.vector.tensor_reduce(nm[:, v % RING:v % RING + 1], Ssb[:, v % RING, 0:w],
                                            AX.X, ALU.max, negate=True).then_inc(sc_mx, 1)

                def invert_sum(v):
                    dve.wait_ge(sc_ex, UNITS * l + v + 1)
                    nc.vector.reciprocal(rinv[:, v % RING:v % RING + 1],
                                         rsum[:, v % RING:v % RING + 1]).then_inc(sc_rc, 1)

                def output_lo(pair):
                    dve.wait_ge(o_hi, PAIRS * l + pair + 1)
                    hi, lo = out_parts(l, pair)
                    nc.vector.tensor_tensor(
                        lo, out_bank(pair)[:, :].rearrange("p (t c) -> p t c", t=TT), hi,
                        ALU.subtract).then_inc(o_lo, 1)

                for job in JOBS[l]:
                    if job.step == -1:
                        part_lo(job)
                for v in range(STEPS):
                    if v < UNITS:
                        add_bias(v)
                    if 0 <= v - SCALE_LAG < UNITS:
                        invert_sum(v - SCALE_LAG)
                    for job in JOBS[l]:
                        if job.step == v:
                            part_lo(job)
                    if v >= O_LO_LAG and (v - O_LO_LAG) % 8 == 7:
                        output_lo((v - O_LO_LAG) // 8)
                    if l == 1 and TOP_K_LATE + v < 3 * ROUNDS:
                        top_k(TOP_K_LATE + v)

                def add_chunk(bank, gate, m, x_ap):
                    nc.vector.scalar_tensor_tensor(
                        out=x_ap, in0=psum[bank][:, :], scalar=mods[:, l, bass.ds(gate + m, 1)]
                        if not isinstance(m, int) else mods[:, l, gate + m:gate + m + 1],
                        in1=x_ap, op0=ALU.mult, op1=ALU.add).then_inc(x_done, 1)

                for i in range(4):
                    n = OUT_BASE[l] + i
                    cut_lo(n + 1, (n + 1) % 2, 2048)
                    dve.wait_ge(y_half, 4 * l + i + 1)
                    add_chunk(4, 16, 2 * i, xT[:, 2 * i, :])
                    dve.wait_ge(w_used, n + 1 + W_FREE)
                    add_chunk(5, 16, 2 * i + 1, xT[:, 2 * i + 1, :])
                norm_h(2 * l + 1, l, 24)

                for half in range(2):
                    nh, n0, f0 = HALF[half], GU_BASE[l][half], FT * l + HALF[0] * half

                    def hidden(n, f, b, hi_ap, lo_ap):
                        dve.wait_ge(g_si, f + 1)
                        dve.wait_ge(g_hi, f + 1)
                        dve.wait_ge(g_lo, f + 1)
                        nc.vector.tensor_tensor(tmp[b][:, :], sq[b][:, :], psum[2 * b + 1][:, :],
                                                ALU.mult).then_inc(g_a, 1)
                        dve.wait_ge(g_hi, f + (1 + GHI_FREE))
                        nc.vector.tensor_tensor(lo_ap, tmp[b][:, :], hi_ap, ALU.subtract)\
                            .then_inc(g_lo, 1)

                    with dve.Fori(0, nh // 2 - 1) as pair_of_slots:
                        i = pair_of_slots * 2
                        for j in range(2):
                            cut_lo(i + (n0 + j + 1), (n0 + j + 1) % 2, 2048)
                            if l == 0 and half == 0:
                                ada_panel(i + (12 + j), i * 16 + 16 * (9 + j), j)
                            hidden(i + (n0 + j), i + (f0 + j), j,
                                   acthi[:, bass.ds(i + j, 1), :], actlo[:, bass.ds(i + j, 1), :])
                    for j in (nh - 2, nh - 1):
                        cut_lo(n0 + j + 1, (n0 + j + 1) % 2, 2048 if j < nh - 1 else nh * P)
                        if l == 0 and half == 0:
                            ada_panel(12 + j, 16 * (9 + j), j % 2)
                        hidden(n0 + j, f0 + j, j % 2, acthi[:, j:j + 1, :], actlo[:, j:j + 1, :])
                    if l == 0 and half == 0:
                        take_mods(1, 0, 48, 24)
                        take_coef(2, 1, 8, 104)
                        take_coef(3, 1, 32, 120)
                    n0 = DN_BASE[l][half]
                    with dve.Fori(0, 3) as pair_of_slots:
                        i = pair_of_slots * 2
                        for j in range(2):
                            cut_lo(i + (n0 + j + 1), (n0 + j + 1) % 2, nh * P)
                            dve.wait_ge(w_used, i + (n0 + j + 1 + W_FREE))
                            add_chunk(4 + j, 40, i + j, xT[:, bass.ds(i + j, 1), :])
                    for j in (6, 7):
                        if not (l == 1 and half == 1 and j == 7):
                            cut_lo(n0 + j + 1, (n0 + j + 1) % 2, nh * P if j == 6 else 2048)
                        dve.wait_ge(w_used, n0 + j + 1 + W_FREE)
                        add_chunk(4 + j % 2, 40, j, xT[:, j, :])

        @block.tensor
        def _(pe):
            pe.sem_inc(w_used, W_FREE)
            pe.sem_inc(acc_used, ACC_FREE)
            pe.sem_inc(ss_mm, 1)

            def three(dst, a_hi, a_lo, b_hi, b_lo, first, last):
                nc.tensor.matmul(dst, a_hi, b_hi, start=first, stop=False)
                nc.tensor.matmul(dst, a_hi, b_lo, start=False, stop=False)
                return nc.tensor.matmul(dst, a_lo, b_hi, start=False, stop=last)

            def sum_squares(q, b, first, last):
                pe.wait_ge(q_sq, q + 1)
                for t in range(TT):
                    ins = nc.tensor.matmul(psum[6][:, t:t + 1], sq[b][:, P * t:P * t + P],
                                           ones[:, 0:1], start=first and t == 0, stop=last,
                                           skip_group_check=True)
                ins.then_inc(ss_mm, 1)

            def spread(nn):
                pe.wait_ge(n_dg, nn + 1)
                for t in range(TT):
                    ins = nc.tensor.matmul(psum[5][:, P * t:P * t + P], ones[:, :], diag[:, t, :],
                                           start=True, stop=True)
                ins.then_inc(n_bc, 1)

            def mods_mm(panel, b, col):
                pe.wait_ge(ac_step, panel * 8 + (8 + ADA_FREE))
                for j in range(4):
                    ins = nc.tensor.matmul(psum[7][:, bass.ds(col + j, 1)],
                                           acc[b][:, P * j:P * j + P], ones[:, 0:1],
                                           start=True, stop=True)
                ins.then_inc(acc_used, 1)

            pe.wait_ge(consts, 3)
            pe.wait_ge(c_in, 16)
            nc.tensor.transpose(psum[4][:, 0:8], rows3[:, :], ident[0:8, 0:8]).then_inc(c_mm, 1)
            pe.wait_ge(x_in, 16 * TT)
            for k in range(KC):
                if k >= 2:
                    pe.wait_ge(x_done, k - 1)
                for t in range(TT):
                    ins = nc.tensor.transpose(psum[k % 2][:, P * t:P * t + P],
                                              xtok[:, t, P * k:P * k + P], ident[:, :])
                ins.then_inc(xt_mm, 1)
            for m in range(KC):
                sum_squares(m, m % 2, m == 0, m == KC - 1)
            for panel in range(4):
                mods_mm(panel, panel % 2, 4 * panel)
            pe.wait_ge(small_in, 16 * N_SMALL)
            nc.tensor.transpose(psum[5][:, 0:P], rows1[:, :], ident[:, :]).then_inc(rows_t, 1)
            nc.tensor.transpose(psum[5][:, P:P + 16], rows2[:, :], ident[0:16, 0:16])\
                .then_inc(rows_t, 1)

            for l in range(2):
                n0, s0 = SLOT_BASE[l], IN_BASE[l]
                pe.wait_ge(cols_d, 2)
                spread(2 * l)

                def project_first(n, s, width):
                    b = n0 % 2
                    pe.wait_ge(w_lo, n + (1 + RAW_FREE))
                    pe.wait_ge(p_ev, s * 4 + TT)
                    for k in range(KC):
                        pe.wait_ge(h_lo, 16 * l + k + 1)
                        cols = slice(k * width, k * width + width)
                        for t in range(TT):
                            tok = slice(P * t, P * t + P)
                            ins = three(psum[t][:, 0:width], hhi[:, k, tok],
                                        hlo[:, k, tok], whi[b][:, cols], wlo[b][:, cols],
                                        k == 0, k == KC - 1)
                            if k == KC - 1:
                                ins.then_inc(p_mm if t < 3 else w_used, 1)

                def project(n, s, j, width):
                    b = (n0 + j) % 2
                    pe.wait_ge(w_lo, n + (1 + RAW_FREE))
                    for t in range(TT):
                        pe.wait_ge(p_ev, s * 4 + (t + 1))
                        for k in range(KC):
                            tok = slice(P * t, P * t + P)
                            cols = slice(k * width, k * width + width)
                            ins = three(psum[t][:, 0:width], hhi[:, k, tok],
                                        hlo[:, k, tok], whi[b][:, cols], wlo[b][:, cols],
                                        k == 0, k == KC - 1)
                        ins.then_inc(p_mm if t < 3 else w_used, 1)
                        if l == 1 and (j, t) in INDEX_TURNS:
                            turn_index(INDEX_TURNS[j, t])
                        if l == 1 and (j, t) in INDEX_PRODUCTS:
                            index_products(*INDEX_PRODUCTS[j, t])
                        if l == 1 and (j, t) == CUM_AT:
                            accumulate()
                        if l == 1 and (j, t) in SPREAD:
                            spread_head(SPREAD[j, t])

                def accumulate():
                    pe.wait_ge(consts, N_CONST1)
                    pe.wait_ge(fg_n, 1)
                    pe.wait_ge(ix_rl, 12)
                    for t in range(TT):
                        ins = nc.tensor.matmul(psum[4][0:8, :], zt[:, t, :],
                                               TRI[:, 384 - P * t:896 - P * t],
                                               start=t == 0, stop=t == TT - 1)
                    ins.then_inc(cm_mm, 1)

                def spread_head(h):
                    pe.wait_ge(cm_ev, max(h, 1))
                    nc.tensor.matmul(psum[4 + 3 * (h % 2)][:, :], SEL[:, h, :], cumT[:, :],
                                     start=True, stop=True).then_inc(cm_mm, 1)

                def turn_index(m):
                    pe.wait_ge(ij_in, m + 1)
                    if m >= 2:
                        pe.wait_ge(ij_lo, m - 1)
                    for t in range(TT):
                        ins = nc.tensor.transpose(psum[5 + m % 2][:, P * t:P * t + P],
                                                  ijn[m % 2][:, t, :], ident[:, :])
                    ins.then_inc(ij_mm, 1)

                def index_products(t, head):
                    pe.wait_ge(ij_lo, 5)
                    for h in (head, head + 1):
                        u = 4 * (t - 1) + h
                        if u >= 2:
                            pe.wait_ge(ix_rl, u - 1)
                        dst = psum[4 + 3 * (h % 2)][:, 0:P * (t + 1)]
                        query = iq[h][:, P * t:P * t + P]
                        nc.tensor.matmul(dst, query, ikh[:, 0:P * (t + 1)],
                                         start=True, stop=False)
                        nc.tensor.matmul(dst, query, ikl[:, 0:P * (t + 1)],
                                         start=False, stop=True).then_inc(ix_mm, 1)

                project_first(n0, s0, 256)
                if l == 0:
                    mods_mm(4, 0, 16)
                    with pe.Fori(0, 3) as pair_of_slots:
                        i = pair_of_slots * 2
                        for j in (1, 2):
                            project(i + (n0 + j), i + (s0 + j), j, 256)
                            mods_mm(i + (4 + j), j % 2, i * 4 + (16 + 4 * j))
                    project(n0 + 7, s0 + 7, 7, 256)
                    mods_mm(11, 1, 16 + 4 * 7)
                for i in range(8 if l == 0 else 1, IN_SLOTS[l]):
                    project(n0 + i, s0 + i, i, in_width(l, BLOCKS[l][i]))

                def turn(job):
                    pe.wait_ge(j_in, job.n + 1)
                    if job.n >= 2:
                        pe.wait_ge(j_lo, job.n - 1)
                    for t in range(TT):
                        ins = nc.tensor.transpose(psum[5 + job.n % 2][:, P * t:P * t + P],
                                                  jn[job.n % 2][:, t, :], ident[:, :])
                    ins.then_inc(j_mm, 1)

                pe.wait_ge(p_ev, ALL_EV[l])
                if l == 1:
                    pe.wait_ge(cm_ev, 9)
                if l == 0:
                    pe.wait_ge(mods_done, 1)
                pe.wait_ge(consts, N_CONST0)
                def scores(v):
                    u = Unit(l, v)
                    if v % 4 == 0:
                        heads = [j.n for j in JOBS[l] if j.step >= -1 and j.pair == u.pair
                                 and j.h <= u.h]
                        if u.pair == 0 and l == 0:
                            heads += [1]
                        pe.wait_ge(j_lo, max(heads) + 1)
                    if u.n >= 2:
                        pe.wait_ge(sc_dv, u.n - 1)
                    b, h = u.keys
                    bank, w = psum[v % 2], u.width
                    query = qs[u.pair % 2][u.h][:, P * u.t:P * u.t + P]
                    masked = u.group.kind == "C"
                    if masked:
                        nc.tensor.matmul(bank[:, w - P:w], identb[:, :], maskb[:, :],
                                         start=True, stop=False, skip_group_check=True)
                    for part, keys in enumerate((kh[b][h], kl[b][h])):
                        ins = nc.tensor.matmul(bank[:, 0:w], query,
                                               keys[:, P * u.first:P * u.first + w],
                                               start=not masked and part == 0, stop=part == 1,
                                               skip_group_check=masked)
                    ins.then_inc(sc_mm, 1)

                def turn_probs(v):
                    u = Unit(l, v)
                    pe.wait_ge(sc_dg, u.n + 1)
                    if u.n >= 2:
                        pe.wait_ge(pt_ev, u.n - 1)
                    for k in range(u.t + 1 - u.first):
                        ins = nc.tensor.matmul(psum[2 + v % 2][:, P * k:P * k + P],
                                               Ssb[:, v % RING, P * k:P * k + P],
                                               dg[v % DIAGS][:, :], start=True, stop=True)
                    ins.then_inc(pt_mm, 1)

                def values(head, k):
                    u = Unit(l, 4 * head)
                    g, p = u.group, u.pair % 4
                    pe.wait_ge(pt_ev, u.n + 4)
                    n = PAIRS * l + u.pair
                    if u.h == 0 and k == 0 and n >= 2:
                        pe.wait_ge(o_lo, n - 1)
                    if g.kind == "A":
                        vcol = g.vcol + HD * (p // 2)
                    else:
                        vcol = g.vcol + (P * p + HD * u.h if g.own_keys else 0)
                    cols = slice(P * k, min(P * k + 2 * P, S) if g.kind == "A" else S)
                    ins = nc.tensor.matmul(
                        out_bank(u.pair)[HD * u.h:HD * u.h + HD, cols],
                        proj[l][:, k, vcol:vcol + HD], PT[u.h][:, k, cols],
                        start=k == 0, stop=k == TT - 1, skip_group_check=True)
                    if k == TT - 1:
                        ins.then_inc(pv_mm, 1)

                for job in JOBS[l]:
                    if job.step == -1:
                        turn(job)
                for v in range(STEPS):
                    for job in JOBS[l]:
                        if job.step == v:
                            turn(job)
                    if v < UNITS:
                        scores(v)
                    if 0 <= v - VALUES_LAG < UNITS:
                        values((v - VALUES_LAG) // 4, v % TT)
                    if 0 <= v - TURN_LAG < UNITS:
                        turn_probs(v - TURN_LAG)
                def chunk(bank, b, nk, cols, parts, late=None):
                    for k in range(nk):
                        if late is not None and k == nk - 1:
                            pe.wait_ge(*late)
                        a = cols(k)
                        hi, lo = parts(k)
                        ins = three(psum[bank][:, :], whi[b][:, a:a + P], wlo[b][:, a:a + P],
                                    hi, lo, k == 0, k == nk - 1)
                    return ins

                pe.wait_ge(o_lo, PAIRS * (l + 1) - 1)
                for i in range(4):
                    n = OUT_BASE[l] + i
                    pe.wait_ge(w_lo, n + 1 + RAW_FREE)
                    for m in (2 * i, 2 * i + 1):
                        pe.wait_ge(x_done, 24 * l + m + 7)
                        ins = chunk(4 + m % 2, n % 2, KC,
                                    lambda k: 256 * k + P * (m % 2),
                                    lambda k: out_parts(l, k),
                                    (o_lo, PAIRS * (l + 1)) if m == 0 else None)
                        ins.then_inc(y_half if m % 2 == 0 else w_used, 1)
                        if m:
                            sum_squares(16 * l + 8 + m - 1, (m - 1) % 2, m == 1, False)
                sum_squares(16 * l + 8 + 7, 1, False, True)
                spread(2 * l + 1)

                for half in range(2):
                    nh, n0, f0 = HALF[half], GU_BASE[l][half], FT * l + HALF[0] * half

                    def gate_up(n, f, b, j):
                        pe.wait_ge(w_lo, n + (1 + RAW_FREE))
                        pe.wait_ge(g_a, f + 1)
                        for q in range(2):
                            ins = chunk(2 * j + q, b, KC, lambda k: 1024 * q + P * k,
                                        lambda k: (hhi[:, k, :], hlo[:, k, :]))
                        ins.then_inc(w_used, 1)

                    def gate_up_first(n, f):
                        b = n % 2
                        pe.wait_ge(w_lo, n + (1 + RAW_FREE))
                        pe.wait_ge(g_a, f + 1)
                        for k in range(KC):
                            pe.wait_ge(h_lo, 16 * l + 8 + k + 1)
                            for q in range(2):
                                a = 1024 * q + P * k
                                ins = three(psum[q][:, :], whi[b][:, a:a + P], wlo[b][:, a:a + P],
                                            hhi[:, k, :], hlo[:, k, :], k == 0, k == KC - 1)
                        ins.then_inc(w_used, 1)

                    if half == 0:
                        gate_up_first(n0, f0)
                        if l == 0:
                            mods_mm(12, 0, 0)
                        with pe.Fori(0, nh // 2 - 1) as pair_of_slots:
                            i = pair_of_slots * 2
                            for j in (1, 2):
                                gate_up(i + (n0 + j), i + (f0 + j), (n0 + j) % 2, j % 2)
                                if l == 0:
                                    mods_mm(i + (12 + j), j % 2, i * 4 + 4 * j)
                        gate_up(n0 + nh - 1, f0 + nh - 1, (n0 + nh - 1) % 2, (nh - 1) % 2)
                        if l == 0:
                            mods_mm(12 + nh - 1, (nh - 1) % 2, 4 * (nh - 1))
                    else:
                        with pe.Fori(0, nh // 2) as pair_of_slots:
                            i = pair_of_slots * 2
                            for j in range(2):
                                gate_up(i + (n0 + j), i + (f0 + j), (n0 + j) % 2, j)
                    tiles_done = FT * l + HALF[0] * half + nh + GLO_FREE
                    pe.wait_ge(g_lo, tiles_done - 1)
                    n0 = DN_BASE[l][half]
                    squares = l == 0 and half == 1

                    def down(n, y, b, j):
                        pe.wait_ge(w_lo, n + (1 + RAW_FREE))
                        pe.wait_ge(x_done, y + 7)
                        chunk(4 + j, b, nh, lambda k: P * k,
                              lambda k: (acthi[:, k, :], actlo[:, k, :]),
                              (g_lo, tiles_done)).then_inc(w_used, 1)

                    y0 = 24 * l + 8 + 8 * half
                    if squares:
                        down(n0, y0, n0 % 2, 0)
                        down(n0 + 1, y0 + 1, (n0 + 1) % 2, 1)
                        sum_squares(16, 0, True, False)
                    with pe.Fori(1 if squares else 0, 4) as pair_of_slots:
                        i = pair_of_slots * 2
                        for j in range(2):
                            down(i + (n0 + j), i + (y0 + j), (n0 + j) % 2, j)
                            if squares:
                                sum_squares(i + (16 + j - 1), (j + 1) % 2, False, False)
                    if squares:
                        sum_squares(23, 1, False, True)

            for m in range(KC):
                pe.wait_ge(x_done, 48 + m + 1 if m else 8 + 48)
                if m >= 2:
                    pe.wait_ge(yt_ev, m - 1)
                for t in range(TT):
                    ins = nc.tensor.transpose(psum[m % 2][:, P * t:P * t + P],
                                              xT[:, m, P * t:P * t + P], ident[:, :])
                ins.then_inc(yt_mm, 1)


_INS = ['x', 'c', 'ada_w', 'ada_b', 'mix_norm_g', 'ffn_norm_g', 'ab_w_in', 'ab_w_out', 'a_q_norm',
        'a_k_norm', 'a_sink', 'b_q_norm', 'b_k_norm', 'b_rel_bias', 'cd_w_in', 'cd_w_out',
        'c_q_norm', 'c_k_norm', 'c_forget_bias', 'd_q_norm', 'd_k_norm', 'ffn_w_gate_up',
        'ffn_w_down']
_OUTS = [((1, 512, 1024), 'float32')]


def kernel(**inputs):
    import numpy as _np
    import concourse.bacc as _bacc
    from concourse import mybir as _mybir
    from concourse.bass_utils import run_bass_kernel_spmd as _run

    nc = _bacc.Bacc("TRN2", target_bir_lowering=False, num_devices=1)
    arrays, args = {}, []
    for name in _INS:
        a = _np.ascontiguousarray(inputs[name])
        arrays[f"in_{name}_dram"] = a
        args.append(nc.dram_tensor(f"in_{name}_dram", a.shape, _mybir.dt.from_np(a.dtype),
                                   kind="ExternalInput").ap())
    for i, (shape, dtype) in enumerate(_OUTS):
        dt = _mybir.dt.from_np(_np.dtype(dtype))
        args.append(nc.dram_tensor(f"out_{i}_dram", shape, dt, kind="ExternalOutput").ap())
    build_program(nc, *args)
    r = _run(nc, [arrays], core_ids=[0])
    return _np.asarray(r.results[0]["out_0_dram"])
```

```python
from contextlib import ExitStack

import numpy as np
import concourse.bass as bass
from concourse import mybir

F32 = mybir.dt.float32
F32R = mybir.dt.float32r
BF16 = mybir.dt.bfloat16
I32 = mybir.dt.int32
ALU = mybir.AluOpType
ACT = mybir.ActivationFunctionType
AX = mybir.AxisListType

P = 128
D = 1024
S = 512
KC = D // P
TT = S // P
HD = 64
CHUNK = 64
FF = 2816
FT = FF // P
HALF = (12, 10)
AB_IN, CD_IN = 2304, 2508
IN_W = (AB_IN, CD_IN)
IN_SLOTS = (9, 10)
SLOT_BASE = (0, IN_SLOTS[0] + 4 + FT + 16)
REL = 256
RELW = 640
BIG = 1e30
OUT_OF_REACH = -1e38
TAKEN = -3.4e38
TOPK = 128
EPS = 1e-6
QA, KA, VA, QB, KB, VB = 0, 512, 640, 768, 1280, 1792
QC, KCOL, VC, FC, QD, KD, VD, QI, KI, WI = 0, 512, 1024, 1536, 1544, 2056, 2120, 2184, 2440, 2504
NORMED = (((QA, 10, 0), (QB, 16, 10)), ((QC, 16, 0), (QD, 9, 16)))
NSTAT = 26


class Group:

    def __init__(self, kind, qcol, qstat, kcol, kstat, vcol, qgain, kgain):
        self.kind, self.qcol, self.qstat, self.kcol, self.kstat = kind, qcol, qstat, kcol, kstat
        self.vcol, self.qgain, self.kgain = vcol, qgain, kgain
        self.own_keys = kind in "BC"


GROUPS = ((Group("A", QA, 0, KA, 8, VA, 8, 9), Group("B", QB, 10, KB, 18, VB, 10, 11)),
          (Group("C", QC, 0, KCOL, 8, VC, 12, 13), Group("D", QD, 16, KD, 24, VD, 14, 15)))
PAIRS, HEADS, UNITS = 8, 16, 64


class Unit:

    def __init__(self, l, v):
        self.v = v
        self.n = UNITS * l + v
        self.t, self.head, self.pair = v % TT, v // 4, v // 8
        self.h = self.head % 2
        self.group = GROUPS[l][self.pair // 4]
        self.group_head = self.head % 8
        self.first = max(self.t - 1, 0) if self.group.kind == "A" else 0
        self.width = P * (self.t + 1 - self.first)
        if self.group.kind == "A":
            self.keys = (0, self.pair // 2)
        elif self.group.kind == "D":
            self.keys = (1, 0)
        else:
            self.keys = ((self.pair + 1) % 2, self.h)


JOB_LEAD = {2: (6, 5), 3: (6, 5, 3), 4: (6, 5, 3, 2)}


class Job:

    def __init__(self, what, buf, h, col, stat, gain, pair, step):
        self.what, self.buf, self.h = what, buf, h
        self.col, self.stat, self.gain = col, stat, gain
        self.pair, self.step = pair, step
        self.n = 0


def layer_jobs(l):
    jobs = []
    if l == 0:
        jobs += [Job("k", 0, j, KA + HD * j, 8 + j, 9, 0, -1) for j in range(2)]
    for pair in range(PAIRS):
        g, p = GROUPS[l][pair // 4], pair % 4
        mine = []
        if g.kind == "D" and p == 0:
            mine.append(("k", 1, 0, g.kcol, g.kstat, g.kgain))
        for h in range(2):
            mine.append(("q", pair % 2, h, g.qcol + P * p + HD * h, g.qstat + 2 * p + h, g.qgain))
            if g.own_keys:
                mine.append(("k", (pair + 1) % 2, h, g.kcol + P * p + HD * h,
                             g.kstat + 2 * p + h, g.kgain))
        jobs += [Job(*m, pair, max(8 * pair - JOB_LEAD[len(mine)][i], -1)) for i, m in enumerate(mine)]
    return jobs


JOBS = (layer_jobs(0), layer_jobs(1))
for number, each in enumerate(JOBS[0] + JOBS[1]):
    each.n = number
BLOCKS = (tuple(range(9)), (8, 9, 6, 7, 0, 1, 2, 3, 4, 5))
INDEX_COLS = (KI, QI, QI + HD, QI + 2 * HD, QI + 3 * HD)
INDEX_TURNS = {(2, 1): 0, (2, 2): 1, (2, 3): 2, (3, 0): 3, (3, 1): 4}
INDEX_PRODUCTS = {(3, 2): (1, 0), (3, 3): (1, 2), (4, 0): (2, 0), (4, 1): (2, 2), (4, 2): (3, 0),
                  (4, 3): (3, 2)}
TOP_K_SLOTS = {4: (0, 6), 5: (6, 14), 6: (14, 22), 7: (22, 29), 8: (29, 31)}
TOP_K_LATE = 31
STATS = ({(8, 0): (0, 1), (8, 1): (2,), (8, 2): (3,)},
         {(8, 0): (0,), (8, 2): (1,), (9, 0): (2,), (9, 2): (3,)})
FORGET_SLOT, CUM_AT, MID_AT, REST_SLOT, LOW_SLOT = 4, (5, 3), (6, 3), 6, 7
SCALE_LAG, TURN_LAG, OUT_LAG, VALUES_LAG, O_HI_LAG, O_LO_LAG = 1, 3, 3, 8, 9, 10
LAY_AHEAD = 3

STEPS = UNITS + O_LO_LAG
DIAGS = 4
RING, SCORE_W = 5, 514
ROUNDS = TOPK // 8
W_FREE, RAW_FREE, ADA_FREE, ACC_FREE, PEV_FREE = 2, 2, 8, 2, 4
GA_FREE, GHI_FREE, GLO_FREE = 2, 2, 2


def build_program(nc, x, c, ada_w, ada_b, mix_norm_g, ffn_norm_g, ab_w_in, ab_w_out, a_q_norm,
                  a_k_norm, a_sink, b_q_norm, b_k_norm, b_rel_bias, cd_w_in, cd_w_out,
                  c_q_norm, c_k_norm, c_forget_bias, d_q_norm, d_k_norm, ffn_w_gate_up,
                  ffn_w_down, out):
    ctx = ExitStack()
    with ctx:
        arena = nc.alloc_sbuf_tensor("arena", [P, 52000], F32)
        del arena
        base = [16640]

        def at(name, shape, dt=F32, offset=None):
            size = int(np.prod(shape[1:])) * (2 if dt == BF16 else 4)
            if offset is None:
                offset = base[0]
                base[0] += (size + 63) // 64 * 64
            t = nc.alloc_sbuf_tensor_at(name, shape, dt, offset=offset)
            return t, offset

        def sb(name, shape, dt=F32, offset=None):
            return at(name, shape, dt, offset)[0]

        xT = sb("xT", [P, KC, S])
        raw = [sb(f"raw{i}", [P, 2048]) for i in range(2)]
        whi = [sb(f"whi{i}", [P, 2048], F32R) for i in range(2)]
        wlo = [sb(f"wlo{i}", [P, 2048], F32R) for i in range(2)]
        ada_at = base[0]
        ada = [sb(f"ada{i}", [P, 4, 512]) for i in range(2)]
        toep = sb("toep", [P, 8, S], offset=ada_at)
        kh = [[sb(f"kh{b}{h}", [P, S], F32R, offset=ada_at + 8192 * b + 4096 * h)
               for h in range(2)] for b in range(2)]
        kl = [[sb(f"kl{b}{h}", [P, S], F32R, offset=ada_at + 8192 * b + 4096 * h + 2048)
               for h in range(2)] for b in range(2)]
        hhi, hhi_at = at("hhi", [P, KC, S], F32R)
        hlo, hlo_at = at("hlo", [P, KC, S], F32R)
        ijn = [sb(f"ijn{i}", [P, TT, P], offset=ada_at + 2048 * i) for i in range(2)]
        iq = [sb(f"iq{h}", [P, S], F32R, offset=ada_at + 4096 + 2048 * h) for h in range(4)]
        ikh = sb("ikh", [P, S], F32R, offset=ada_at + 12288)
        ikl = sb("ikl", [P, S], F32R, offset=ada_at + 14336)
        ytok = sb("ytok", [P, TT, D], offset=ada_at)
        mid0 = sb("mid0", [8, S], BF16, offset=ada_at)
        qs = [[sb(f"qs{b}{h}", [P, S], F32R, offset=hhi_at + 4096 + 4096 * b + 2048 * h)
               for h in range(2)] for b in range(2)]
        PT = [sb(f"PT{i}", [P, TT, S], offset=hlo_at + 8192 * i) for i in range(2)]
        U = base[0]
        acthi = sb("acthi", [P, HALF[0], S], F32R)
        actlo = sb("actlo", [P, HALF[0], S], F32R)
        proj = [sb("projAB", [P, TT, AB_IN], offset=U), sb("projCD", [P, TT, CD_IN], offset=U)]
        projR = [sb("projABr", [P, TT, AB_IN], F32R, offset=U),
                 sb("projCDr", [P, TT, CD_IN], F32R, offset=U)]
        loA = sb("loA", [P, 4, S], F32R, offset=U + TT * AB_IN * 4)
        xtok = sb("xtok", [P, TT, D], offset=U)
        ada_first = [ada] + [[sb(f"ada_first{p}{i}", [P, 4, 512], offset=at_ + 8192 * i)
                              for i in range(2)]
                             for p, at_ in enumerate((hhi_at, hlo_at, U + TT * D * 4))]
        TRI = sb("TRI", [P, 896], offset=U + TT * CD_IN * 4)
        SEL = sb("SEL", [96, 8, P], BF16, offset=U + TT * CD_IN * 4 + 3584)
        cum3 = sb("cum3", [96, S], BF16, offset=U + TT * CD_IN * 4 + 5632)
        rest = sb("rest", [8, S], offset=U + TT * CD_IN * 4 + 6656)
        BT, BT_at = at("BT", [P, 8, S])
        loD = sb("loD", [P, 4, S], F32R, offset=BT_at)
        relv = sb("relv", [8, RELW], offset=BT_at)
        sqs = [[sb(f"sqs{l}{i}", [P, HD * NSTAT], offset=at_ + 6656 * i) for i in range(2)]
               for l, at_ in enumerate((BT_at + 2560, ada_at + 2048))]
        dsel = sb("dsel", [P, 1280])
        DS_OFF = (0, 128, 384, 768)
        scratch, Ssb_at = at("scratch", [P, 2080])
        Ssb = sb("Ssb", [P, RING, SCORE_W], offset=Ssb_at)
        dg = [sb(f"dg{i}", [P, P], offset=Ssb_at + 10304 + 512 * i) for i in range(DIAGS)]
        sq = [sb(f"sq{i}", [P, S]) for i in range(2)]
        tmp = [sb(f"tmp{i}", [P, S]) for i in range(2)]
        jn = [sb(f"jn{i}", [P, TT, P], offset=Ssb_at + 12416 + 2048 * i) for i in range(2)]
        AD = sb("AD", [P, S])
        AW = sb("AW", [P, 256])
        adi = sb("adi", [P, S], I32, offset=BT_at + 8192)
        ident = sb("ident", [P, P])
        identb = sb("identb", [P, P], BF16)
        maskb = sb("maskb", [P, P], BF16)
        ones = sb("ones", [P, P])
        diag = sb("diag", [P, TT, P], offset=Ssb_at)
        acc = [sb(f"acc{i}", [P, 512], offset=Ssb_at + 2048 + 2048 * i) for i in range(2)]
        rows1 = sb("rows1", [P, P], offset=Ssb_at + 6144)
        rows2 = sb("rows2", [16, P], offset=Ssb_at + 6656)
        rows3 = sb("rows3", [8, P], offset=Ssb_at + 7168)
        cols1 = sb("cols1", [P, P])
        cols2 = sb("cols2", [P, 16])
        qg8 = sb("qg8", [P, 16])
        cond = sb("cond", [P, 8])
        mods = sb("mods", [P, 2, 48])
        coef = sb("coef", [P, 4, 8])
        snk = sb("snk", [P, 8])
        fb = sb("fb", [P, 8])
        slopes = sb("slopes", [P, 8])
        ssq = sb("ssq", [P, TT, NSTAT])
        rt = sb("rt", [P, TT, NSTAT])
        rs = sb("rs", [P, TT, NSTAT])
        nt1 = sb("nt1", [P, TT, NSTAT])
        nms = sb("nms", [P, TT])
        nsr = sb("nsr", [P, TT])
        nrs = sb("nrs", [P, TT])
        nnt = sb("nnt", [P, TT])
        epsc = sb("epsc", [P, 1])
        zt = sb("zt", [P, TT, 8])
        za = sb("za", [P, TT, 8])
        ze = sb("ze", [P, TT, 8])
        wis = sb("wis", [P, TT, 4])
        nm = sb("nm", [P, RING])
        scr4 = sb("scr4", [P, 4])
        rsum = sb("rsum", [P, RING])
        rinv = sb("rinv", [P, RING])
        top8 = sb("top8", [P, 8])
        assert base[0] <= 229000, base[0]

        psum = [ctx.enter_context(nc.psum_tensor(f"bank{i}", [P, 512], F32)) for i in range(8)]
        rel_scratch = nc.dram_tensor("rel_scratch", (8, RELW), F32, kind="Internal").ap()

        def sem(name):
            return ctx.enter_context(nc.semaphore(name))

        small_in = sem("small_in")
        x_in = sem("x_in")
        raw_in = [sem("raw_in0"), sem("raw_in1")]
        c_mm = sem("c_mm")
        c_in = sem("c_in")
        first_in = [sem(f"first_in{p}") for p in range(4)]
        ada_in = [sem("ada_in0"), sem("ada_in1")]
        rel_in = sem("rel_in")
        rel_rev = sem("rel_rev")
        rel_out = sem("rel_out")
        bt_in = sem("bt_in")
        bt_ok = sem("bt_ok")
        y_out = sem("y_out")
        consts = sem("consts")
        w_hi = sem("w_hi")
        w_lo = sem("w_lo")
        w_used = sem("w_used")
        ac_step = sem("ac_step")
        acc_used = sem("acc_used")
        mods_done = sem("mods_done")
        rows_t = sem("rows_t")
        cols_d = sem("cols_d")
        cond_ok = sem("cond_ok")
        dchain = sem("dchain")
        xt_mm = sem("xt_mm")
        x_done = sem("x_done")
        q_sq = sem("q_sq")
        sq_add = sem("sq_add")
        ss_mm = sem("ss_mm")
        n_rt = sem("n_rt")
        n_dg = sem("n_dg")
        n_bc = sem("n_bc")
        h_t = sem("h_t")
        h_hi = sem("h_hi")
        h_lo = sem("h_lo")
        p_mm = sem("p_mm")
        p_ev = sem("p_ev")
        st_sq = sem("st_sq")
        st_rd = sem("st_rd")
        st_rt = sem("st_rt")
        st_ok = sem("st_ok")
        j_in = sem("j_in")
        j_mm = sem("j_mm")
        j_hi = sem("j_hi")
        j_lo = sem("j_lo")
        sc_mm = sem("sc_mm")
        sc_dv = sem("sc_dv")
        sink_in = sem("sink_in")
        sc_mx = sem("sc_mx")
        sc_ex = sem("sc_ex")
        sc_rc = sem("sc_rc")
        sc_dg = sem("sc_dg")
        pt_mm = sem("pt_mm")
        pt_ev = sem("pt_ev")
        pv_mm = sem("pv_mm")
        o_hi = sem("o_hi")
        o_lo = sem("o_lo")
        fg_z = sem("fg_z")
        fg_e = sem("fg_e")
        fg_l = sem("fg_l")
        fg_n = sem("fg_n")
        cm_mm = sem("cm_mm")
        cm_hi = sem("cm_hi")
        cm_lo = sem("cm_lo")
        ij_in = sem("ij_in")
        ij_mm = sem("ij_mm")
        ij_hi = sem("ij_hi")
        ij_lo = sem("ij_lo")
        ix_mm = sem("ix_mm")
        ix_rl = sem("ix_rl")
        ix_ac = sem("ix_ac")
        tk = sem("tk")
        sel_done = sem("sel_done")
        y_half = sem("y_half")
        g_si = sem("g_si")
        g_a = sem("g_a")
        g_hi = sem("g_hi")
        g_lo = sem("g_lo")
        yt_mm = sem("yt_mm")
        yt_ev = sem("yt_ev")

        w_in = (ab_w_in[0], cd_w_in[0])
        w_out = (ab_w_out[0], cd_w_out[0])
        OUT_BASE = [SLOT_BASE[l] + IN_SLOTS[l] for l in range(2)]
        GU_BASE = [[OUT_BASE[l] + 4, OUT_BASE[l] + 4 + HALF[0] + 8] for l in range(2)]
        DN_BASE = [[GU_BASE[l][0] + HALF[0], GU_BASE[l][1] + HALF[1]] for l in range(2)]
        N_SMALL = 6 + 1 + 16 + 2
        IN_BASE = (0, IN_SLOTS[0])
        ALL_EV = [4 * (IN_BASE[l] + IN_SLOTS[l]) + PEV_FREE for l in range(2)]

        IX_EV = 4 * (IN_BASE[1] + 2) + PEV_FREE

        def in_width(l, j):
            return min(256, IN_W[l] - 256 * j)

        def in_slot_width(l, i):
            return KC * in_width(l, BLOCKS[l][i]) if i < IN_SLOTS[l] else 2048

        def out_parts(l, pair):
            g, p = GROUPS[l][pair // 4], pair % 4
            hi = projR[l][:, :, g.qcol + P * p:g.qcol + P * p + P]
            if g.own_keys:
                return hi, projR[l][:, :, g.kcol + P * p:g.kcol + P * p + P]
            lo = (loA if g.kind == "A" else loD)[:, p, :]
            return hi, lo.rearrange("p (t c) -> p t c", t=TT)

        def out_bank(pair):
            return psum[4 if pair % 2 == 0 else 7]

        X_BASE = (0, 8, 24, 32)

        def copied_out(n):
            return n + 1 if n < UNITS else n + 1 - UNITS // 2

        block = ctx.enter_context(nc.Block())

        @block.sync
        def _(sp):
            def first_panel(p):
                src = ada_w[0].rearrange("(k p) c -> p k c", p=P)
                for half in range(2):
                    sp.dma_start(ada_first[p][half][:, :, :],
                                 src[:, 4 * half:4 * half + 4, 512 * p:512 * p + 512])\
                        .then_inc(first_in[p], 16)

            sp.dma_start(rows3[:, :], c.rearrange("a (r f) -> (a r) f", f=P)).then_inc(c_in, 16)
            for p in range(2):
                first_panel(p)
            sp.dma_start(rows2[0:8, :], c.rearrange("a (r f) -> (a r) f", f=P)).then_inc(small_in, 16)
            for i, g in enumerate((a_q_norm, a_k_norm, b_q_norm, b_k_norm, c_q_norm, c_k_norm,
                                   d_q_norm, d_k_norm)):
                for h in range(2):
                    sp.dma_start(rows2[8 + i:9 + i, HD * h:HD * h + HD], g).then_inc(small_in, 16)
            for l in range(2):
                sp.dma_start(rows1[48 * l:48 * l + 48, :],
                             ada_b[l].rearrange("(r f) -> r f", f=P)).then_inc(small_in, 16)
                sp.dma_start(rows1[96 + 8 * l:104 + 8 * l, :],
                             mix_norm_g[l].rearrange("(r f) -> r f", f=P)).then_inc(small_in, 16)
                sp.dma_start(rows1[112 + 8 * l:120 + 8 * l, :],
                             ffn_norm_g[l].rearrange("(r f) -> r f", f=P)).then_inc(small_in, 16)
            sp.dma_start(snk[:, :], a_sink.partition_broadcast(P)[:, 0, :]).then_inc(small_in, 16)
            sp.dma_start(fb[:, :], c_forget_bias.partition_broadcast(P)[:, 0, :])\
                .then_inc(small_in, 16)
            for p in range(2, 4):
                first_panel(p)
            sp.dma_start(relv[:, 0:384], b_rel_bias[0, :, REL - P + 1:2 * REL + 1])\
                .then_inc(rel_in, 16)

            def load(n, parity, dst_src):
                sp.wait_ge(w_lo, n + 1)
                for dst, src in dst_src:
                    sp.dma_start(dst, src).then_inc(raw_in[parity], 16)

            def in_slot(l, col, width, parity):
                dst = raw[parity][:, 0:KC * width].rearrange("p (k c) -> p k c", k=KC)
                src = w_in[l].rearrange("(k p) c -> p k c", p=P)
                return [(dst[:, 4 * a:4 * a + 4, :], src[:, 4 * a:4 * a + 4, bass.ds(col, width)])
                        for a in range(2)]

            def out_slot(l, i, parity):
                dst = raw[parity][:, :].rearrange("p (k c) -> p k c", k=KC)
                src = w_out[l].rearrange("(k p) c -> p k c", p=P)
                return [(dst[:, 4 * a:4 * a + 4, :],
                         src[:, 4 * a:4 * a + 4, 256 * i:256 * i + 256]) for a in range(2)]

            def gu_slot(l, col, parity):
                dst = raw[parity][:, :].rearrange("p (h k c) -> p h k c", h=2, k=KC)
                src = ffn_w_gate_up[l].rearrange("(k p) c -> p k c", p=P)
                return [(dst[:, h], src[:, :, bass.ds(col + FF * h, P)]) for h in range(2)]

            def down_slot(l, half, col, parity):
                n_k = HALF[half]
                row = P * HALF[0] * half
                dst = raw[parity][:, 0:n_k * P].rearrange("p (k c) -> p k c", k=n_k)
                src = ffn_w_down[l, row:row + P * n_k, :].rearrange("(k p) c -> p k c", p=P)
                m = n_k // 2
                return [(dst[:, a * m:a * m + m, :], src[:, a * m:a * m + m, bass.ds(col, P)])
                        for a in range(2)]

            for l in range(2):
                n0 = SLOT_BASE[l]
                if l == 1:
                    for i, block in enumerate(BLOCKS[1][0:4]):
                        load(n0 + i, (n0 + i) % 2,
                             in_slot(l, 256 * block, in_width(l, block), (n0 + i) % 2))
                first = n0 + 4 * l
                with sp.Fori(0, 4 - l) as pair_of_slots:
                    i = pair_of_slots * 2
                    for j in range(2):
                        b = (first + j) % 2
                        load(i + (first + j), b, in_slot(l, i * 256 + 256 * j, 256, b))
                if l == 0:
                    load(n0 + 8, (n0 + 8) % 2, in_slot(l, 2048, 256, (n0 + 8) % 2))
                for i in range(4):
                    n = OUT_BASE[l] + i
                    load(n, n % 2, out_slot(l, i, n % 2))
                    if l == 0 and i == 0:
                        sp.wait_ge(rel_rev, 1)
                        sp.dma_start(rel_scratch, relv[:, :]).then_inc(rel_out, 16)
                        sp.wait_ge(rel_out, 16)
                        sp.wait_ge(ac_step, 12 * 8 + ADA_FREE)
                        sp.dma_start(toep[:, :, :], bass.AP(tensor=rel_scratch.tensor, offset=0,
                                                            ap=[[1, P], [RELW, 8], [1, S]]))\
                            .then_inc(bt_in, 16)
                for half in range(2):
                    n0 = GU_BASE[l][half]
                    with sp.Fori(0, HALF[half] // 2) as pair_of_slots:
                        i = pair_of_slots * 2
                        for j in range(2):
                            b = (n0 + j) % 2
                            load(i + (n0 + j), b,
                                 gu_slot(l, i * P + P * (HALF[0] * half + j), b))
                    n0 = DN_BASE[l][half]
                    with sp.Fori(0, 4) as pair_of_slots:
                        i = pair_of_slots * 2
                        for j in range(2):
                            b = (n0 + j) % 2
                            load(i + (n0 + j), b, down_slot(l, half, i * P + P * j, b))
            for q in range(KC // 2):
                sp.wait_ge(yt_ev, 2 * q + 2)
                cols = slice(2 * P * q, 2 * P * q + 2 * P)
                sp.dma_start(out[0].rearrange("(t p) f -> p t f", p=P)[:, :, cols],
                             ytok[:, :, cols]).then_inc(y_out, 16)
            sp.wait_ge(y_out, 16 * (KC // 2))

        @block.gpsimd
        def _(pool):
            n_const = [0]

            def step(ins):
                n_const[0] += 1
                ins.then_inc(consts, 1)
                pool.wait_ge(consts, n_const[0])

            def ada_load(l, a, col, half):
                pool.wait_ge(ac_step, a * 4 + 4)
                src = ada_w[l].rearrange("(k p) c -> p k c", p=P)
                pool.dma_start(ada[half][:, :, :],
                               src[:, 4 * half:4 * half + 4, bass.ds(col, 512)])\
                    .then_inc(ada_in[half], 16)

            step(nc.gpsimd.memset(ident[:, :], 0.0))
            step(nc.gpsimd.affine_select(out=ident[:, :], in_=ident[:, :],
                                         compare_op=ALU.not_equal, fill=1.0, base=0,
                                         pattern=[[-1, P]], channel_multiplier=1))
            step(nc.gpsimd.memset(ones[:, :], 1.0))
            step(nc.gpsimd.memset(epsc[:, :], EPS))
            step(nc.gpsimd.iota(adi[:, :], pattern=[[-1, S]], base=S - P, channel_multiplier=1))
            for h in range(8):
                step(nc.gpsimd.memset(slopes[:, h:h + 1], -2.0 ** (-(h + 1))))
            step(nc.gpsimd.memset(maskb[:, :], 0.0))
            step(nc.gpsimd.affine_select(out=maskb[:, :], in_=maskb[:, :], compare_op=ALU.is_ge,
                                         fill=-BIG, base=0, pattern=[[-1, P]],
                                         channel_multiplier=1))
            step(nc.gpsimd.tensor_copy(identb[:, :], ident[:, :]))
            def add_squares(nn):
                for m in range(1, KC - 1):
                    pool.wait_ge(q_sq, 8 * nn + m + 1)
                    if m >= 2:
                        pool.wait_ge(sq_add, 6 * nn + m - 1)
                    nc.gpsimd.tensor_tensor(tmp[0][:, :], tmp[0][:, :], sq[m % 2][:, :],
                                            ALU.add).then_inc(sq_add, 1)

            add_squares(0)
            with pool.Fori(0, 8) as i:
                for half in range(2):
                    ada_load(0, i * 2 + (8 + half), i * 512 + 2048, half)

            def lay_out(l, job):
                if job.n >= 2:
                    pool.wait_ge(j_mm, job.n - 1)
                for half in range(2):
                    dst = jn[job.n % 2][:, :, HD * half:HD * half + HD]
                    src = proj[l][:, :, job.col:job.col + HD]
                    ins = nc.gpsimd.tensor_tensor(
                        dst, src, rs[:, :, job.stat:job.stat + 1].to_broadcast([P, TT, HD]),
                        ALU.mult)
                ins.then_inc(j_in, 1)

            for l in range(2):
                if l == 1:
                    pool.wait_ge(p_ev, IX_EV)
                    for n, col in enumerate(INDEX_COLS):
                        if n >= 2:
                            pool.wait_ge(ij_mm, n - 1)
                        for half in range(2):
                            ins = nc.gpsimd.tensor_copy(
                                ijn[n % 2][:, :, HD * half:HD * half + HD],
                                proj[1][:, :, col:col + HD])
                        ins.then_inc(ij_in, 1)
                pool.wait_ge(st_ok, l + 1)
                for v in range(UNITS + SCALE_LAG):
                    for job in JOBS[l]:
                        if job.step == v + LAY_AHEAD or v == 0 and -1 <= job.step < LAY_AHEAD:
                            lay_out(l, job)
                    if v >= SCALE_LAG:
                        u = Unit(l, v - SCALE_LAG)
                        if u.n >= DIAGS:
                            pool.wait_ge(pt_mm, u.n - DIAGS + 1)
                        pool.wait_ge(sc_rc, u.n + 1)
                        nc.gpsimd.tensor_scalar(dg[u.v % DIAGS][:, :], ident[:, :],
                                                rinv[:, u.v % RING:u.v % RING + 1],
                                                None, ALU.mult).then_inc(sc_dg, 1)
                if l == 0:
                    pool.wait_ge(sc_mm, UNITS)
                    for half in range(2):
                        ada_load(1, 24 + half, 0, half)
                    add_squares(1)
                    with pool.Fori(1, 12) as i:
                        for half in range(2):
                            ada_load(1, i * 2 + (24 + half), i * 512, half)
                    add_squares(2)
                    pool.wait_ge(x_done, 8 + 24)
                    step(nc.gpsimd.memset(TRI[:, 0:384], 0.0))
                    step(nc.gpsimd.memset(TRI[:, 384:896], 1.0))
                    step(nc.gpsimd.affine_select(out=TRI[:, 384:512], in_=TRI[:, 384:512],
                                                 compare_op=ALU.is_ge, fill=0.0, base=0,
                                                 pattern=[[1, P]], channel_multiplier=-1))
                    step(nc.gpsimd.memset(SEL[:, :, :], 0.0))
                    for part in range(3):
                        step(nc.gpsimd.affine_select(out=SEL[:, :, :], in_=SEL[:, :, :],
                                                     compare_op=ALU.not_equal, fill=1.0,
                                                     base=-32 * part, pattern=[[-1, 8], [0, P]],
                                                     channel_multiplier=1))
                    step(nc.gpsimd.memset(cum3[:, :], 0.0))
                else:
                    add_squares(3)

        N_CONST0 = 5 + 8 + 3
        N_CONST1 = N_CONST0 + 8

        @block.scalar
        def _(act):
            for t in range(TT):
                act.dma_start(xtok[:, t, :], x[0, P * t:P * t + P, :]).then_inc(x_in, 16)
            act.sem_inc(p_ev, PEV_FREE)
            act.sem_inc(g_hi, GHI_FREE)

            def cut_hi(n, b, landed, width):
                act.wait_ge(raw_in[b], landed)
                act.wait_ge(w_used, n + 1)
                nc.scalar.activation(whi[b][:, 0:width], raw[b][:, 0:width], ACT.Copy)\
                    .then_inc(w_hi, 1)

            def landed(n):
                return 32 * (n // 2 + 1)

            def square(nn, m):
                act.wait_ge(x_done, X_BASE[nn] + m + 1)
                if m >= 3:
                    act.wait_ge(sq_add, 6 * nn + m - 2)
                elif nn > 0:
                    act.wait_ge(ss_mm, 2 * nn)
                nc.scalar.activation((tmp[0] if m == 0 else sq[m % 2])[:, :], xT[:, m, :],
                                     ACT.Square).then_inc(q_sq, 1)

            def norm_rms(nn):
                act.wait_ge(ss_mm, 2 * nn + 2)
                nc.scalar.activation(nsr[:, :], psum[6][:, 0:TT], ACT.Sqrt, bias=epsc[:, 0:1],
                                     scale=1.0 / D).then_inc(n_rt, 1)

            def norm_h(nn, shift, l):
                if nn:
                    norm_rms(nn)
                n = (SLOT_BASE[l] if shift == 0 else GU_BASE[l][0]) + 1
                cut_hi(n, n % 2, landed(n), in_slot_width(l, 1) if shift == 0 else 2048)
                for k in range(KC):
                    act.wait_ge(h_t, 8 * nn + k + 1)
                    nc.scalar.activation(hhi[:, k, :], tmp[k % 2][:, :], ACT.Identity,
                                         bias=mods[:, l, shift + k:shift + k + 1])\
                        .then_inc(h_hi, 1)

            def in_out(l, s, t, width, col):
                if t < 3:
                    act.wait_ge(p_mm, s * 3 + (t + 1))
                else:
                    act.wait_ge(w_used, s + (SLOT_BASE[l] - IN_BASE[l] + 1 + W_FREE))
                nc.scalar.activation(proj[l][:, t, bass.ds(col, width)],
                                     psum[t][:, 0:width], ACT.Copy).then_inc(p_ev, 1)

            def result_out(m):
                act.wait_ge(yt_mm, m + 1)
                nc.scalar.activation(ytok[:, :, P * m:P * m + P],
                                     psum[m % 2][:, :].rearrange("p (t c) -> p t c", t=TT),
                                     ACT.Copy).then_inc(yt_ev, 1)

            act.wait_ge(consts, 4)
            act.wait_ge(c_mm, 1)
            nc.scalar.activation(cond[:, :], psum[4][:, 0:8], ACT.Silu).then_inc(cond_ok, 1)
            for m in range(KC):
                square(0, m)
            norm_rms(0)
            cut_hi(0, 0, landed(0), 2048)

            for l in range(2):
                n0, s0 = SLOT_BASE[l], IN_BASE[l]
                norm_h(2 * l, 0, l)
                nst = NORMED[l][1][2] + NORMED[l][1][1]
                if l == 0:
                    with act.Fori(0, 4) as pair_of_slots:
                        i = pair_of_slots * 2
                        for j in range(2):
                            for t in range(TT):
                                in_out(l, i + (s0 + j), t, 256, i * 256 + 256 * j)
                            cut_hi(i + (n0 + j + 2), (n0 + j) % 2, i * 16 + landed(n0 + j + 2),
                                   2048)
                for i in range(8 if l == 0 else 0, IN_SLOTS[l]):
                    if l == 1 and i == FORGET_SLOT:
                        act.wait_ge(fg_z, 2)
                        nc.scalar.activation(ze[:, :, :], za[:, :, :], ACT.Exp, scale=-1.0)\
                            .then_inc(fg_e, 1)
                        act.wait_ge(fg_e, 1)
                        nc.scalar.activation(za[:, :, :], ze[:, :, :], ACT.Ln,
                                             bias=ones[:, 0:1]).then_inc(fg_l, 1)
                    for t in range(TT):
                        if i == IN_SLOTS[l] - 1 and t == TT - 1:
                            act.wait_ge(st_rd, 4 * l + TT)
                            nc.scalar.activation(rt[:, :, 0:nst], ssq[:, :, 0:nst], ACT.Sqrt,
                                                 bias=epsc[:, 0:1], scale=1.0 / HD)\
                                .then_inc(st_rt, 1)
                        block = BLOCKS[l][i]
                        in_out(l, s0 + i, t, in_width(l, block), 256 * block)
                        for tile in STATS[l].get((i, t), ()):
                            act.wait_ge(p_ev, 4 * (s0 + 8) + PEV_FREE)
                            if tile >= 2:
                                act.wait_ge(st_rd, 4 * l + tile - 1)
                            for col, heads, stat in NORMED[l]:
                                ins = nc.scalar.activation(
                                    sqs[l][tile % 2][:, HD * stat:HD * (stat + heads)],
                                    proj[l][:, tile, col:col + HD * heads], ACT.Square)
                            ins.then_inc(st_sq, 1)
                        if l == 1 and (i, t) == CUM_AT:
                            act.wait_ge(cm_mm, 1)
                            nc.scalar.activation(cum3[0:8, :], psum[4][0:8, :], ACT.Copy)\
                                .then_inc(cm_hi, 1)
                        if l == 1 and (i, t) == MID_AT:
                            act.wait_ge(cm_lo, 1)
                            nc.scalar.activation(mid0[:, :], rest[:, :], ACT.Copy)\
                                .then_inc(cm_hi, 1)
                            act.wait_ge(cm_hi, 2)
                            nc.scalar.activation(cum3[32:40, :], mid0[:, :], ACT.Copy)\
                                .then_inc(cm_hi, 1)
                        if l == 1 and (i, t) in INDEX_TURNS:
                            n = INDEX_TURNS[i, t]
                            act.wait_ge(ij_mm, n + 1)
                            dst = ikh if n == 0 else iq[n - 1]
                            nc.scalar.activation(dst[:, :], psum[5 + n % 2][:, :], ACT.Copy)\
                                .then_inc(ij_hi, 1)
                        if l == 1 and (i, t) in INDEX_PRODUCTS:
                            tile, head = INDEX_PRODUCTS[i, t]
                            for h in (head, head + 1):
                                u = 4 * (tile - 1) + h
                                act.wait_ge(ix_mm, u + 1)
                                if u >= 2:
                                    act.wait_ge(ix_ac, u - 1)
                                nc.scalar.activation(sq[h % 2][:, 0:P * (tile + 1)],
                                                     psum[4 + 3 * (h % 2)][:, 0:P * (tile + 1)],
                                                     ACT.Relu).then_inc(ix_rl, 1)
                    if i + 2 <= IN_SLOTS[l]:
                        cut_hi(n0 + i + 2, (n0 + i) % 2, landed(n0 + i + 2),
                               in_slot_width(l, i + 2))

                def part_hi(job):
                    act.wait_ge(j_mm, job.n + 1)
                    if job.pair >= 2:
                        act.wait_ge(sc_mm, UNITS * l + 8 * (job.pair - 1))
                    dst = (qs if job.what == "q" else kh)[job.buf][job.h]
                    gain = (qg8 if job.what == "q" else cols2)[:, job.gain:job.gain + 1]
                    nc.scalar.activation(dst[:, :], psum[5 + job.n % 2][:, :], ACT.Copy,
                                         scale=gain).then_inc(j_hi, 1)

                if l == 0:
                    act.wait_ge(bt_ok, 1)

                def exps(v):
                    u = Unit(l, v)
                    w = u.width + (u.group.kind == "A")
                    act.wait_ge(sc_mx, u.n + 1)
                    src = Ssb[:, v % RING, 0:w]
                    if u.group.kind == "C":
                        act.wait_ge(pt_mm, u.n - RING + 1)
                        src = psum[v % 2][:, 0:w]
                    nc.scalar.activation(Ssb[:, v % RING, 0:w], src, ACT.Exp,
                                         bias=nm[:, v % RING:v % RING + 1],
                                         accum_out=rsum[:, v % RING:v % RING + 1]).then_inc(sc_ex, 1)

                def probs_out(v):
                    u = Unit(l, v)
                    act.wait_ge(pt_mm, u.n + 1)
                    if u.head >= 2:
                        act.wait_ge(pv_mm, HEADS * l + u.head - 1)
                    nc.scalar.activation(
                        PT[u.h][:, u.first:u.t + 1, P * u.t:P * u.t + P],
                        psum[2 + v % 2][:, 0:u.width].rearrange("p (k c) -> p k c", c=P),
                        ACT.Copy).then_inc(pt_ev, 1)

                def output_hi(pair):
                    act.wait_ge(pv_mm, HEADS * l + 2 * pair + 2)
                    nc.scalar.activation(
                        out_parts(l, pair)[0],
                        out_bank(pair)[:, :].rearrange("p (t c) -> p t c", t=TT),
                        ACT.Copy).then_inc(o_hi, 1)

                for job in JOBS[l]:
                    if job.step == -1:
                        part_hi(job)
                for v in range(STEPS):
                    for job in JOBS[l]:
                        if job.step == v:
                            part_hi(job)
                    if v < UNITS:
                        exps(v)
                    if 0 <= v - OUT_LAG < UNITS:
                        probs_out(v - OUT_LAG)
                    if v >= O_HI_LAG and (v - O_HI_LAG) % 8 == 7:
                        output_hi((v - O_HI_LAG) // 8)

                for i in range(4):
                    n = OUT_BASE[l] + i
                    cut_hi(n + 1, (n + 1) % 2, landed(n + 1), 2048)
                    for m in (2 * i, 2 * i + 1):
                        square(2 * l + 1, m)
                norm_h(2 * l + 1, 24, l)

                for half in range(2):
                    nh, n0, f0 = HALF[half], GU_BASE[l][half], FT * l + HALF[0] * half

                    def hidden(n, f, b, out_ap):
                        act.wait_ge(w_used, n + (1 + W_FREE))
                        act.wait_ge(g_a, f + 1)
                        nc.scalar.activation(sq[b][:, :], psum[2 * b][:, :], ACT.Silu)\
                            .then_inc(g_si, 1)
                        act.wait_ge(g_a, f + (1 + GA_FREE))
                        nc.scalar.activation(out_ap, tmp[b][:, :], ACT.Copy).then_inc(g_hi, 1)

                    if half == 1:
                        cut_hi(n0 + 1, (n0 + 1) % 2, landed(n0 + 1), 2048)
                    with act.Fori(0, nh // 2 - 1) as pair_of_slots:
                        i = pair_of_slots * 2
                        for j in range(2):
                            hidden(i + (n0 + j), i + (f0 + j), j,
                                   acthi[:, bass.ds(i + j, 1), :])
                            cut_hi(i + (n0 + j + 2), (n0 + j) % 2, i * 16 + landed(n0 + j + 2),
                                   2048)
                    for j in (nh - 2, nh - 1):
                        hidden(n0 + j, f0 + j, j % 2, acthi[:, j:j + 1, :])
                        if j == nh - 2:
                            cut_hi(n0 + nh, (n0 + nh) % 2, landed(n0 + nh), nh * P)
                    n0 = DN_BASE[l][half]
                    squares, end = (l, half) == (0, 1), (l, half) == (1, 1)
                    if not squares and not end:
                        with act.Fori(0, 3) as pair_of_slots:
                            i = pair_of_slots * 2
                            for j in range(2):
                                b = (n0 + j + 1) % 2
                                cut_hi(i + (n0 + j + 1), b, i * 16 + landed(n0 + j + 1), nh * P)
                    for j in range(0 if squares or end else 6, 8):
                        if not (l == 1 and half == 1 and j == 7):
                            cut_hi(n0 + j + 1, (n0 + j + 1) % 2, landed(n0 + j + 1),
                                   nh * P if j < 7 else 2048)
                        if squares:
                            square(2, j)
                        if end and j >= 1:
                            result_out(j - 1)
            result_out(KC - 1)

        @block.vector
        def _(dve):
            dve.sem_inc(w_lo, RAW_FREE)
            dve.sem_inc(ac_step, ADA_FREE)
            dve.sem_inc(g_a, GA_FREE)
            dve.sem_inc(g_lo, GLO_FREE)
            links = [0]

            def link(ins):
                links[0] += 1
                ins.then_inc(dchain, 1)
                dve.wait_ge(dchain, links[0])

            def cut_lo(n, b, width):
                dve.wait_ge(w_hi, n + 1)
                nc.vector.tensor_tensor(wlo[b][:, 0:width], raw[b][:, 0:width],
                                        whi[b][:, 0:width], ALU.subtract).then_inc(w_lo, 1)

            def ada_panel(panel, landed, b, first=False, late=False):
                for half in range(2):
                    if first:
                        dve.wait_ge(first_in[panel], 32)
                    else:
                        dve.wait_ge(ada_in[half], landed)
                    for k in range(4):
                        s = 4 * half + k
                        halves = ada_first[panel] if first else ada
                        src, by = halves[half][:, k, :], cond[:, s:s + 1]
                        dve.wait_ge(ac_step, panel * 8 + (s + ADA_FREE))
                        if s == 0:
                            dve.wait_ge(acc_used, panel + (1 if first or not late else 2))
                            ins = nc.vector.tensor_scalar(acc[b][:, :], src, by, None, ALU.mult)
                        else:
                            ins = nc.vector.scalar_tensor_tensor(
                                out=acc[b][:, :], in0=src, scalar=by, in1=acc[b][:, :],
                                op0=ALU.mult, op1=ALU.add)
                        ins.then_inc(ac_step, 1)

            def take_mods(l, lo, hi, panels):
                dve.wait_ge(acc_used, panels + ACC_FREE)
                link(nc.vector.tensor_tensor(mods[:, l, lo:hi], psum[7][:, lo:hi],
                                             cols1[:, 48 * l + lo:48 * l + hi], ALU.add))

            def take_coef(nn, l, scale, gain):
                link(nc.vector.scalar_tensor_tensor(
                    out=coef[:, nn, :], in0=mods[:, l, scale:scale + 8], scalar=1.0,
                    in1=cols1[:, gain:gain + 8], op0=ALU.add, op1=ALU.mult))

            def inverse(out_ap, root, mean, t1):
                link(nc.vector.reciprocal(out_ap, root))
                link(nc.vector.tensor_tensor(t1, out_ap, out_ap, ALU.mult))
                link(nc.vector.tensor_tensor(t1, t1, mean, ALU.mult))
                link(nc.vector.tensor_scalar(t1, t1, -0.5, 1.5, ALU.mult, ALU.add))
                return nc.vector.tensor_tensor(out_ap, out_ap, t1, ALU.mult)

            def norm_rms(nn):
                dve.wait_ge(n_rt, nn + 1)
                link(nc.vector.tensor_scalar(nms[:, :], psum[6][:, 0:TT], 1.0 / D, EPS,
                                             ALU.mult, ALU.add))
                link(inverse(nrs[:, :], nsr[:, :], nms[:, :], nnt[:, :]))
                for t in range(TT):
                    ins = nc.vector.tensor_scalar(diag[:, t, :], ident[:, :], nrs[:, t:t + 1],
                                                  None, ALU.mult)
                ins.then_inc(n_dg, 1)

            def norm_h(nn, l, shift):
                if nn:
                    norm_rms(nn)
                    n = (SLOT_BASE[l] if shift == 0 else GU_BASE[l][0]) + 1
                    cut_lo(n, n % 2, in_slot_width(l, 1) if shift == 0 else 2048)
                dve.wait_ge(n_bc, nn + 1)

                def lo(k):
                    dve.wait_ge(h_hi, 8 * nn + k + 1)
                    nc.vector.scalar_tensor_tensor(
                        out=hlo[:, k, :], in0=tmp[k % 2][:, :],
                        scalar=mods[:, l, shift + k:shift + k + 1], in1=hhi[:, k, :],
                        op0=ALU.add, op1=ALU.subtract).then_inc(h_lo, 1)

                for k in range(KC):
                    if k >= 2:
                        dve.wait_ge(h_lo, 8 * nn + k - 1)
                    nc.vector.scalar_tensor_tensor(
                        out=tmp[k % 2][:, :], in0=xT[:, k, :], scalar=coef[:, nn, k:k + 1],
                        in1=psum[5][:, :], op0=ALU.mult, op1=ALU.mult).then_inc(h_t, 1)
                    if k:
                        lo(k - 1)
                lo(KC - 1)

            def index_scores(t, head):
                w = P * (t + 1)
                row = dsel[:, DS_OFF[t]:DS_OFF[t] + w]
                for h in (head, head + 1):
                    v = 4 * (t - 1) + h
                    dve.wait_ge(ix_rl, v + 1)
                    by = wis[:, t, h:h + 1]
                    if h == 0:
                        ins = nc.vector.tensor_scalar(row, sq[h % 2][:, 0:w], by, 0.0,
                                                      ALU.mult, ALU.add)
                    else:
                        dve.wait_ge(ix_ac, v)
                        ins = nc.vector.scalar_tensor_tensor(
                            out=row, in0=sq[h % 2][:, 0:w], scalar=by, in1=row,
                            op0=ALU.mult, op1=ALU.add)
                    ins.then_inc(ix_ac, 1)

            def top_k(r):
                t, q = 1 + r // ROUNDS, r % ROUNDS
                w = P * (t + 1)
                row = dsel[:, DS_OFF[t]:DS_OFF[t] + w]
                if q == 0:
                    link(nc.vector.memset(
                        dsel[0:CHUNK, DS_OFF[t] + w - 64:DS_OFF[t] + w], OUT_OF_REACH))
                nc.vector.max(top8[:, :], row).then_inc(tk, 1)
                dve.wait_ge(tk, 2 * r + 1)
                nc.vector.match_replace(row, top8[:, :], row, TAKEN).then_inc(tk, 1)
                dve.wait_ge(tk, 2 * r + 2)
                if q == ROUNDS - 1:
                    link(nc.vector.tensor_scalar(row, row, 2 * OUT_OF_REACH, BIG,
                                                 ALU.is_gt, ALU.mult))
                    link(nc.vector.tensor_tensor(row, row, AD[:, S - w:S], ALU.add))

            dve.wait_ge(cond_ok, 1)
            ada_panel(0, None, 0, first=True)
            for k in range(KC):
                dve.wait_ge(xt_mm, k + 1)
                nc.vector.tensor_copy(xT[:, k, :], psum[k % 2][:, :]).then_inc(x_done, 1)
            ada_panel(1, None, 1, first=True)
            for r, (dst, n) in enumerate(((cols1, P), (cols2, 16))):
                dve.wait_ge(rows_t, 2)
                nc.vector.tensor_copy(dst[:, :], psum[3][:, P * r:P * r + n]).then_inc(cols_d, 1)
            dve.wait_ge(cols_d, 2)
            link(nc.vector.tensor_scalar(qg8[:, :], cols2[:, :], HD ** -0.5, None, ALU.mult))
            ada_panel(2, None, 0, first=True)
            norm_rms(0)
            ada_panel(3, None, 1, first=True)
            cut_lo(0, 0, 2048)
            take_mods(0, 0, 16, 4)
            take_coef(0, 0, 8, 96)
            cut_lo(1, 1, 2048)

            for l in range(2):
                n0, s0 = SLOT_BASE[l], IN_BASE[l]
                nst = NORMED[l][1][2] + NORMED[l][1][1]
                norm_h(2 * l, l, 0)
                if l == 0:
                    dve.wait_ge(consts, 5)
                    link(nc.vector.scalar_tensor_tensor(out=AD[:, :], in0=adi[:, :], scalar=-1.0,
                                                        in1=adi[:, :], op0=ALU.mult, op1=ALU.max))
                    link(nc.vector.memset(AD[0:CHUNK, 448:512], BIG))
                    link(nc.vector.tensor_copy(AW[:, :], AD[:, 256:512]))
                    link(nc.vector.memset(AW[0:CHUNK, 0:64], BIG))
                    link(nc.vector.memset(AW[CHUNK:P, 0:128], BIG))
                    dve.wait_ge(rel_in, 16)
                    nc.vector.tensor_copy(relv[:, 384:RELW],
                                          relv[:, 383:384].to_broadcast([8, 256]))\
                        .then_inc(rel_rev, 1)
                    with dve.Fori(0, 4) as pair_of_slots:
                        i = pair_of_slots * 2
                        for j in range(2):
                            ada_panel(i + (4 + j), i * 16 + 16 * (1 + j), j)
                            cut_lo(i + (n0 + j + 2), (n0 + j) % 2, 2048)
                for i in range(8 if l == 0 else 0, IN_SLOTS[l]):
                    if l == 1 and i == FORGET_SLOT:
                        dve.wait_ge(p_ev, 4 * (s0 + 3) + PEV_FREE)
                        link(nc.vector.tensor_tensor(
                            zt[:, :, :], proj[1][:, :, FC:FC + 8],
                            fb[:, :].unsqueeze(1).to_broadcast([P, TT, 8]), ALU.add))
                        nc.vector.scalar_tensor_tensor(
                            out=za[:, :, :], in0=zt[:, :, :], scalar=-1.0, in1=zt[:, :, :],
                            op0=ALU.mult, op1=ALU.max).then_inc(fg_z, 1)
                        nc.vector.tensor_scalar(zt[:, :, :], zt[:, :, :], 0.0, None, ALU.min)\
                            .then_inc(fg_z, 1)
                        dve.wait_ge(fg_z, 2)
                    if l == 1 and i == REST_SLOT:
                        dve.wait_ge(cm_hi, 1)
                        nc.vector.tensor_tensor(rest[:, :], psum[4][0:8, :], cum3[0:8, :],
                                                ALU.subtract).then_inc(cm_lo, 1)
                    if l == 1 and i == LOW_SLOT:
                        dve.wait_ge(cm_hi, 2)
                        nc.vector.tensor_tensor(cum3[64:72, :], rest[:, :], mid0[:, :],
                                                ALU.subtract).then_inc(cm_lo, 1)
                    if l == 1 and i == FORGET_SLOT + 1:
                        dve.wait_ge(fg_l, 1)
                        nc.vector.tensor_tensor(zt[:, :, :], za[:, :, :], zt[:, :, :],
                                                ALU.subtract).then_inc(fg_n, 1)
                    for t in range(TT):
                        for tile in STATS[l].get((i, t), ()):
                            dve.wait_ge(st_sq, 4 * l + tile + 1)
                            nc.vector.tensor_reduce(
                                ssq[:, tile, 0:nst],
                                sqs[l][tile % 2][:, 0:HD * nst].rearrange("p (h d) -> p h d", d=HD),
                                AX.X, ALU.add).then_inc(st_rd, 1)
                    if i == IN_SLOTS[l] - 1:
                        dve.wait_ge(st_rt, l + 1)
                        link(nc.vector.tensor_scalar(ssq[:, :, 0:nst], ssq[:, :, 0:nst], 1.0 / HD,
                                                     EPS, ALU.mult, ALU.add))
                        inverse(rs[:, :, 0:nst], rt[:, :, 0:nst], ssq[:, :, 0:nst],
                                nt1[:, :, 0:nst]).then_inc(st_ok, 1)
                    if l == 0:
                        continue
                    if i == 2:
                        dve.wait_ge(p_ev, IX_EV)
                        link(nc.vector.tensor_scalar(wis[:, :, :], proj[1][:, :, WI:WI + 4],
                                                     (HD * 4) ** -0.5, None, ALU.mult))
                        link(nc.vector.tensor_copy(dsel[:, 0:P], AD[:, S - P:S]))
                    for t in range(TT):
                        if (i, t) in INDEX_TURNS:
                            n = INDEX_TURNS[i, t]
                            dve.wait_ge(ij_hi, n + 1)
                            if n == 0:
                                hi, lo, rows = ikh, ikl, slice(0, P)
                            else:
                                hi, lo, rows = iq[n - 1], iq[n - 1], slice(HD, P)
                            nc.vector.tensor_tensor(lo[rows, :], psum[5 + n % 2][rows, :],
                                                    hi[rows, :], ALU.subtract).then_inc(ij_lo, 1)
                        if (i, t) in INDEX_PRODUCTS:
                            index_scores(*INDEX_PRODUCTS[i, t])
                    for q in range(*TOP_K_SLOTS.get(i, (0, 0))):
                        if q == 0:
                            dve.wait_ge(ix_ac, 12)
                        top_k(q)
                    if i + 2 <= IN_SLOTS[l]:
                        cut_lo(n0 + i + 2, (n0 + i) % 2, in_slot_width(l, i + 2))
                if l == 0:
                    take_mods(0, 16, 48, 12)
                    take_coef(1, 0, 32, 112)
                    nc.vector.memset(scr4[:, 0:1], 0.0).then_inc(mods_done, 1)

                def part_lo(job):
                    dve.wait_ge(j_hi, job.n + 1)
                    rows = slice(HD, P) if job.what == "q" else slice(0, P)
                    hi = (qs if job.what == "q" else kh)[job.buf][job.h][rows, :]
                    lo = (qs if job.what == "q" else kl)[job.buf][job.h][rows, :]
                    src = psum[5 + job.n % 2][rows, :]
                    gain = (qg8 if job.what == "q" else cols2)[rows, job.gain:job.gain + 1]
                    nc.vector.scalar_tensor_tensor(out=lo, in0=src, scalar=gain, in1=hi,
                                                   op0=ALU.mult, op1=ALU.subtract)\
                        .then_inc(j_lo, 1)

                if l == 0:
                    dve.wait_ge(bt_in, 16)
                    link(nc.vector.tensor_copy(BT[:, :, :], toep[:, :, ::-1]))
                    nc.vector.memset(BT[0:CHUNK, :, S - CHUNK:S], -BIG).then_inc(bt_ok, 1)
                    dve.wait_ge(bt_ok, 1)

                def add_bias(v):
                    u = Unit(l, v)
                    w, kind, head = u.width, u.group.kind, u.group_head
                    dve.wait_ge(sc_mm, u.n + 1)
                    if kind == "C":
                        nc.vector.tensor_reduce(nm[:, v % RING:v % RING + 1],
                                                psum[v % 2][:, 0:w], AX.X, ALU.max,
                                                negate=True).then_inc(sc_mx, 1)
                        return
                    if u.n >= RING:
                        dve.wait_ge(pt_mm, u.n - RING + 1)
                    s_out = Ssb[:, v % RING, 0:w]
                    if kind in "AD":
                        if kind == "A":
                            table = AW[:, 256 - w:256]
                        else:
                            table = dsel[:, DS_OFF[u.t]:DS_OFF[u.t] + w]
                        nc.vector.scalar_tensor_tensor(
                            out=s_out, in0=table, scalar=slopes[:, head:head + 1],
                            in1=psum[v % 2][:, 0:w], op0=ALU.mult, op1=ALU.add).then_inc(sc_dv, 1)
                    else:
                        nc.vector.tensor_tensor(s_out, psum[v % 2][:, 0:w], BT[:, head, S - w:S],
                                                ALU.add).then_inc(sc_dv, 1)
                    if kind == "A":
                        nc.vector.tensor_copy(Ssb[:, v % RING, w:w + 1], snk[:, head:head + 1])\
                            .then_inc(sink_in, 1)
                        dve.wait_ge(sink_in, u.n + 1)
                        w += 1
                    dve.wait_ge(sc_dv, copied_out(u.n))
                    nc.vector.tensor_reduce(nm[:, v % RING:v % RING + 1], Ssb[:, v % RING, 0:w],
                                            AX.X, ALU.max, negate=True).then_inc(sc_mx, 1)

                def invert_sum(v):
                    dve.wait_ge(sc_ex, UNITS * l + v + 1)
                    nc.vector.reciprocal(rinv[:, v % RING:v % RING + 1],
                                         rsum[:, v % RING:v % RING + 1]).then_inc(sc_rc, 1)

                def output_lo(pair):
                    dve.wait_ge(o_hi, PAIRS * l + pair + 1)
                    hi, lo = out_parts(l, pair)
                    nc.vector.tensor_tensor(
                        lo, out_bank(pair)[:, :].rearrange("p (t c) -> p t c", t=TT), hi,
                        ALU.subtract).then_inc(o_lo, 1)

                for job in JOBS[l]:
                    if job.step == -1:
                        part_lo(job)
                for v in range(STEPS):
                    if v < UNITS:
                        add_bias(v)
                    if 0 <= v - SCALE_LAG < UNITS:
                        invert_sum(v - SCALE_LAG)
                    for job in JOBS[l]:
                        if job.step == v:
                            part_lo(job)
                    if v >= O_LO_LAG and (v - O_LO_LAG) % 8 == 7:
                        output_lo((v - O_LO_LAG) // 8)
                    if l == 1 and TOP_K_LATE + v < 3 * ROUNDS:
                        top_k(TOP_K_LATE + v)

                def add_chunk(bank, gate, m, x_ap):
                    nc.vector.scalar_tensor_tensor(
                        out=x_ap, in0=psum[bank][:, :], scalar=mods[:, l, bass.ds(gate + m, 1)]
                        if not isinstance(m, int) else mods[:, l, gate + m:gate + m + 1],
                        in1=x_ap, op0=ALU.mult, op1=ALU.add).then_inc(x_done, 1)

                for i in range(4):
                    n = OUT_BASE[l] + i
                    cut_lo(n + 1, (n + 1) % 2, 2048)
                    dve.wait_ge(y_half, 4 * l + i + 1)
                    add_chunk(4, 16, 2 * i, xT[:, 2 * i, :])
                    dve.wait_ge(w_used, n + 1 + W_FREE)
                    add_chunk(5, 16, 2 * i + 1, xT[:, 2 * i + 1, :])
                norm_h(2 * l + 1, l, 24)

                for half in range(2):
                    nh, n0, f0 = HALF[half], GU_BASE[l][half], FT * l + HALF[0] * half

                    def hidden(n, f, b, hi_ap, lo_ap):
                        dve.wait_ge(g_si, f + 1)
                        dve.wait_ge(g_hi, f + 1)
                        dve.wait_ge(g_lo, f + 1)
                        nc.vector.tensor_tensor(tmp[b][:, :], sq[b][:, :], psum[2 * b + 1][:, :],
                                                ALU.mult).then_inc(g_a, 1)
                        dve.wait_ge(g_hi, f + (1 + GHI_FREE))
                        nc.vector.tensor_tensor(lo_ap, tmp[b][:, :], hi_ap, ALU.subtract)\
                            .then_inc(g_lo, 1)

                    if half == 1:
                        cut_lo(n0 + 1, (n0 + 1) % 2, 2048)
                    with dve.Fori(0, nh // 2 - 1) as pair_of_slots:
                        i = pair_of_slots * 2
                        for j in range(2):
                            if l == 0 and j == 0 and half == 1:
                                ada_panel(pair_of_slots + 19,
                                          pair_of_slots * 16 + 16 * 16, 0, late=True)
                            hidden(i + (n0 + j), i + (f0 + j), j,
                                   acthi[:, bass.ds(i + j, 1), :], actlo[:, bass.ds(i + j, 1), :])
                            cut_lo(i + (n0 + j + 2), (n0 + j) % 2, 2048)
                            if l == 0 and j == 0 and half == 0:
                                ada_panel(pair_of_slots + 12,
                                          pair_of_slots * 16 + 16 * 9, 0, late=True)
                    for j in (nh - 2, nh - 1):
                        if l == 0 and j == nh - 2 and half == 1:
                            ada_panel(23, 16 * 20, 0, late=True)
                        hidden(n0 + j, f0 + j, j % 2, acthi[:, j:j + 1, :], actlo[:, j:j + 1, :])
                        if j == nh - 2:
                            cut_lo(n0 + nh, (n0 + nh) % 2, nh * P)
                        if l == 0 and j == nh - 2 and half == 0:
                            ada_panel(17, 16 * 14, 0, late=True)
                    if l == 0 and half == 1:
                        take_mods(1, 0, 48, 24)
                        take_coef(2, 1, 8, 104)
                        take_coef(3, 1, 32, 120)
                    n0 = DN_BASE[l][half]
                    with dve.Fori(0, 3) as pair_of_slots:
                        i = pair_of_slots * 2
                        for j in range(2):
                            cut_lo(i + (n0 + j + 1), (n0 + j + 1) % 2, nh * P)
                            dve.wait_ge(w_used, i + (n0 + j + 1 + W_FREE))
                            add_chunk(4 + j, 40, i + j, xT[:, bass.ds(i + j, 1), :])
                    for j in (6, 7):
                        if not (l == 1 and half == 1 and j == 7):
                            cut_lo(n0 + j + 1, (n0 + j + 1) % 2, nh * P if j == 6 else 2048)
                        dve.wait_ge(w_used, n0 + j + 1 + W_FREE)
                        add_chunk(4 + j % 2, 40, j, xT[:, j, :])
                        if l == 0 and half == 0 and j == 6:
                            ada_panel(18, 16 * 15, 0, late=True)

        @block.tensor
        def _(pe):
            pe.sem_inc(w_used, W_FREE)
            pe.sem_inc(acc_used, ACC_FREE)

            def three(dst, a_hi, a_lo, b_hi, b_lo, first, last):
                nc.tensor.matmul(dst, a_hi, b_hi, start=first, stop=False)
                nc.tensor.matmul(dst, a_hi, b_lo, start=False, stop=False)
                return nc.tensor.matmul(dst, a_lo, b_hi, start=False, stop=last)

            def turn_result(m):
                pe.wait_ge(x_done, 48 + m + 1)
                if m >= 2:
                    pe.wait_ge(yt_ev, m - 1)
                for t in range(TT):
                    ins = nc.tensor.transpose(psum[m % 2][:, P * t:P * t + P],
                                              xT[:, m, P * t:P * t + P], ident[:, :])
                ins.then_inc(yt_mm, 1)

            def sum_squares(nn):
                for last, src in enumerate((tmp[0], sq[1])):
                    if last:
                        pe.wait_ge(q_sq, 8 * nn + 8)
                    else:
                        pe.wait_ge(sq_add, 6 * nn + 6)
                    for t in range(TT):
                        ins = nc.tensor.matmul(psum[6][:, t:t + 1], src[:, P * t:P * t + P],
                                               ones[:, 0:1], start=not last and t == 0,
                                               stop=last == 1, skip_group_check=True)
                    ins.then_inc(ss_mm, 1)

            def spread(nn):
                pe.wait_ge(n_dg, nn + 1)
                for t in range(TT):
                    ins = nc.tensor.matmul(psum[5][:, P * t:P * t + P], ones[:, :], diag[:, t, :],
                                           start=True, stop=True)
                ins.then_inc(n_bc, 1)

            def mods_mm(panel, b, col):
                pe.wait_ge(ac_step, panel * 8 + (8 + ADA_FREE))
                for j in range(4):
                    ins = nc.tensor.matmul(psum[7][:, bass.ds(col + j, 1)],
                                           acc[b][:, P * j:P * j + P], ones[:, 0:1],
                                           start=True, stop=True)
                ins.then_inc(acc_used, 1)

            pe.wait_ge(consts, 3)
            pe.wait_ge(c_in, 16)
            nc.tensor.transpose(psum[4][:, 0:8], rows3[:, :], ident[0:8, 0:8]).then_inc(c_mm, 1)
            pe.wait_ge(x_in, 16 * TT)
            for k in range(KC):
                if k >= 2:
                    pe.wait_ge(x_done, k - 1)
                for t in range(TT):
                    ins = nc.tensor.transpose(psum[k % 2][:, P * t:P * t + P],
                                              xtok[:, t, P * k:P * k + P], ident[:, :])
                ins.then_inc(xt_mm, 1)
            mods_mm(0, 0, 0)
            pe.wait_ge(small_in, 16 * N_SMALL)
            nc.tensor.transpose(psum[3][:, 0:P], rows1[:, :], ident[:, :]).then_inc(rows_t, 1)
            nc.tensor.transpose(psum[3][:, P:P + 16], rows2[:, :], ident[0:16, 0:16])\
                .then_inc(rows_t, 1)
            mods_mm(1, 1, 4)
            sum_squares(0)
            spread(0)
            for panel in (2, 3):
                mods_mm(panel, panel % 2, 4 * panel)
            pe.wait_ge(cols_d, 2)

            for l in range(2):
                n0, s0 = SLOT_BASE[l], IN_BASE[l]
                if l:
                    spread(2 * l)

                def project_first(n, s, width):
                    b = n0 % 2
                    pe.wait_ge(w_lo, n + (1 + RAW_FREE))
                    pe.wait_ge(p_ev, s * 4 + TT)
                    for k in range(KC):
                        pe.wait_ge(h_lo, 16 * l + k + 1)
                        cols = slice(k * width, k * width + width)
                        for t in range(TT):
                            tok = slice(P * t, P * t + P)
                            ins = three(psum[t][:, 0:width], hhi[:, k, tok],
                                        hlo[:, k, tok], whi[b][:, cols], wlo[b][:, cols],
                                        k == 0, k == KC - 1)
                            if k == KC - 1:
                                ins.then_inc(p_mm if t < 3 else w_used, 1)

                def project(n, s, j, width):
                    b = (n0 + j) % 2
                    pe.wait_ge(w_lo, n + (1 + RAW_FREE))
                    for t in range(TT):
                        pe.wait_ge(p_ev, s * 4 + (t + 1))
                        for k in range(KC):
                            tok = slice(P * t, P * t + P)
                            cols = slice(k * width, k * width + width)
                            ins = three(psum[t][:, 0:width], hhi[:, k, tok],
                                        hlo[:, k, tok], whi[b][:, cols], wlo[b][:, cols],
                                        k == 0, k == KC - 1)
                        ins.then_inc(p_mm if t < 3 else w_used, 1)
                        if l == 1 and (j, t) in INDEX_TURNS:
                            turn_index(INDEX_TURNS[j, t])
                        if l == 1 and (j, t) in INDEX_PRODUCTS:
                            index_products(*INDEX_PRODUCTS[j, t])
                        if l == 1 and (j, t) == CUM_AT:
                            accumulate()

                def accumulate():
                    pe.wait_ge(consts, N_CONST1)
                    pe.wait_ge(fg_n, 1)
                    pe.wait_ge(ix_rl, 12)
                    for t in range(TT):
                        ins = nc.tensor.matmul(psum[4][0:8, :], zt[:, t, :],
                                               TRI[:, 384 - P * t:896 - P * t],
                                               start=t == 0, stop=t == TT - 1)
                    ins.then_inc(cm_mm, 1)

                def turn_index(m):
                    pe.wait_ge(ij_in, m + 1)
                    if m >= 2:
                        pe.wait_ge(ij_lo, m - 1)
                    for t in range(TT):
                        ins = nc.tensor.transpose(psum[5 + m % 2][:, P * t:P * t + P],
                                                  ijn[m % 2][:, t, :], ident[:, :])
                    ins.then_inc(ij_mm, 1)

                def index_products(t, head):
                    pe.wait_ge(ij_lo, 5)
                    for h in (head, head + 1):
                        u = 4 * (t - 1) + h
                        if u >= 2:
                            pe.wait_ge(ix_rl, u - 1)
                        dst = psum[4 + 3 * (h % 2)][:, 0:P * (t + 1)]
                        query = iq[h][:, P * t:P * t + P]
                        nc.tensor.matmul(dst, query, ikh[:, 0:P * (t + 1)],
                                         start=True, stop=False)
                        nc.tensor.matmul(dst, query, ikl[:, 0:P * (t + 1)],
                                         start=False, stop=True).then_inc(ix_mm, 1)

                project_first(n0, s0, 256)
                if l == 0:
                    mods_mm(4, 0, 16)
                    with pe.Fori(0, 3) as pair_of_slots:
                        i = pair_of_slots * 2
                        for j in (1, 2):
                            project(i + (n0 + j), i + (s0 + j), j, 256)
                            mods_mm(i + (4 + j), j % 2, i * 4 + (16 + 4 * j))
                    project(n0 + 7, s0 + 7, 7, 256)
                    mods_mm(11, 1, 16 + 4 * 7)
                for i in range(8 if l == 0 else 1, IN_SLOTS[l]):
                    project(n0 + i, s0 + i, i, in_width(l, BLOCKS[l][i]))

                def turn(job):
                    pe.wait_ge(j_in, job.n + 1)
                    if job.n >= 2:
                        pe.wait_ge(j_lo, job.n - 1)
                    for t in range(TT):
                        ins = nc.tensor.transpose(psum[5 + job.n % 2][:, P * t:P * t + P],
                                                  jn[job.n % 2][:, t, :], ident[:, :])
                    ins.then_inc(j_mm, 1)

                pe.wait_ge(p_ev, ALL_EV[l])
                if l == 1:
                    pe.wait_ge(cm_hi, 3)
                    pe.wait_ge(cm_lo, 2)
                if l == 0:
                    pe.wait_ge(mods_done, 1)
                pe.wait_ge(consts, N_CONST0)

                def scores(v):
                    u = Unit(l, v)
                    if v % 4 == 0:
                        heads = [j.n for j in JOBS[l] if j.step >= -1 and j.pair == u.pair
                                 and j.h <= u.h]
                        if u.pair == 0 and l == 0:
                            heads += [1]
                        pe.wait_ge(j_lo, max(heads) + 1)
                    if u.n >= 2:
                        if l == 1 and 2 <= v < UNITS // 2 + 2:
                            pe.wait_ge(sc_ex, u.n - 1)
                        else:
                            pe.wait_ge(sc_dv, copied_out(u.n - 2))
                    b, h = u.keys
                    bank, w = psum[v % 2], u.width
                    query = qs[u.pair % 2][u.h][:, P * u.t:P * u.t + P]
                    biased = u.group.kind == "C"
                    if biased:
                        nc.tensor.matmul(bank[:, 0:w], SEL[:, u.group_head, :], cum3[:, 0:w],
                                         start=True, stop=False, skip_group_check=True)
                        nc.tensor.matmul(bank[:, w - P:w], identb[:, :], maskb[:, :],
                                         start=False, stop=False, skip_group_check=True)
                    for part, keys in enumerate((kh[b][h], kl[b][h])):
                        ins = nc.tensor.matmul(bank[:, 0:w], query,
                                               keys[:, P * u.first:P * u.first + w],
                                               start=not biased and part == 0, stop=part == 1,
                                               skip_group_check=biased)
                    ins.then_inc(sc_mm, 1)

                def turn_probs(v):
                    u = Unit(l, v)
                    pe.wait_ge(sc_dg, u.n + 1)
                    if u.n >= 2:
                        pe.wait_ge(pt_ev, u.n - 1)
                    for k in range(u.t + 1 - u.first):
                        ins = nc.tensor.matmul(psum[2 + v % 2][:, P * k:P * k + P],
                                               Ssb[:, v % RING, P * k:P * k + P],
                                               dg[v % DIAGS][:, :], start=True, stop=True)
                    ins.then_inc(pt_mm, 1)

                def values(head, k):
                    u = Unit(l, 4 * head)
                    g, p = u.group, u.pair % 4
                    pe.wait_ge(pt_ev, u.n + 4)
                    n = PAIRS * l + u.pair
                    if u.h == 0 and k == 0 and n >= 2:
                        pe.wait_ge(o_lo, n - 1)
                    if g.kind == "A":
                        vcol = g.vcol + HD * (p // 2)
                    else:
                        vcol = g.vcol + (P * p + HD * u.h if g.own_keys else 0)
                    cols = slice(P * k, min(P * k + 2 * P, S) if g.kind == "A" else S)
                    ins = nc.tensor.matmul(
                        out_bank(u.pair)[HD * u.h:HD * u.h + HD, cols],
                        proj[l][:, k, vcol:vcol + HD], PT[u.h][:, k, cols],
                        start=k == 0, stop=k == TT - 1, skip_group_check=True)
                    if k == TT - 1:
                        ins.then_inc(pv_mm, 1)

                for job in JOBS[l]:
                    if job.step == -1:
                        turn(job)
                for v in range(STEPS):
                    for job in JOBS[l]:
                        if job.step == v:
                            turn(job)
                    if v < UNITS:
                        scores(v)
                    if 0 <= v - VALUES_LAG < UNITS:
                        values((v - VALUES_LAG) // 4, v % TT)
                    if 0 <= v - TURN_LAG < UNITS:
                        turn_probs(v - TURN_LAG)

                def chunk(bank, b, nk, cols, parts, late=None):
                    for k in range(nk):
                        if late is not None and k == nk - 1:
                            pe.wait_ge(*late)
                        a = cols(k)
                        hi, lo = parts(k)
                        ins = three(psum[bank][:, :], whi[b][:, a:a + P], wlo[b][:, a:a + P],
                                    hi, lo, k == 0, k == nk - 1)
                    return ins

                pe.wait_ge(o_lo, PAIRS * (l + 1) - 1)
                for i in range(4):
                    n = OUT_BASE[l] + i
                    pe.wait_ge(w_lo, n + 1 + RAW_FREE)
                    for m in (2 * i, 2 * i + 1):
                        pe.wait_ge(x_done, 24 * l + m + 7)
                        ins = chunk(4 + m % 2, n % 2, KC,
                                    lambda k: 256 * k + P * (m % 2),
                                    lambda k: out_parts(l, k),
                                    (o_lo, PAIRS * (l + 1)) if m == 0 else None)
                        ins.then_inc(y_half if m % 2 == 0 else w_used, 1)
                sum_squares(2 * l + 1)
                spread(2 * l + 1)

                for half in range(2):
                    nh, n0, f0 = HALF[half], GU_BASE[l][half], FT * l + HALF[0] * half

                    def gate_up(n, f, b, j):
                        pe.wait_ge(w_lo, n + (1 + RAW_FREE))
                        pe.wait_ge(g_a, f + 1)
                        for q in range(2):
                            ins = chunk(2 * j + q, b, KC, lambda k: 1024 * q + P * k,
                                        lambda k: (hhi[:, k, :], hlo[:, k, :]))
                        ins.then_inc(w_used, 1)

                    def gate_up_first(n, f):
                        b = n % 2
                        pe.wait_ge(w_lo, n + (1 + RAW_FREE))
                        pe.wait_ge(g_a, f + 1)
                        for k in range(KC):
                            pe.wait_ge(h_lo, 16 * l + 8 + k + 1)
                            for q in range(2):
                                a = 1024 * q + P * k
                                ins = three(psum[q][:, :], whi[b][:, a:a + P], wlo[b][:, a:a + P],
                                            hhi[:, k, :], hlo[:, k, :], k == 0, k == KC - 1)
                        ins.then_inc(w_used, 1)

                    if half == 0:
                        gate_up_first(n0, f0)
                        with pe.Fori(0, nh // 2 - 1) as pair_of_slots:
                            i = pair_of_slots * 2
                            for j in (1, 2):
                                gate_up(i + (n0 + j), i + (f0 + j), (n0 + j) % 2, j % 2)
                            if l == 0:
                                mods_mm(pair_of_slots + 12, 0, pair_of_slots * 4)
                        gate_up(n0 + nh - 1, f0 + nh - 1, (n0 + nh - 1) % 2, (nh - 1) % 2)
                        if l == 0:
                            mods_mm(17, 0, 4 * 5)
                    else:
                        with pe.Fori(0, nh // 2) as pair_of_slots:
                            i = pair_of_slots * 2
                            for j in range(2):
                                gate_up(i + (n0 + j), i + (f0 + j), (n0 + j) % 2, j)
                            if l == 0:
                                mods_mm(pair_of_slots + 19, 0, pair_of_slots * 4 + 4 * 7)
                    tiles_done = FT * l + HALF[0] * half + nh + GLO_FREE
                    pe.wait_ge(g_lo, tiles_done - 1)
                    n0 = DN_BASE[l][half]

                    def down(n, y, b, j):
                        pe.wait_ge(w_lo, n + (1 + RAW_FREE))
                        pe.wait_ge(x_done, y + 7)
                        chunk(4 + j, b, nh, lambda k: P * k,
                              lambda k: (acthi[:, k, :], actlo[:, k, :]),
                              (g_lo, tiles_done)).then_inc(w_used, 1)

                    y0 = 24 * l + 8 + 8 * half
                    if l == 1 and half == 1:
                        for j in range(KC):
                            down(n0 + j, y0 + j, (n0 + j) % 2, j % 2)
                            if j:
                                turn_result(j - 1)
                        turn_result(KC - 1)
                        continue
                    with pe.Fori(0, 4) as pair_of_slots:
                        i = pair_of_slots * 2
                        for j in range(2):
                            down(i + (n0 + j), i + (y0 + j), (n0 + j) % 2, j)
                    if l == 0:
                        if half == 0:
                            mods_mm(18, 0, 4 * 6)
                        else:
                            sum_squares(2)


_INS = ['x', 'c', 'ada_w', 'ada_b', 'mix_norm_g', 'ffn_norm_g', 'ab_w_in', 'ab_w_out', 'a_q_norm',
        'a_k_norm', 'a_sink', 'b_q_norm', 'b_k_norm', 'b_rel_bias', 'cd_w_in', 'cd_w_out',
        'c_q_norm', 'c_k_norm', 'c_forget_bias', 'd_q_norm', 'd_k_norm', 'ffn_w_gate_up',
        'ffn_w_down']
_OUTS = [((1, 512, 1024), 'float32')]


def kernel(**inputs):
    import numpy as _np
    import concourse.bacc as _bacc
    from concourse import mybir as _mybir
    from concourse.bass_utils import run_bass_kernel_spmd as _run

    nc = _bacc.Bacc("TRN2", target_bir_lowering=False, num_devices=1)
    arrays, args = {}, []
    for name in _INS:
        a = _np.ascontiguousarray(inputs[name])
        arrays[f"in_{name}_dram"] = a
        args.append(nc.dram_tensor(f"in_{name}_dram", a.shape, _mybir.dt.from_np(a.dtype),
                                   kind="ExternalInput").ap())
    for i, (shape, dtype) in enumerate(_OUTS):
        dt = _mybir.dt.from_np(_np.dtype(dtype))
        args.append(nc.dram_tensor(f"out_{i}_dram", shape, dt, kind="ExternalOutput").ap())
    build_program(nc, *args)
    r = _run(nc, [arrays], core_ids=[0])
    return _np.asarray(r.results[0]["out_0_dram"])
```
